# Optimizing a Trainium2 kernel written in Bass

```python
import jax
import jax.numpy as jnp
from jax import lax
import numpy as np

'''Hybrid autoregressive decoder layer (Hymba-style parallel head groups).
Each layer runs: pre-RMSNorm -> ONE combined input projection whose columns are partitioned
into an mLSTM head group (chunkwise-parallel matrix memory) and a multi-head latent attention
head group (low-rank compressed KV, decoupled rotary key, QK-norm) -> concatenation of both
groups' head outputs -> ONE output projection -> residual add; then pre-RMSNorm -> PEER
product-key single-neuron expert retrieval -> residual add.
Inputs: x (BATCH, SEQ, D_MODEL) float32, positions (BATCH, SEQ) int32, all per-layer
parameters stacked on a leading DEPTH axis. Output: (BATCH, SEQ, D_MODEL).
'''

D_MODEL = 1024
BATCH = 1
SEQ = 512
DEPTH = 1

D_MIX = D_MODEL
RMS_EPS = 1e-6
MLSTM_HEADS = 4
MLSTM_DQK = 128
MLSTM_DV = 128
MLSTM_CHUNK = 64
MLA_HEADS = 4
MLA_Q_RANK = 256
MLA_KV_RANK = 128
MLA_NOPE = 128
MLA_ROPE = 64
MLA_DV = 128
MLA_DQK = MLA_NOPE + MLA_ROPE
ATTN_Q_BLOCK = 128
ROPE_THETA = 10000.0
PEER_HEADS = 8
PEER_N_KEYS = 128
PEER_N_EXPERTS = PEER_N_KEYS * PEER_N_KEYS
PEER_D_KEY = 256
PEER_TOPK = 16
PEER_TOKEN_BLOCK = 128
IN_SPLITS = (
    MLSTM_HEADS * MLSTM_DQK,
    MLSTM_HEADS * MLSTM_DQK,
    MLSTM_HEADS * MLSTM_DV,
    MLSTM_HEADS * MLSTM_DV,
    MLSTM_HEADS,
    MLSTM_HEADS,
    MLA_Q_RANK,
    MLA_KV_RANK,
    MLA_ROPE,
)
D_IN = sum(IN_SPLITS)

kernel_name = 'hybrid_mlstm_mla_peer_layer'

def rms_norm(x, g):
    xf = x.astype(jnp.float32)
    y = xf * lax.rsqrt(jnp.mean(xf * xf, axis=-1, keepdims=True) + RMS_EPS)
    return (y * g.astype(jnp.float32)).astype(x.dtype)

def mlstm_group(mq, mk, mv, mo, mi, mf, b_i, b_f, norm_g):
    B, S, _ = mq.shape
    H, L = MLSTM_HEADS, MLSTM_CHUNK
    NC = S // L
    f32 = jnp.float32

    def heads(t, d):
        return t.reshape(B, S, H, d).transpose(0, 2, 1, 3).astype(f32)

    q = heads(mq, MLSTM_DQK)
    k = heads(mk, MLSTM_DQK) * (MLSTM_DQK ** -0.5)
    v = heads(mv, MLSTM_DV)
    i_pre = jnp.moveaxis((mi + b_i).astype(f32), -1, 1)
    log_f = jax.nn.log_sigmoid(jnp.moveaxis((mf + b_f).astype(f32), -1, 1))

    def to_chunks(t):
        return jnp.moveaxis(t.reshape(B, H, NC, L, *t.shape[3:]), 2, 0)

    causal = jnp.tril(jnp.ones((L, L), dtype=bool))

    def chunk_step(carry, xs):
        C, n, m = carry
        qc, kc, vc, ic, fc = xs
        b = jnp.cumsum(fc, axis=-1)
        a = b + m[..., None]
        D = b[..., :, None] - b[..., None, :] + ic[..., None, :]
        D = jnp.where(causal, D, -jnp.inf)
        m_t = jnp.maximum(a, jnp.max(D, axis=-1))
        Dw = jnp.exp(D - m_t[..., None])
        aw = jnp.exp(a - m_t)
        s = jnp.einsum('bhtd,bhsd->bhts', qc, kc) * Dw
        num = aw[..., None] * jnp.einsum('bhtd,bhde->bhte', qc, C) + jnp.einsum('bhts,bhse->bhte', s, vc)
        den = aw * jnp.einsum('bhtd,bhd->bht', qc, n) + jnp.sum(s, axis=-1)
        h = num / jnp.maximum(jnp.abs(den), jnp.exp(-m_t))[..., None]
        bL = b[..., -1]
        g = bL[..., None] - b + ic
        m_new = jnp.maximum(bL + m, jnp.max(g, axis=-1))
        decay = jnp.exp(bL + m - m_new)
        w = jnp.exp(g - m_new[..., None])
        C_new = decay[..., None, None] * C + jnp.einsum('bhs,bhsd,bhse->bhde', w, kc, vc)
        n_new = decay[..., None] * n + jnp.einsum('bhs,bhsd->bhd', w, kc)
        return (C_new, n_new, m_new), h

    init = (jnp.zeros((B, H, MLSTM_DQK, MLSTM_DV), f32),
            jnp.zeros((B, H, MLSTM_DQK), f32),
            jnp.zeros((B, H), f32))
    xs = (to_chunks(q), to_chunks(k), to_chunks(v), to_chunks(i_pre), to_chunks(log_f))
    _, h = lax.scan(chunk_step, init, xs)
    h = jnp.moveaxis(h, 0, 2).reshape(B, H, S, MLSTM_DV).transpose(0, 2, 1, 3)
    h = rms_norm(h, norm_g.reshape(H, MLSTM_DV)).reshape(B, S, H * MLSTM_DV)
    return (jax.nn.sigmoid(mo.astype(f32)) * h).astype(mq.dtype)

def apply_rope(t, cos, sin):
    nope, rp = t[..., :MLA_NOPE], t[..., MLA_NOPE:]
    half = MLA_ROPE // 2
    r1, r2 = rp[..., :half], rp[..., half:]
    rot = jnp.concatenate([r1 * cos - r2 * sin, r1 * sin + r2 * cos], axis=-1)
    return jnp.concatenate([nope, rot], axis=-1)

def mla_group(cq, ckv, kr, positions, cq_g, w_uq, ckv_g, w_ukv, q_g, k_g):
    B, S, _ = cq.shape
    H = MLA_HEADS
    f32 = jnp.float32
    q = (rms_norm(cq, cq_g) @ w_uq).reshape(B, S, H, MLA_DQK)
    kv = (rms_norm(ckv, ckv_g) @ w_ukv).reshape(B, S, H, MLA_NOPE + MLA_DV)
    k_nope, v = kv[..., :MLA_NOPE], kv[..., MLA_NOPE:]
    k_rope = jnp.broadcast_to(kr[:, :, None, :], (B, S, H, MLA_ROPE))
    k = jnp.concatenate([k_nope, k_rope], axis=-1)
    q = rms_norm(q, q_g)
    k = rms_norm(k, k_g)
    inv_freq = ROPE_THETA ** (-jnp.arange(0, MLA_ROPE, 2, dtype=f32) / MLA_ROPE)
    ang = positions.astype(f32)[..., None] * inv_freq
    cos = jnp.cos(ang)[:, :, None, :].astype(q.dtype)
    sin = jnp.sin(ang)[:, :, None, :].astype(q.dtype)
    q = apply_rope(q, cos, sin).transpose(0, 2, 1, 3)
    k = apply_rope(k, cos, sin).transpose(0, 2, 1, 3)
    v = v.transpose(0, 2, 1, 3)
    QB = ATTN_Q_BLOCK
    NB = S // QB
    scale = MLA_DQK ** -0.5
    key_pos = jnp.arange(S)

    def attend(args):
        q_blk, bi = args
        sc = jnp.einsum('bhqd,bhkd->bhqk', q_blk, k).astype(f32) * scale
        q_pos = bi * QB + jnp.arange(QB)
        sc = jnp.where(key_pos[None, :] <= q_pos[:, None], sc, -jnp.inf)
        p = jax.nn.softmax(sc, axis=-1).astype(v.dtype)
        return jnp.einsum('bhqk,bhkd->bhqd', p, v)

    q_blocks = jnp.moveaxis(q.reshape(B, H, NB, QB, MLA_DQK), 2, 0)
    o = lax.map(attend, (q_blocks, jnp.arange(NB)))
    o = jnp.moveaxis(o, 0, 2).reshape(B, H, S, MLA_DV).transpose(0, 2, 1, 3)
    return o.reshape(B, S, H * MLA_DV)

def peer(h, w_q, keys_1, keys_2, u_table, v_table):
    B, S, D = h.shape
    T = B * S
    TB = PEER_TOKEN_BLOCK
    K = PEER_TOPK
    half = PEER_D_KEY // 2

    def block(xb):
        qry = (xb @ w_q).reshape(TB, PEER_HEADS, PEER_D_KEY)
        s1 = jnp.einsum('thd,nd->thn', qry[..., :half], keys_1)
        s2 = jnp.einsum('thd,nd->thn', qry[..., half:], keys_2)
        v1, i1 = lax.top_k(s1, K)
        v2, i2 = lax.top_k(s2, K)
        cand = (v1[..., :, None] + v2[..., None, :]).reshape(TB, PEER_HEADS, K * K)
        sc, ci = lax.top_k(cand, K)
        idx = (jnp.take_along_axis(i1, ci // K, axis=-1) * PEER_N_KEYS
               + jnp.take_along_axis(i2, ci % K, axis=-1))
        gate = jax.nn.softmax(sc.astype(jnp.float32), axis=-1)
        act = jax.nn.gelu(jnp.einsum('thed,td->the', u_table[idx], xb).astype(jnp.float32), approximate=False)
        return jnp.einsum('the,thed->td', (gate * act).astype(xb.dtype), v_table[idx])

    y = lax.map(block, h.reshape(T // TB, TB, D))
    return y.reshape(B, S, D).astype(h.dtype)

def setup_inputs(seed: int = 0) -> dict:
    key = jax.random.key(seed)
    ks = jax.random.split(key, 24)
    f32 = jnp.float32

    def normal(k, shape, scale):
        return jax.random.normal(k, shape, f32) * scale

    def gain(k, shape):
        return 1.0 + 0.02 * jax.random.normal(k, shape, f32)

    x = jax.random.normal(ks[0], (BATCH, SEQ, D_MODEL), f32)
    offsets = jax.random.randint(ks[1], (BATCH, 1), 0, 1024, dtype=jnp.int32)
    positions = (offsets + jnp.arange(SEQ, dtype=jnp.int32)[None, :]).astype(jnp.int32)
    return {
        'x': x,
        'positions': positions,
        'attn_norm_g': gain(ks[2], (DEPTH, D_MODEL)),
        'w_in': normal(ks[3], (DEPTH, D_MODEL, D_IN), D_MODEL ** -0.5),
        'b_igate': normal(ks[4], (DEPTH, MLSTM_HEADS), 0.1),
        'b_fgate': jnp.linspace(3.0, 6.0, MLSTM_HEADS, dtype=f32)[None, :] + normal(ks[5], (DEPTH, MLSTM_HEADS), 0.1),
        'mlstm_norm_g': gain(ks[6], (DEPTH, MLSTM_HEADS * MLSTM_DV)),
        'cq_norm_g': gain(ks[7], (DEPTH, MLA_Q_RANK)),
        'w_uq': normal(ks[8], (DEPTH, MLA_Q_RANK, MLA_HEADS * MLA_DQK), MLA_Q_RANK ** -0.5),
        'ckv_norm_g': gain(ks[9], (DEPTH, MLA_KV_RANK)),
        'w_ukv': normal(ks[10], (DEPTH, MLA_KV_RANK, MLA_HEADS * (MLA_NOPE + MLA_DV)), MLA_KV_RANK ** -0.5),
        'q_norm_g': gain(ks[11], (DEPTH, MLA_DQK)),
        'k_norm_g': gain(ks[12], (DEPTH, MLA_DQK)),
        'w_out': normal(ks[13], (DEPTH, D_MIX, D_MODEL), D_MIX ** -0.5),
        'ffn_norm_g': gain(ks[14], (DEPTH, D_MODEL)),
        'peer_w_q': normal(ks[15], (DEPTH, D_MODEL, PEER_HEADS * PEER_D_KEY), D_MODEL ** -0.5),
        'peer_keys_1': normal(ks[16], (DEPTH, PEER_N_KEYS, PEER_D_KEY // 2), (PEER_D_KEY // 2) ** -0.5),
        'peer_keys_2': normal(ks[17], (DEPTH, PEER_N_KEYS, PEER_D_KEY // 2), (PEER_D_KEY // 2) ** -0.5),
        'peer_u': normal(ks[18], (DEPTH, PEER_N_EXPERTS, D_MODEL), D_MODEL ** -0.5),
        'peer_v': normal(ks[19], (DEPTH, PEER_N_EXPERTS, D_MODEL), PEER_HEADS ** -0.5),
    }

def reference(x, positions, attn_norm_g, w_in, b_igate, b_fgate, mlstm_norm_g, cq_norm_g, w_uq,
              ckv_norm_g, w_ukv, q_norm_g, k_norm_g, w_out, ffn_norm_g, peer_w_q, peer_keys_1,
              peer_keys_2, peer_u, peer_v):
    split_idx = [int(s) for s in np.cumsum(IN_SPLITS)[:-1]]
    for l in range(DEPTH):
        h = rms_norm(x, attn_norm_g[l])
        proj = h @ w_in[l]
        mq, mk, mv, mo, mi, mf, cq, ckv, kr = jnp.split(proj, split_idx, axis=-1)
        y_m = mlstm_group(mq, mk, mv, mo, mi, mf, b_igate[l], b_fgate[l], mlstm_norm_g[l])
        y_a = mla_group(cq, ckv, kr, positions, cq_norm_g[l], w_uq[l], ckv_norm_g[l], w_ukv[l],
                        q_norm_g[l], k_norm_g[l])
        mixed = jnp.concatenate([y_m.astype(x.dtype), y_a.astype(x.dtype)], axis=-1)
        x = x + mixed @ w_out[l]
        h = rms_norm(x, ffn_norm_g[l])
        x = x + peer(h, peer_w_q[l], peer_keys_1[l], peer_keys_2[l], peer_u[l], peer_v[l])
    return x


_drawn_inputs = setup_inputs


def setup_inputs(seed=0):
    import zlib

    import numpy as np

    out = dict(_drawn_inputs(seed))
    spreads = {}
    factors = {'b_igate': 64.0,
     'mlstm_norm_g': 26.317,
     'cq_norm_g': 6.922,
     'ckv_norm_g': 5.536,
     'q_norm_g': 6.882,
     'k_norm_g': 6.886,
     'ffn_norm_g': 8.0}
    for name, (base, spread) in spreads.items():
        noise = np.random.default_rng([zlib.crc32(name.encode()), seed]).standard_normal(out[name].shape)
        drawn = base * np.exp(spread * noise) if base else spread * noise
        out[name] = jnp.asarray(drawn.astype(out[name].dtype))
    for name, factor in factors.items():
        out[name] = (out[name] * factor).astype(out[name].dtype)
    return out
```

```python
from contextlib import ExitStack

import concourse.bass as bass
import numpy as np
from concourse import mybir

F32 = mybir.dt.float32
F32R = mybir.dt.float32r
I32 = mybir.dt.int32
U32 = mybir.dt.uint32
ALU = mybir.AluOpType
ACT = mybir.ActivationFunctionType
AX_X = mybir.AxisListType.X

P = 128
D = 1024
S = 512
TB = S // P
KD = D // P
H = 4
DH = 128
ROPE = 64
HALF = ROPE // 2
DQK = DH + ROPE
QR, KVR = 256, 128
D_IN = 4 * H * DH + 2 * H + QR + KVR + ROPE
COL_Q, COL_K, COL_V, COL_O = 0, H * DH, 2 * H * DH, 3 * H * DH
COL_I = 4 * H * DH
COL_F = COL_I + H
COL_C = COL_F + H
CW = QR + KVR + ROPE
EPS = 1e-6
PH = 8
NK = 128
TOPK = 16
NEG = -1e30
LOWEST = -3.0e38
TWO_PI = 2.0 * np.pi
MAGIC = 1.5 * 2.0**23

RUNS = []
_pos, _a = 0, 0
while _a < TOPK:
    _len = TOPK // (_a + 1)
    _n = 1
    while _a + _n < TOPK and TOPK // (_a + _n + 1) == _len:
        _n += 1
    RUNS.append((_a, _n, _len, _pos))
    _pos += _n * _len
    _a += _n
CAND = _pos

C_ID, C_IOTA, C_MIN, C_NEG, C_FREQ, C_GQ, C_GK = 0, 128, 256, 384, 512, 544, 736
C_W = 928
V_ATT, V_FFN, V_ML, V_CQ, V_CKV, V_BI, V_BF = 0, 8, 16, 20, 22, 23, 24
V_W = 25

E_BLOCKS = NK
GROUP = 4
GROUPS = E_BLOCKS // GROUP
CHUNK = 32
CHUNKS = S // CHUNK
BATCH = 4
PRE_BODY, PRE_TRIPS = 4, 8
MAIN_BODY, MAIN_TRIPS = 12, 8
BATCHES_AT = [1, 1, 2] * 4
MAIN_BATCHES = sum(BATCHES_AT)
PRE = PRE_BODY * PRE_TRIPS
assert PRE + MAIN_BODY * MAIN_TRIPS == E_BLOCKS
assert MAIN_BATCHES * BATCH * MAIN_TRIPS == S and MAIN_BATCHES * BATCH == 2 * CHUNK


def front_jobs():
    jobs = [(("hT", k), "DA"[k % 2]) for k in range(KD)]
    jobs += [(("gi",), "D"), (("gf",), "D")]
    jobs += [(("c", t), "D") for t in range(TB)]
    jobs += [(("mq", h), "A") for h in range(H)] + [(("mk", h), "D") for h in range(H)]
    jobs += [(("mv", t), "A") for t in range(TB)] + [(("mo", t), "A") for t in range(TB)]
    jobs += [(("cT", k), "D") for k in range(3)]
    jobs += [(("q", t, i), "A") for t in range(TB) for i in range(2)]
    jobs += [(("kv", t, i), "D") for t in range(TB) for i in range(2)]
    jobs += [(("rowT",), "D")]
    for h in range(H):
        jobs += [(("negM", h), "D")] + [(("S", h, s), "D") for s in range(TB)]
        jobs += [(("num", h, i), "A") for i in range(2)]
    jobs += [(("qkT", w, h), "DA"[h % 2]) for w in range(4) for h in range(H)]
    units = [(h, t) for h in range(H) for t in range(TB)]
    for n in range(len(units) + 2):
        if n < len(units):
            jobs.append((("sc", *units[n]), "A"))
        if 1 <= n <= len(units):
            jobs.append((("pT", *units[n - 1]), "A"))
        if n >= 2:
            jobs.append((("pv", *units[n - 2]), "D"))
    jobs += [(("mT", k), "DA"[k % 2]) for k in range(KD)]
    jobs += [(("out", t, i), "D") for t in range(TB) for i in range(2)]
    jobs += [(("h2T", k), "D") for k in range(KD)]
    for h in range(PH):
        jobs += [(("qry", h, s), "A") for s in range(2)]
        jobs += [(("s12", h, i), "D") for i in range(2)]
    return jobs


JOBS = front_jobs()
INDEX = {name: n for n, (name, _) in enumerate(JOBS)}
ENGINE_OF = dict(JOBS)
NTH = {name: sum(e == eng for _, e in JOBS[: n + 1]) for n, (name, eng) in enumerate(JOBS)}
D_OFF = [0, 512, 896, 1152]
D_ALL = 1280


def build(nc, a):
    ctx = ExitStack()
    with ctx:
        base = 16512

        def at(name, kb, shape, dt=F32):
            return nc.alloc_sbuf_tensor_at(name, shape, dt, offset=base + int(kb * 1024))

        def sem(name):
            return ctx.enter_context(nc.semaphore(name))

        fence = ctx.enter_context(nc.sbuf_tensor("whole_sbuf", [P, (212800 // 4)], F32))
        ps = ctx.enter_context(nc.psum_tensor("banks", [P, 8, 512], F32))

        x_res = at("x_res", 0, [P, TB, D])
        consts = at("consts", 16, [P, C_W])
        vecs = at("vecs", 19.75, [P, 32])
        sel = at("head_rows", 20, [H, H, P])
        ident = consts[:, C_ID:C_ID + P]
        iota = consts[:, C_IOTA:C_IOTA + P]
        mask_min = consts[:, C_MIN:C_MIN + P]
        mask_neg = consts[:, C_NEG:C_NEG + P]
        freq = consts[:, C_FREQ:C_FREQ + HALF]
        gq = consts[:, C_GQ:C_GQ + DQK]
        gk = consts[:, C_GK:C_GK + DQK]

        w_in = at("w_in", 22, [P, KD, D_IN])
        hT = at("hT", 101, [P, KD, S])
        mqT = at("mqT", 117, [P, H, S])
        mkT = at("mkT", 125, [P, H, S])
        v_aug = at("v_aug", 133, [P, TB, H, DH + 1])
        og = at("og", 141.5, [P, TB, H * DH])
        h_nat = at("h_nat", 150, [P, TB, D])
        grow = [at(n, 150 + 2 * i, [H, S]) for i, n in enumerate(
            ("g_i", "g_f", "g_tmp", "g_F", "g_u", "g_M", "g_negM", "g_em"))]
        g_i, g_f, g_tmp, g_F, g_u, g_M, g_negM, g_em = grow
        w_uq = at("w_uq", 166, [P, 2, H * DQK])
        w_ukv = at("w_ukv", 172, [P, 2 * H * DH])
        c_sq = at("c_sq", 183, [P, TB, CW])
        cT = at("cT", 190, [P, 3, S])
        c_nat = at("c_nat", 196, [P, TB, CW])
        stat = at("stat", 204, [P, 16, 32])
        junk = at("junk", 176, [P, D])

        q_nat = at("q_nat", 22, [P, TB, H, DQK])
        kv_nat = at("kv_nat", 34, [P, TB, H, 2, DH])
        k_nat = at("k_nat", 50, [P, TB, H, DQK])
        qkT = at("qkT", 62, [P, 4, H, S])
        cosin = at("cosin", 94, [P, 2, TB, HALF])
        ang = at("ang", 95, [P, 4, TB, HALF])
        pos_i = at("pos_i", 97, [P, TB], I32)
        pos_f = at("pos_f", 97.125, [P, TB])

        dexp = at("dexp", 176, [P, 2, D_ALL])
        sT = at("sT", 186, [P, 2, D_ALL])
        numall = at("numall", 166, [P, TB, H, DH + 1])
        h_sq = at("h_sq", 176, [P, TB, H, DH])
        qk_sq = at("qk_sq", 176, [P, TB, H, DQK])
        rtmp = at("rtmp", 188, [P, 4, TB * H * HALF // 1])
        mixed = at("mixed", 150, [P, TB, D])
        p_nat = at("p_nat", 176, [P, 3, S])
        pT = at("pT", 182, [P, 3, S])
        mixT = at("mixT", 101, [P, KD, S])
        w_out = at("w_out", 117, [P, KD, D])

        h2_nat = at("h2_nat", 184, [P, TB, D])
        h2T = at("h2T", 101, [P, KD, S])
        h2_hi = at("h2_hi", 150, [P, KD, S], F32R)
        h2_lo = at("h2_lo", 166, [P, KD, S], F32R)
        w_q = at("w_q", 22, [P, KD, 2 * PH * P])
        qryT = at("qryT", 184, [P, 3, S])
        keysT = at("keysT", 206.25, [P, 2, NK])
        best_v = at("best_v", 86, [P, 2, TB, PH, TOPK])
        best_i = at("best_i", 90, [P, 2, TB, PH, TOPK], U32)
        best_tmp = at("best_tmp", 94, [P, 2, NK])

        u_raw = at("u_raw", 117, [P, 4, KD, P])
        u_hi = at("u_hi", 133, [P, 2, KD, P], F32R)
        u_lo = at("u_lo", 141, [P, 2, KD, P], F32R)
        act_out = at("act_out", 200, [P, 2, S])
        stage = at("stage", 22, [P, 2, NK, CHUNK])
        oh2 = at("oh2", 54, [P, 2, BATCH, NK], F32R)
        oh1 = at("oh1", 58, [P, 2, BATCH, NK])
        gate_hi = at("gate_hi", 62, [P, 2, BATCH, NK], F32R)
        gate_lo = at("gate_lo", 66, [P, 2, BATCH, NK], F32R)
        cand = at("cand", 70, [P, PH, CAND])
        pay = at("pay", 71.75, [P, PH, CAND])
        picked = at("picked", 73.5, [P, PH // 2, TOPK, CAND])
        pay_f = at("pay_f", 94, [P, 2, PH, TOPK])
        cand_tmp = at("cand_tmp", 95, [P, PH, CAND])
        iota_c = at("iota_c", 96.75, [P, CAND])
        sc_v = at("sc_v", 97, [P, PH, TOPK])
        sc_i = at("sc_i", 97.5, [P, PH, TOPK], U32)
        sc_f = at("sc_f", 98, [P, PH, TOPK])
        e_f = at("e_f", 98.5, [P, PH, TOPK])
        e_i = at("e_i", 99, [P, 3, PH, TOPK], I32)
        sums = at("sums", 100.5, [P, 2, PH])
        tri = at("tri", 192, [P, TB, 3, PH * TOPK])
        tab = at("tab", 184, [P, 3, S])
        tab_hi = at("tab_hi", 190, [P, S], F32R)
        tab_lo = at("tab_lo", 198, [P, S])

        v_raw = at("v_raw", 22, [P, 4, D])
        v_hi = at("v_hi", 38, [P, 2, GROUP, D], F32R)
        v_lo = at("v_lo", 70, [P, 2, GROUP, D], F32R)
        act_in = at("act_in", 102, [P, 2, GROUP, S])
        gates = at("gates", 118, [P, 2, CHUNKS, GROUP, CHUNK])
        w32 = at("w32", 134, [P, GROUP, S])
        w_hi = at("w_hi", 142, [P, 2, GROUP, S], F32R)
        w_lo = at("w_lo", 158, [P, 2, GROUP, S], F32R)

        act_d = nc.dram_tensor("act_scratch", [E_BLOCKS, P, S], F32).ap()
        gate_d = nc.dram_tensor("gate_scratch", [CHUNKS, NK, NK, CHUNK], F32).ap()

        consts_in = sem("consts_in")
        x_in = sem("x_in")
        win_in = [sem(f"win_in{i}") for i in range(5)]
        wsmall_in = sem("wsmall_in")
        wout_in = sem("wout_in")
        wq_in = sem("wq_in")
        bank_done = sem("bank_done")
        freed = {"A": sem("bank_freed_scalar"), "D": sem("bank_freed_vector")}
        dve_step = sem("dve_step")
        act_step = sem("act_step")
        pool_step = sem("pool_step")
        var_ready = sem("var_ready")
        root_ready = sem("root_ready")
        h_ready = sem("h_ready")
        fabs_ready = sem("fabs_ready")
        ln_ready = sem("ln_ready")
        m_ready = sem("m_ready")
        em_ready = sem("em_ready")
        c_ready = sem("c_ready")
        ang_ready = sem("ang_ready")
        trig_ready = sem("trig_ready")
        ones_ready = sem("ones_ready")
        dpre_ready = sem("dpre_ready")
        dexp_ready = sem("dexp_ready")
        s_ready = sem("s_ready")
        qk_ready = sem("qk_ready")
        rowmax_ready = sem("rowmax_ready")
        mixed_ready = sem("mixed_ready")
        x2_ready = sem("x2_ready")
        x2_sq = sem("x2_sq")
        h2_ready = sem("h2_ready")
        h2hi_ready = sem("h2hi_ready")
        h2lo_ready = sem("h2lo_ready")
        gate_pre = sem("gate_pre")
        gate_exp = sem("gate_exp")
        tri_ready = sem("tri_ready")
        triT_done = sem("triT_done")
        tab_ready = sem("tab_ready")
        u_in = [sem(f"u_in{i}") for i in range(4)]
        uhi_ready = sem("uhi_ready")
        ulo_ready = sem("ulo_ready")
        z_done = sem("z_done")
        act_ready = sem("act_ready")
        act_saved = [sem(f"act_saved{i}") for i in range(2)]
        oh_step = sem("oh_step")
        oh_ready = sem("oh_ready")
        gate_done = sem("gate_done")
        gate_staged = sem("gate_staged")
        gate_saved = [sem(f"gate_saved{i}") for i in range(2)]
        v_in = [sem(f"v_in{i}") for i in range(4)]
        actg_in = [sem(f"actg_in{i}") for i in range(2)]
        gates_in = [sem(f"gates_in{i}") for i in range(2)]
        vhi_ready = sem("vhi_ready")
        vlo_ready = sem("vlo_ready")
        w_ready = sem("w_ready")
        whi_ready = sem("whi_ready")
        wlo_ready = sem("wlo_ready")
        y_done = sem("y_done")
        y_added = sem("y_added")
        out_saved = sem("out_saved")

        def bank(job):
            return ps[:, INDEX[job] % 8, :]

        def arrived(eng, job):
            eng.wait_ge(bank_done, INDEX[job] + 1)

        def emptied(eng, job):
            eng.wait_ge(freed[ENGINE_OF[job]], NTH[job])

        def free(ins, job):
            ins.then_inc(freed[ENGINE_OF[job]], 1)

        block = ctx.enter_context(nc.Block())

        @block.sync
        def _(sp):
            for t in range(TB):
                sp.dma_start(x_res[:, t, :], a["x"][t * P:(t + 1) * P, :]).then_inc(x_in, 16)
            sp.dma_start(consts[:], a["consts"]).then_inc(consts_in, 16)
            sp.dma_start(vecs[:, 0:V_W], a["vecs"]).then_inc(consts_in, 16)
            sp.dma_start(sel[:], a["head_rows"]).then_inc(consts_in, 16)
            w_v = a["w_in"].rearrange("(k p) n -> p k n", p=P)
            for i, (c0, c1) in enumerate(((COL_I, D_IN), (COL_Q, COL_K), (COL_K, COL_V),
                                          (COL_V, COL_O), (COL_O, COL_I))):
                sp.dma_start(w_in[:, :, c0:c1], w_v[:, :, c0:c1]).then_inc(win_in[i], 16)
            sp.dma_start(w_uq[:], a["w_uq"].rearrange("(k p) n -> p k n", p=P)).then_inc(wsmall_in, 16)
            sp.dma_start(w_ukv[:], a["w_ukv"]).then_inc(wsmall_in, 16)
            sp.dma_start(keysT[:], a["keysT"]).then_inc(wsmall_in, 16)
            emptied(sp, ("mo", TB - 1))
            sp.dma_start(pos_i[:], a["positions"]).then_inc(consts_in, 16)
            sp.wait_ge(mixed_ready, 1)
            sp.dma_start(w_out[:], a["w_out"].rearrange("(k p) n -> p k n", p=P)).then_inc(wout_in, 16)
            emptied(sp, ("pv", H - 1, TB - 1))
            wq_v = a["w_q"].rearrange("(k p) n -> p k n", p=P)
            for i in range(4):
                c = slice(i * 512, (i + 1) * 512)
                sp.dma_start(w_q[:, :, c], wq_v[:, :, c]).then_inc(wq_in, 16)
            emptied(sp, ("out", TB - 1, 1))

            def load_u(n, j):
                sp.dma_start(u_raw[:, j % 4, :, :],
                             a["uT"][bass.ds(n, 1)].rearrange("o p k e -> (o p) k e")).then_inc(u_in[j % 4], 16)

            def save_act(n, j):
                sp.wait_ge(act_ready, n + 1)
                sp.dma_start(act_d[bass.ds(n, 1)].rearrange("o p t -> (o p) t"),
                             act_out[:, j % 2, :]).then_inc(act_saved[j % 2], 16)

            for j in range(4):
                load_u(j, j)

            with sp.Fori(0, PRE_TRIPS) as i:
                for j in range(PRE_BODY):
                    n = i * PRE_BODY + j
                    sp.wait_ge(ulo_ready, n + 1)
                    load_u(n + 4, j)
                    save_act(n, j)

            def main(i):
                chunk = 0
                staged = 0
                for j in range(MAIN_BODY):
                    n = i * MAIN_BODY + (PRE + j)
                    if not isinstance(i, int) or n + 4 < E_BLOCKS:
                        sp.wait_ge(ulo_ready, n + 1)
                        load_u(n + 4, j)
                    save_act(n, j)
                    staged += BATCHES_AT[j]
                    if staged * BATCH >= CHUNK * (chunk + 1):
                        sp.wait_ge(gate_staged, i * MAIN_BATCHES + (chunk + 1) * CHUNK // BATCH)
                        c = i * 2 + chunk
                        sp.dma_start(gate_d[bass.ds(c, 1)].rearrange("o p n t -> (o p) (n t)"),
                                     stage[:, chunk, :, :].rearrange("p n t -> p (n t)")
                                     ).then_inc(gate_saved[chunk], 16)
                        chunk += 1

            with sp.Fori(0, MAIN_TRIPS - 1) as i:
                main(i)
            main(MAIN_TRIPS - 1)

            for q in range(2):
                sp.wait_ge(act_saved[q], 16 * E_BLOCKS // 2)
                sp.wait_ge(gate_saved[q], 16 * CHUNKS // 2)
            sp.wait_ge(z_done, E_BLOCKS)

            def load_v(n, j):
                sp.dma_start(v_raw[:, j, :], a["v"][bass.ds(n, 1)].rearrange("o p d -> (o p) d")
                             ).then_inc(v_in[j], 16)

            def load_group(g, q):
                sp.dma_start(act_in[:, q, :, :],
                             act_d[bass.ds(g * GROUP, GROUP)].rearrange("n p t -> p n t")).then_inc(actg_in[q], 16)
                sp.dma_start(gates[:, q, :, :, :].rearrange("p c n t -> p c (n t)"),
                             gate_d[:, :, bass.ds(g * GROUP, GROUP), :].rearrange("c p n t -> p c (n t)")
                             ).then_inc(gates_in[q], 16)

            for j in range(4):
                load_v(j, j)
            for q in range(2):
                load_group(q, q)

            def second(i):
                for q in range(2):
                    g = i * 2 + q
                    for j in range(GROUP):
                        sp.wait_ge(vlo_ready, g * GROUP + (j + 1))
                        if not isinstance(i, int) or g + 1 < GROUPS:
                            load_v(g * GROUP + (GROUP + j), j)
                    if not isinstance(i, int) or g + 2 < GROUPS:
                        sp.wait_ge(w_ready, g + 1)
                        load_group(g + 2, q)

            with sp.Fori(0, GROUPS // 2 - 1) as i:
                second(i)
            second(GROUPS // 2 - 1)
            for t in range(TB):
                sp.wait_ge(y_added, 8 * (GROUPS - 1) + 2 * t + 2)
                sp.dma_start(a["out"][t * P:(t + 1) * P, :], x_res[:, t, :]).then_inc(out_saved, 16)
            sp.wait_ge(out_saved, 16 * TB)

        @block.gpsimd
        def _(pool):
            nc.gpsimd.memset(v_aug[:, :, :, DH:DH + 1], 1.0).then_inc(ones_ready, 1)

            def split_u(n, j):
                pool.wait_ge(uhi_ready, n + 1)
                nc.gpsimd.tensor_tensor(u_lo[:, j % 2, :, :], u_raw[:, j % 4, :, :],
                                        u_hi[:, j % 2, :, :].bitcast(F32), ALU.subtract).then_inc(ulo_ready, 1)

            with pool.Fori(0, PRE_TRIPS) as i:
                for j in range(PRE_BODY):
                    split_u(i * PRE_BODY + j, j)
            with pool.Fori(0, MAIN_TRIPS) as i:
                for j in range(MAIN_BODY):
                    split_u(i * MAIN_BODY + (PRE + j), j)
            with pool.Fori(0, GROUPS // 2) as i:
                for q in range(2):
                    for j in range(GROUP):
                        pool.wait_ge(vhi_ready, (i * 2 + q) * GROUP + (j + 1))
                        nc.gpsimd.tensor_tensor(v_lo[:, q, j, :], v_raw[:, j, :],
                                                v_hi[:, q, j, :].bitcast(F32), ALU.subtract).then_inc(vlo_ready, 1)

        @block.scalar
        def _(act):
            roots = [0]

            def root(cols):
                roots[0] += 1
                act.wait_ge(var_ready, roots[0])
                nc.scalar.activation(cols, cols, ACT.Sqrt).then_inc(root_ready, 1)

            act.wait_ge(x_in, 16 * TB)
            for t in range(TB):
                nc.scalar.activation(junk[:], x_res[:, t, :], ACT.Square,
                                     accum_out=stat[:, 0, t:t + 1]).then_inc(act_step, 1)
                act.wait_ge(act_step, t + 1)
            root(stat[:, 1, 0:TB])
            act.wait_ge(consts_in, 48)
            for k in range(1, KD, 2):
                arrived(act, ("hT", k))
                free(nc.scalar.activation(hT[:, k, :], bank(("hT", k)), ACT.Copy,
                                          scale=vecs[:, V_ATT + k:V_ATT + k + 1]), ("hT", k))
            root(stat[:, 1, 4:12])
            act.wait_ge(fabs_ready, 1)
            nc.scalar.activation(g_tmp[:], g_tmp[:], ACT.Exp, scale=-1.0).then_inc(act_step, 1)
            act.wait_ge(act_step, TB + 1)
            nc.scalar.activation(g_tmp[:], g_tmp[:], ACT.Ln, bias=1.0).then_inc(ln_ready, 1)
            for h in range(H):
                arrived(act, ("mq", h))
                free(nc.scalar.activation(mqT[:, h, :], bank(("mq", h)), ACT.Copy), ("mq", h))
            for t in range(TB):
                arrived(act, ("mv", t))
                free(nc.scalar.activation(v_aug[:, t, :, 0:DH],
                                          bank(("mv", t)).rearrange("p (h d) -> p h d", h=H), ACT.Copy), ("mv", t))
            for t in range(TB):
                arrived(act, ("mo", t))
                free(nc.scalar.activation(og[:, t, :], bank(("mo", t)), ACT.Sigmoid), ("mo", t))
            act.wait_ge(m_ready, 1)
            nc.scalar.activation(g_em[:], g_em[:], ACT.Exp, scale=-1.0).then_inc(em_ready, 1)
            for t in range(TB):
                for i in range(2):
                    j = ("q", t, i)
                    arrived(act, j)
                    free(nc.scalar.activation(q_nat[:, t, 2 * i:2 * i + 2, :],
                                              bank(j)[:, 0:2 * DQK].rearrange("p (h d) -> p h d", h=2), ACT.Copy), j)
            act.wait_ge(ang_ready, 1)
            nc.scalar.activation(cosin[:], ang[:, 0:2, :, :], ACT.Sin).then_inc(trig_ready, 1)
            for h in range(H):
                act.wait_ge(dpre_ready, h + 1)
                nc.scalar.activation(dexp[:, h % 2, :], dexp[:, h % 2, :], ACT.Exp).then_inc(dexp_ready, 1)
                for i in range(2):
                    j = ("num", h, i)
                    arrived(act, j)
                    free(nc.scalar.activation(numall[:, 2 * i:2 * i + 2, h, :],
                                              bank(j)[:, 0:2 * (DH + 1)].rearrange("p (t d) -> p t d", t=2),
                                              ACT.Copy), j)
            root(stat[:, 4, 0:32])
            root(stat[:, 6, 0:16])
            for w in range(4):
                rows = DH if w % 2 == 0 else ROPE
                for h in range(1, H, 2):
                    j = ("qkT", w, h)
                    arrived(act, j)
                    free(nc.scalar.activation(qkT[0:rows, w, h, :], bank(j)[0:rows, :], ACT.Copy), j)
            units = [(h, t) for h in range(H) for t in range(TB)]
            for n in range(len(units) + 1):
                if n < len(units):
                    h, t = units[n]
                    j = ("sc", h, t)
                    act.wait_ge(rowmax_ready, n + 1)
                    if n >= 3:
                        arrived(act, ("pT", *units[n - 3]))
                    w = (t + 1) * P
                    free(nc.scalar.activation(p_nat[:, n % 3, 0:w], bank(j)[:, 0:w], ACT.Exp,
                                              bias=stat[:, 8, n:n + 1], scale=float(DQK) ** -0.5,
                                              accum_out=stat[:, 9, n:n + 1]), j)
                if n >= 1:
                    h, t = units[n - 1]
                    j = ("pT", h, t)
                    arrived(act, j)
                    if n >= 4:
                        arrived(act, ("pv", *units[n - 4]))
                    w = (t + 1) * P
                    free(nc.scalar.activation(pT[:, (n - 1) % 3, 0:w], bank(j)[:, 0:w], ACT.Copy), j)
            for k in range(1, KD, 2):
                j = ("mT", k)
                arrived(act, j)
                if k < H:
                    free(nc.scalar.activation(mixT[:, k, :], bank(j), ACT.Copy,
                                              scale=vecs[:, V_ML + k:V_ML + k + 1]), j)
                else:
                    free(nc.scalar.activation(mixT[:, k, :], bank(j), ACT.Copy), j)
            for t in range(TB):
                act.wait_ge(x2_ready, 2 * t + 2)
                nc.scalar.activation(h2_nat[:, 0, :], x_res[:, t, :], ACT.Square,
                                     accum_out=stat[:, 10, t:t + 1]).then_inc(x2_sq, 1)
                act.wait_ge(x2_sq, t + 1)
            root(stat[:, 11, 0:TB])
            for k in range(KD):
                emptied(act, ("h2T", k))
                nc.scalar.activation(h2_hi[:, k, :], h2T[:, k, :], ACT.Copy).then_inc(h2hi_ready, 1)
            for h in range(PH):
                for s in range(2):
                    j = ("qry", h, s)
                    n = 2 * h + s
                    arrived(act, j)
                    if n >= 3:
                        arrived(act, ("s12", (n - 3) // 2, 1))
                    free(nc.scalar.activation(qryT[:, n % 3, :], bank(j), ACT.Copy), j)

            def round_u(n, j, first=False):
                act.wait_ge(u_in[j % 4], n // 4 * 16 + 16 if isinstance(n, int) else (n - j % 4) * 4 + 16)
                if not first:
                    act.wait_ge(z_done, n - 1)
                nc.scalar.activation(u_hi[:, j % 2, :, :], u_raw[:, j % 4, :, :], ACT.Copy).then_inc(uhi_ready, 1)

            def gelu(n, j, first=False):
                act.wait_ge(z_done, n + 1)
                if not first:
                    act.wait_ge(act_saved[j % 2], (n - j % 2) * 8)
                nc.scalar.activation(act_out[:, j % 2, :], ps[:, j % 2, :], ACT.Gelu).then_inc(act_ready, 1)

            emptied(act, ("s12", PH - 1, 1))
            round_u(0, 0, True)
            for j in range(PRE_BODY):
                round_u(j + 1, j + 1, j == 0)
                gelu(j, j, j < 2)
            with act.Fori(1, 3) as i:
                for j in range(PRE_BODY):
                    round_u(i * PRE_BODY + (j + 1), j + 1)
                    gelu(i * PRE_BODY + j, j)
            for t in range(TB):
                act.wait_ge(gate_pre, t + 1)
                nc.scalar.activation(sc_v[:], sc_v[:], ACT.Exp).then_inc(gate_exp, 1)
                with act.Fori(3 + t, 4 + t) as i:
                    for j in range(PRE_BODY):
                        round_u(i * PRE_BODY + (j + 1), j + 1)
                        gelu(i * PRE_BODY + j, j)
            with act.Fori(7, PRE_TRIPS) as i:
                for j in range(PRE_BODY):
                    round_u(i * PRE_BODY + (j + 1), j + 1)
                    gelu(i * PRE_BODY + j, j)

            def main(i):
                b = 0
                for j in range(MAIN_BODY):
                    n = i * MAIN_BODY + (PRE + j)
                    if not isinstance(i, int) or n + 1 < E_BLOCKS:
                        round_u(n + 1, j + 1)
                    for _ in range(BATCHES_AT[j]):
                        act.wait_ge(gate_done, i * MAIN_BATCHES + (b + 1))
                        chunk, at_b = divmod(b * BATCH, CHUNK)
                        if at_b == 0 and not (isinstance(i, int) and i == 0):
                            act.wait_ge(gate_saved[chunk], i * 16)
                        nc.scalar.activation(
                            stage[:, chunk, :, at_b:at_b + BATCH].rearrange("p n t -> p t n"),
                            ps[:, 2 + b % 2, :].rearrange("p (t n) -> p t n", t=BATCH),
                            ACT.Copy).then_inc(gate_staged, 1)
                        b += 1
                    gelu(n, j)

            main(0)
            with act.Fori(1, MAIN_TRIPS - 1) as i:
                main(i)
            main(MAIN_TRIPS - 1)

            def round_v(g, q, j, first=False):
                act.wait_ge(v_in[j], g * 16 + 16)
                if not first:
                    act.wait_ge(y_done, (g - 1) * 8)
                nc.scalar.activation(v_hi[:, q, j, :], v_raw[:, j, :], ACT.Copy).then_inc(vhi_ready, 1)

            def round_w(g, q):
                act.wait_ge(w_ready, g + 1)
                nc.scalar.activation(w_hi[:, q, :, :], w32[:], ACT.Copy).then_inc(whi_ready, 1)

            def second(i, first=False):
                for q in range(2):
                    round_w(i * 2 + q, q)
                    for j in range(GROUP):
                        round_v(i * 2 + q, q, j, first)

            second(0, True)
            with act.Fori(1, GROUPS // 2) as i:
                second(i)

        @block.vector
        def _(dve):
            steps = [0]

            def step(ins):
                steps[0] += 1
                ins.then_inc(dve_step, 1)

            def settle():
                dve.wait_ge(dve_step, steps[0])

            roots = [0]

            def inv_root(sums_ap, n, var, out):
                roots[0] += 1
                nc.vector.tensor_scalar(var, sums_ap, 1.0 / n, EPS, ALU.mult, ALU.add).then_inc(var_ready, 1)
                dve.wait_ge(root_ready, roots[0])
                step(nc.vector.reciprocal(out, var))
                settle()

            def bc(ap, axis, n):
                u = ap.unsqueeze(axis)
                shape = list(u.shape)
                shape[axis] = n
                return u.to_broadcast(shape)

            dve.wait_ge(act_step, TB)
            inv_root(stat[:, 0, 0:TB], D, stat[:, 1, 0:TB], stat[:, 2, 0:TB])
            for t in range(TB):
                nc.vector.tensor_scalar(h_nat[:, t, :], x_res[:, t, :], stat[:, 2, t:t + 1], None,
                                        ALU.mult).then_inc(h_ready, 1)
            dve.wait_ge(consts_in, 48)
            for k in range(0, KD, 2):
                arrived(dve, ("hT", k))
                free(nc.vector.tensor_scalar(hT[:, k, :], bank(("hT", k)), vecs[:, V_ATT + k:V_ATT + k + 1], None,
                                             ALU.mult), ("hT", k))
            for j, row, v in ((("gi",), g_i, V_BI), (("gf",), g_f, V_BF)):
                arrived(dve, j)
                free(nc.vector.tensor_scalar(row[:], bank(j)[0:H, :], vecs[0:H, v:v + 1], None, ALU.add), j)
            emptied(dve, ("gf",))
            step(nc.vector.tensor_scalar(g_F[:], g_f[:], -1.0, None, ALU.mult))
            settle()
            nc.vector.tensor_tensor(g_tmp[:], g_f[:], g_F[:], ALU.max).then_inc(fabs_ready, 1)
            for t in range(TB):
                arrived(dve, ("c", t))
                free(nc.vector.tensor_copy(c_nat[:, t, :], bank(("c", t))[:, 0:CW]), ("c", t))
            emptied(dve, ("c", TB - 1))
            step(nc.vector.tensor_tensor(c_sq[:], c_nat[:], c_nat[:], ALU.mult))
            settle()
            step(nc.vector.reduce_sum(stat[:, 0, 4:8], c_sq[:, :, 0:QR], axis=AX_X))
            step(nc.vector.reduce_sum(stat[:, 0, 8:12], c_sq[:, :, QR:QR + KVR], axis=AX_X))
            step(nc.vector.reduce_sum(stat[:, 0, 12:16], c_sq[:, :, QR + KVR:CW], axis=AX_X))
            settle()
            step(nc.vector.tensor_scalar(stat[:, 0, 8:12], stat[:, 0, 8:12], float(QR) / KVR, None, ALU.mult))
            settle()
            inv_root(stat[:, 0, 4:12], QR, stat[:, 1, 4:12], stat[:, 2, 4:12])
            nc.vector.tensor_tensor(c_sq[:, :, 0:QR], c_nat[:, :, 0:QR], bc(stat[:, 2, 4:8], 2, QR),
                                    ALU.mult).then_inc(c_ready, 1)
            nc.vector.tensor_tensor(c_sq[:, :, QR:QR + KVR], c_nat[:, :, QR:QR + KVR],
                                    bc(stat[:, 2, 8:12], 2, KVR), ALU.mult).then_inc(c_ready, 1)
            dve.wait_ge(ln_ready, 1)
            step(nc.vector.scalar_tensor_tensor(out=g_f[:], in0=g_f[:], scalar=0.0, in1=g_tmp[:],
                                                op0=ALU.min, op1=ALU.subtract))
            step(nc.vector.memset(g_negM[:], 1.0))
            settle()
            step(nc.vector.tensor_tensor_scan(out=g_F[:], data0=g_negM[:], data1=g_f[:], initial=0.0,
                                              op0=ALU.mult, op1=ALU.add))
            settle()
            step(nc.vector.tensor_tensor(g_u[:], g_i[:], g_F[:], ALU.subtract))
            settle()
            step(nc.vector.tensor_tensor_scan(out=g_M[:], data0=g_negM[:], data1=g_u[:], initial=0.0,
                                              op0=ALU.mult, op1=ALU.max))
            settle()
            nc.vector.tensor_tensor(g_em[:], g_F[:], g_M[:], ALU.add).then_inc(m_ready, 1)
            nc.vector.tensor_scalar(g_negM[:], g_M[:], -1.0, None, ALU.mult).then_inc(m_ready, 1)
            for h in range(H):
                arrived(dve, ("mk", h))
                free(nc.vector.tensor_copy(mkT[:, h, :], bank(("mk", h))), ("mk", h))
            for k in range(3):
                j = ("cT", k)
                arrived(dve, j)
                free(nc.vector.tensor_scalar(cT[:, k, :], bank(j), vecs[:, V_CQ + k:V_CQ + k + 1], None,
                                             ALU.mult), j)
            for t in range(TB):
                for i in range(2):
                    j = ("kv", t, i)
                    arrived(dve, j)
                    free(nc.vector.tensor_copy(kv_nat[:, t, 2 * i:2 * i + 2, :, :],
                                               bank(j).rearrange("p (h w d) -> p h w d", h=2, w=2)), j)
            dve.wait_ge(consts_in, 64)
            step(nc.vector.tensor_copy(pos_f[:], pos_i[:]))
            settle()
            for t in range(TB):
                step(nc.vector.tensor_scalar(ang[:, 0, t, :], freq, pos_f[:, t:t + 1], None, ALU.mult))
            settle()
            step(nc.vector.tensor_scalar(ang[:, 1, :, :], ang[:, 0, :, :], 1.0 / TWO_PI, MAGIC, ALU.mult, ALU.add))
            settle()
            step(nc.vector.tensor_scalar(ang[:, 1, :, :], ang[:, 1, :, :], MAGIC, None, ALU.subtract))
            settle()
            c1 = 6.28125
            c2 = float(np.float32(np.round((TWO_PI - c1) * 2**20) / 2**20))
            c3 = float(TWO_PI - c1 - c2)
            for c in (c1, c2, c3):
                step(nc.vector.scalar_tensor_tensor(out=ang[:, 0, :, :], in0=ang[:, 1, :, :], scalar=-c,
                                                    in1=ang[:, 0, :, :], op0=ALU.mult, op1=ALU.add))
                settle()
            pi = float(np.float32(3.1415925))
            step(nc.vector.tensor_scalar(ang[:, 0, :, :], ang[:, 0, :, :], pi, -pi, ALU.min, ALU.max))
            settle()
            step(nc.vector.tensor_scalar(ang[:, 2, :, :], ang[:, 0, :, :], -1.0, None, ALU.mult))
            settle()
            step(nc.vector.tensor_tensor(ang[:, 1, :, :], ang[:, 0, :, :], ang[:, 2, :, :], ALU.max))
            settle()
            nc.vector.tensor_scalar(ang[:, 1, :, :], ang[:, 1, :, :], -1.0, TWO_PI / 4, ALU.mult,
                                    ALU.add).then_inc(ang_ready, 1)

            arrived(dve, ("rowT",))
            free(nc.vector.tensor_copy(stat[:, 12, 0:32], bank(("rowT",))[:, 0:32]), ("rowT",))
            emptied(dve, ("rowT",))
            u_col = stat[:, 12, 0:16].rearrange("p (t h) -> p t h", h=H)
            em_col = stat[:, 12, 16:32]
            for h in range(H):
                j = ("negM", h)
                arrived(dve, j)
                if h >= 2:
                    settle()
                neg_m = bank(j)
                for s in range(TB):
                    lo = D_OFF[s]
                    step(nc.vector.scalar_tensor_tensor(
                        out=dexp[:, h % 2, lo:lo + P], in0=neg_m[:, s * P:(s + 1) * P],
                        scalar=u_col[:, s, h:h + 1], in1=mask_min, op0=ALU.add, op1=ALU.min))
                    if s < TB - 1:
                        step(nc.vector.tensor_scalar(dexp[:, h % 2, lo + P:lo + (TB - s) * P],
                                                     neg_m[:, (s + 1) * P:], u_col[:, s, h:h + 1], None, ALU.add))
                settle()
                free(nc.vector.tensor_copy(stat[:, 13, 0:1], stat[:, 12, 0:1]), j)
                nc.vector.tensor_copy(stat[:, 13, 1:2], stat[:, 12, 0:1]).then_inc(dpre_ready, 1)
                dve.wait_ge(dexp_ready, h + 1)
                if h >= 2:
                    arrived(dve, ("num", h - 2, 1))
                for s in range(TB):
                    j = ("S", h, s)
                    arrived(dve, j)
                    lo, w = D_OFF[s], (TB - s) * P
                    free(nc.vector.scalar_tensor_tensor(
                        out=sT[:, h % 2, lo:lo + w], in0=bank(j)[:, 0:w], scalar=float(DH) ** -0.5,
                        in1=dexp[:, h % 2, lo:lo + w], op0=ALU.mult, op1=ALU.mult), j)
                emptied(dve, ("S", h, TB - 1))

            arrived(dve, ("num", H - 1, 1))
            emptied(dve, ("q", TB - 1, 1))
            emptied(dve, ("kv", TB - 1, 1))
            step(nc.vector.tensor_tensor(qk_sq[:], q_nat[:], q_nat[:], ALU.mult))
            settle()
            th = "p t h -> p (t h)"
            step(nc.vector.reduce_sum(stat[:, 3, 0:16].rearrange("p (t h) -> p t h", h=H), qk_sq[:], axis=AX_X))
            settle()
            step(nc.vector.tensor_tensor(qk_sq[:, :, :, 0:DH], kv_nat[:, :, :, 0, :], kv_nat[:, :, :, 0, :],
                                         ALU.mult))
            settle()
            step(nc.vector.reduce_sum(stat[:, 3, 16:32].rearrange("p (t h) -> p t h", h=H),
                                      qk_sq[:, :, :, 0:DH], axis=AX_X))
            settle()
            step(nc.vector.tensor_tensor(stat[:, 3, 16:32].rearrange("p (t h) -> p t h", h=H),
                                         stat[:, 3, 16:32].rearrange("p (t h) -> p t h", h=H),
                                         bc(stat[:, 0, 12:16], 2, H), ALU.add))
            settle()
            inv_root(stat[:, 3, 0:32], DQK, stat[:, 4, 0:32], stat[:, 5, 0:32])
            rq = stat[:, 5, 0:16].rearrange("p (t h) -> p t h", h=H)
            rk = stat[:, 5, 16:32].rearrange("p (t h) -> p t h", h=H)
            step(nc.vector.tensor_tensor(q_nat[:], q_nat[:], bc(rq, 3, DQK), ALU.mult))
            step(nc.vector.tensor_tensor(k_nat[:, :, :, 0:DH], kv_nat[:, :, :, 0, :], bc(rk, 3, DH), ALU.mult))
            for h in range(H):
                step(nc.vector.tensor_tensor(k_nat[:, :, h, DH:DQK], c_nat[:, :, QR + KVR:CW],
                                             bc(rk[:, :, h], 2, ROPE), ALU.mult))
            settle()
            for x_nat, g in ((q_nat, gq), (k_nat, gk)):
                v = x_nat[:].rearrange("p t h d -> p (t h) d")
                step(nc.vector.tensor_tensor(v, v, bc(g, 1, TB * H), ALU.mult))
            dve.wait_ge(trig_ready, 1)
            settle()
            sin_t = bc(cosin[:, 0, :, :], 2, H)
            cos_t = bc(cosin[:, 1, :, :], 2, H)
            for x_nat in (q_nat, k_nat):
                r1 = x_nat[:, :, :, DH:DH + HALF]
                r2 = x_nat[:, :, :, DH + HALF:DQK]
                tmp = [rtmp[:, i, :].rearrange("p (t h d) -> p t h d", t=TB, h=H) for i in range(4)]
                for o, r, c in ((0, r1, cos_t), (1, r2, sin_t), (2, r1, sin_t), (3, r2, cos_t)):
                    step(nc.vector.tensor_tensor(tmp[o], r, c, ALU.mult))
                settle()
                nc.vector.tensor_tensor(r1, tmp[0], tmp[1], ALU.subtract).then_inc(qk_ready, 1)
                nc.vector.tensor_tensor(r2, tmp[2], tmp[3], ALU.add).then_inc(qk_ready, 1)
                dve.wait_ge(qk_ready, 2 if x_nat is q_nat else 4)

            emptied(dve, ("num", H - 1, 1))
            den = numall[:, :, :, DH]
            num = numall[:, :, :, 0:DH]
            dd = stat[:, 13, 0:16].rearrange("p (t h) -> p t h", h=H)
            em3 = em_col.rearrange("p (t h) -> p t h", h=H)
            step(nc.vector.tensor_scalar(dd, den, -1.0, None, ALU.mult))
            settle()
            step(nc.vector.tensor_tensor(dd, dd, den, ALU.max))
            settle()
            step(nc.vector.tensor_tensor(dd, dd, em3, ALU.max))
            settle()
            step(nc.vector.reciprocal(dd, dd))
            settle()
            step(nc.vector.tensor_tensor(num, num, bc(dd, 3, DH), ALU.mult))
            settle()
            step(nc.vector.tensor_tensor(h_sq[:], num, num, ALU.mult))
            settle()
            step(nc.vector.reduce_sum(stat[:, 14, 0:16].rearrange("p (t h) -> p t h", h=H), h_sq[:], axis=AX_X))
            settle()
            inv_root(stat[:, 14, 0:16], DH, stat[:, 6, 0:16], stat[:, 7, 0:16])
            step(nc.vector.tensor_tensor(num, num, bc(stat[:, 7, 0:16].rearrange("p (t h) -> p t h", h=H), 3, DH),
                                         ALU.mult))
            settle()
            nc.vector.tensor_tensor(mixed[:, :, 0:H * DH].rearrange("p t (h d) -> p t h d", h=H), num,
                                    og[:].rearrange("p t (h d) -> p t h d", h=H), ALU.mult).then_inc(mixed_ready, 1)
            dve.wait_ge(mixed_ready, 1)
            for w in range(4):
                rows = DH if w % 2 == 0 else ROPE
                for h in range(0, H, 2):
                    j = ("qkT", w, h)
                    arrived(dve, j)
                    free(nc.vector.tensor_copy(qkT[0:rows, w, h, :], bank(j)[0:rows, :]), j)
            units = [(h, t) for h in range(H) for t in range(TB)]
            for n in range(len(units) + 2):
                if n < len(units):
                    h, t = units[n]
                    j = ("sc", h, t)
                    arrived(dve, j)
                    w = t * P
                    step(nc.vector.tensor_tensor(bank(j)[:, w:w + P], bank(j)[:, w:w + P], mask_neg, ALU.add))
                    settle()
                    step(nc.vector.reduce_max(stat[:, 13, 16 + n % 16:17 + n % 16], bank(j)[:, 0:w + P], axis=AX_X))
                    settle()
                    nc.vector.tensor_scalar(stat[:, 8, n:n + 1], stat[:, 13, 16 + n % 16:17 + n % 16],
                                            -float(DQK) ** -0.5, None, ALU.mult).then_inc(rowmax_ready, 1)
                if n >= 2:
                    h, t = units[n - 2]
                    j = ("pv", h, t)
                    emptied(dve, ("sc", h, t))
                    step(nc.vector.reciprocal(stat[:, 9, n - 2:n - 1], stat[:, 9, n - 2:n - 1]))
                    arrived(dve, j)
                    settle()
                    c0 = (H + h) * DH
                    free(nc.vector.tensor_scalar(mixed[:, t, c0:c0 + DH], bank(j)[:, 0:DH],
                                                 stat[:, 9, n - 2:n - 1], None, ALU.mult), j)
            for k in range(0, KD, 2):
                j = ("mT", k)
                arrived(dve, j)
                if k < H:
                    free(nc.vector.tensor_scalar(mixT[:, k, :], bank(j), vecs[:, V_ML + k:V_ML + k + 1], None,
                                                 ALU.mult), j)
                else:
                    free(nc.vector.tensor_copy(mixT[:, k, :], bank(j)), j)
            for t in range(TB):
                for i in range(2):
                    j = ("out", t, i)
                    arrived(dve, j)
                    v = x_res[:, t, i * 512:(i + 1) * 512]
                    step(nc.vector.tensor_tensor(v, v, bank(j), ALU.add))
                    settle()
                    nc.vector.tensor_copy(stat[:, 13, 0:1], stat[:, 12, 0:1]).then_inc(x2_ready, 1)
                    free(nc.vector.tensor_copy(stat[:, 13, 1:2], stat[:, 12, 0:1]), j)
            dve.wait_ge(x2_sq, TB)
            inv_root(stat[:, 10, 0:TB], D, stat[:, 11, 0:TB], stat[:, 15, 0:TB])
            for t in range(TB):
                nc.vector.tensor_scalar(h2_nat[:, t, :], x_res[:, t, :], stat[:, 15, t:t + 1], None,
                                        ALU.mult).then_inc(h2_ready, 1)
            for k in range(KD):
                j = ("h2T", k)
                arrived(dve, j)
                free(nc.vector.tensor_scalar(h2T[:, k, :], bank(j), vecs[:, V_FFN + k:V_FFN + k + 1], None,
                                             ALU.mult), j)
            for k in range(KD):
                dve.wait_ge(h2hi_ready, k + 1)
                nc.vector.tensor_tensor(h2_lo[:, k, :], h2T[:, k, :], h2_hi[:, k, :].bitcast(F32),
                                        ALU.subtract).then_inc(h2lo_ready, 1)
            for h in range(PH):
                for i in range(2):
                    j = ("s12", h, i)
                    arrived(dve, j)
                    for tt in range(2):
                        t = 2 * i + tt
                        sc = [bank(j)[:, (2 * tt + s) * NK:(2 * tt + s + 1) * NK] for s in range(2)]
                        bv = [best_v[:, s, t, h, :] for s in range(2)]
                        bi = [best_i[:, s, t, h, :] for s in range(2)]
                        for s in range(2):
                            step(nc.vector.max(bv[s][:, 0:8], sc[s]))
                        settle()
                        for s in range(2):
                            step(nc.vector.max_index(bi[s][:, 0:8], bv[s][:, 0:8], sc[s]))
                            step(nc.vector.match_replace(best_tmp[:, s, :], bv[s][:, 0:8], sc[s], LOWEST))
                        settle()
                        for s in range(2):
                            step(nc.vector.max(bv[s][:, 8:16], best_tmp[:, s, :]))
                        settle()
                        for s in range(2):
                            step(nc.vector.max_index(bi[s][:, 8:16], bv[s][:, 8:16], best_tmp[:, s, :]))
                        settle()
                    free(nc.vector.tensor_copy(stat[:, 13, 0:1], stat[:, 12, 0:1]), j)
            step(nc.vector.tensor_copy(iota_c[:], consts[:, C_IOTA:C_IOTA + CAND]))
            for t in range(TB):
                step(nc.vector.tensor_scalar(pay_f[:, 0, :, :], best_i[:, 0, t, :, :], float(NK), None, ALU.mult))
                step(nc.vector.tensor_copy(pay_f[:, 1, :, :], best_i[:, 1, t, :, :]))
                settle()
                for src, dst in ((best_v[:, :, t, :, :], cand), (pay_f[:], pay)):
                    for a0, na, nb, at0 in RUNS:
                        out = dst[:, :, at0:at0 + na * nb].rearrange("p h (a b) -> p h a b", a=na)
                        step(nc.vector.tensor_tensor(out, bc(src[:, 0, :, a0:a0 + na], 3, nb),
                                                     bc(src[:, 1, :, 0:nb], 2, na), ALU.add))
                settle()
                for h in range(PH):
                    step(nc.vector.max(sc_v[:, h, 0:8], cand[:, h, :]))
                settle()
                for h in range(PH):
                    step(nc.vector.max_index(sc_i[:, h, 0:8], sc_v[:, h, 0:8], cand[:, h, :]))
                    step(nc.vector.match_replace(cand_tmp[:, h, :], sc_v[:, h, 0:8], cand[:, h, :], LOWEST))
                settle()
                for h in range(PH):
                    step(nc.vector.max(sc_v[:, h, 8:16], cand_tmp[:, h, :]))
                settle()
                for h in range(PH):
                    step(nc.vector.max_index(sc_i[:, h, 8:16], sc_v[:, h, 8:16], cand_tmp[:, h, :]))
                settle()
                step(nc.vector.tensor_copy(sums[:, 1, :], sc_v[:, :, 0]))
                step(nc.vector.tensor_copy(sc_f[:], sc_i[:]))
                settle()
                nc.vector.tensor_tensor(sc_v[:], sc_v[:], bc(sums[:, 1, :], 2, TOPK), ALU.subtract
                                        ).then_inc(gate_pre, 1)
                for hh in range(2):
                    hs = slice(hh * PH // 2, (hh + 1) * PH // 2)
                    step(nc.vector.tensor_tensor(
                        picked[:], bc(sc_f[:, hs, :], 3, CAND),
                        bc(bc(iota_c[:], 1, TOPK), 1, PH // 2), ALU.is_equal))
                    settle()
                    step(nc.vector.tensor_tensor(picked[:], picked[:], bc(pay[:, hs, :], 2, TOPK), ALU.mult))
                    settle()
                    step(nc.vector.reduce_sum(e_f[:, hs, :], picked[:], axis=AX_X))
                    settle()
                step(nc.vector.tensor_copy(e_i[:, 0, :, :], e_f[:]))
                settle()
                step(nc.vector.tensor_scalar(e_i[:, 1, :, :], e_i[:, 0, :, :], 7, None, ALU.logical_shift_right))
                step(nc.vector.tensor_scalar(e_i[:, 2, :, :], e_i[:, 0, :, :], NK - 1, None, ALU.bitwise_and))
                settle()
                for s in range(2):
                    nc.vector.tensor_copy(tri[:, t, 1 + s, :].rearrange("p (h k) -> p h k", h=PH),
                                          e_i[:, 1 + s, :, :]).then_inc(tri_ready, 1)
                dve.wait_ge(gate_exp, t + 1)
                step(nc.vector.reduce_sum(sums[:, 0, :], sc_v[:], axis=AX_X))
                settle()
                step(nc.vector.reciprocal(sums[:, 0, :], sums[:, 0, :]))
                settle()
                nc.vector.tensor_tensor(tri[:, t, 0, :].rearrange("p (h k) -> p h k", h=PH), sc_v[:],
                                        bc(sums[:, 0, :], 2, TOPK), ALU.mult).then_inc(tri_ready, 1)
                dve.wait_ge(tri_ready, 3 * t + 3)
            for t in range(TB):
                dve.wait_ge(triT_done, t + 1)
                step(nc.vector.tensor_copy(tab[:, :, t * P:(t + 1) * P],
                                           ps[:, 4 + t, 0:3 * P].rearrange("p (w t) -> p w t", w=3)))
            settle()
            dve.wait_ge(triT_done, TB)
            step(nc.vector.tensor_copy(tab_hi[:], tab[:, 0, :]))
            settle()
            step(nc.vector.tensor_tensor(tab_lo[:], tab[:, 0, :], tab_hi[:].bitcast(F32), ALU.subtract))
            settle()

            iota_b = bc(iota, 1, BATCH)

            def one_hots(i, b, q, first):
                n = i * MAIN_BATCHES + b
                t0 = n * BATCH

                def col(ap):
                    return bc(ap, 2, NK)
                if not first:
                    dve.wait_ge(gate_done, n - 1)
                nc.vector.tensor_tensor(oh2[:, q, :, :], iota_b, col(tab[:, 2, bass.ds(t0, BATCH)]), ALU.is_equal
                                        ).then_inc(oh_ready, 1)
                nc.vector.tensor_tensor(oh1[:, q, :, :], iota_b, col(tab[:, 1, bass.ds(t0, BATCH)]), ALU.is_equal
                                        ).then_inc(oh_step, 1)
                dve.wait_ge(oh_step, n + 1)
                nc.vector.tensor_tensor(gate_hi[:, q, :, :], oh1[:, q, :, :],
                                        col(tab_hi[:, bass.ds(t0, BATCH)].bitcast(F32)), ALU.mult
                                        ).then_inc(oh_ready, 1)
                nc.vector.tensor_tensor(gate_lo[:, q, :, :], oh1[:, q, :, :], col(tab_lo[:, bass.ds(t0, BATCH)]),
                                        ALU.mult).then_inc(oh_ready, 1)

            for b in range(MAIN_BATCHES):
                one_hots(0, b, b % 2, b < 2)
            with dve.Fori(1, MAIN_TRIPS) as i:
                for b in range(MAIN_BATCHES):
                    one_hots(i, b, b % 2, False)

            def weights(g, q, first=False):
                dve.wait_ge(actg_in[q], (g - q) * 8 + 16)
                dve.wait_ge(gates_in[q], (g - q) * 8 + 16)
                if not first:
                    dve.wait_ge(wlo_ready, g)
                nc.vector.tensor_tensor(
                    w32[:].rearrange("p n (c t) -> p n c t", t=CHUNK),
                    act_in[:, q, :, :].rearrange("p n (c t) -> p n c t", t=CHUNK),
                    gates[:, q, :, :, :].rearrange("p c n t -> p n c t"), ALU.mult).then_inc(w_ready, 1)

            def split_w(g, q):
                dve.wait_ge(whi_ready, g + 1)
                nc.vector.tensor_tensor(w_lo[:, q, :, :], w32[:], w_hi[:, q, :, :].bitcast(F32),
                                        ALU.subtract).then_inc(wlo_ready, 1)

            def add_y(g, o):
                t, half = divmod(o, 2)
                dve.wait_ge(y_done, g * 8 + (o + 1))
                v = x_res[:, t, half * 512:(half + 1) * 512]
                nc.vector.tensor_tensor(v, v, ps[:, o, :], ALU.add).then_inc(y_added, 1)

            def second(i, last=False):
                for q in range(2):
                    g = i * 2 + q
                    if not (last and q == 1):
                        weights(g + 1, 1 - q)
                    for o in range(4):
                        add_y(g, o)
                    if not (last and q == 1):
                        split_w(g + 1, 1 - q)
                    for o in range(4, 8):
                        add_y(g, o)

            weights(0, 0, True)
            split_w(0, 0)
            with dve.Fori(0, GROUPS // 2 - 1) as i:
                second(i)
            second(GROUPS // 2 - 1, True)

        @block.tensor
        def _(pe):
            mm = nc.tensor.matmul

            def start(job):
                n = INDEX[job]
                if n >= 8:
                    emptied(pe, JOBS[n - 8][0])
                return bank(job)

            def done(ins):
                ins.then_inc(bank_done, 1)

            pe.wait_ge(h_ready, TB)
            pe.wait_ge(consts_in, 48)
            for k in range(KD):
                o = start(("hT", k))
                for t in range(TB):
                    last = nc.tensor.transpose(o[:, t * P:(t + 1) * P], h_nat[:, t, k * P:(k + 1) * P], ident)
                done(last)
            emptied(pe, ("hT", KD - 2))
            emptied(pe, ("hT", KD - 1))
            pe.wait_ge(win_in[0], 16)
            for j, c0 in ((("gi",), COL_I), (("gf",), COL_F)):
                o = start(j)
                for k in range(KD):
                    last = mm(o[0:H, :], w_in[:, k, c0:c0 + H], hT[:, k, :], start=k == 0, stop=k == KD - 1)
                done(last)

            def natural(j, t, c0, w):
                o = start(j)
                for k in range(KD):
                    last = mm(o[:, 0:w], hT[:, k, t * P:(t + 1) * P], w_in[:, k, c0:c0 + w],
                              start=k == 0, stop=k == KD - 1)
                done(last)

            for t in range(TB):
                natural(("c", t), t, COL_C, CW)
            for i, (name, c0) in enumerate((("mq", COL_Q), ("mk", COL_K))):
                pe.wait_ge(win_in[1 + i], 16)
                for h in range(H):
                    o = start((name, h))
                    for k in range(KD):
                        last = mm(o, w_in[:, k, c0 + h * DH:c0 + (h + 1) * DH], hT[:, k, :],
                                  start=k == 0, stop=k == KD - 1)
                    done(last)
            for i, (name, c0) in enumerate((("mv", COL_V), ("mo", COL_O))):
                pe.wait_ge(win_in[3 + i], 16)
                for t in range(TB):
                    natural((name, t), t, c0, H * DH)
            pe.wait_ge(c_ready, 2)
            for k in range(3):
                o = start(("cT", k))
                for t in range(TB):
                    last = nc.tensor.transpose(o[:, t * P:(t + 1) * P], c_sq[:, t, k * P:(k + 1) * P], ident)
                done(last)
            pe.wait_ge(wsmall_in, 48)
            emptied(pe, ("cT", 2))
            for t in range(TB):
                for i in range(2):
                    o = start(("q", t, i))
                    for k in range(2):
                        last = mm(o[:, 0:2 * DQK], cT[:, k, t * P:(t + 1) * P],
                                  w_uq[:, k, i * 2 * DQK:(i + 1) * 2 * DQK], start=k == 0, stop=k == 1)
                    done(last)
            for t in range(TB):
                for i in range(2):
                    o = start(("kv", t, i))
                    done(mm(o, cT[:, 2, t * P:(t + 1) * P], w_ukv[:, i * 512:(i + 1) * 512], start=True, stop=True))
            pe.wait_ge(m_ready, 2)
            pe.wait_ge(em_ready, 1)
            o = start(("rowT",))
            for w, row in enumerate((g_u, g_em)):
                for t in range(TB):
                    last = nc.tensor.transpose(o[:, (w * TB + t) * H:(w * TB + t + 1) * H],
                                               row[:, t * P:(t + 1) * P], ident[0:H, 0:H])
            done(last)
            emptied(pe, ("mq", H - 1))
            emptied(pe, ("mk", H - 1))
            emptied(pe, ("mv", TB - 1))
            pe.wait_ge(ones_ready, 1)
            for h in range(H):
                o = start(("negM", h))
                done(mm(o, sel[:, h, :], g_negM[:], start=True, stop=True))
                for s in range(TB):
                    o = start(("S", h, s))
                    done(mm(o[:, 0:(TB - s) * P], mkT[:, h, s * P:(s + 1) * P], mqT[:, h, s * P:], start=True,
                            stop=True))
                emptied(pe, ("S", h, TB - 1))
                for i in range(2):
                    o = start(("num", h, i))
                    for tt in range(2):
                        t = 2 * i + tt
                        for s in range(t + 1):
                            c0 = D_OFF[s] + (t - s) * P
                            last = mm(o[:, tt * (DH + 1):(tt + 1) * (DH + 1)], sT[:, h % 2, c0:c0 + P],
                                      v_aug[:, s, h, :], start=s == 0, stop=s == t)
                    done(last)
            for w in range(4):
                src = q_nat if w < 2 else k_nat
                pe.wait_ge(qk_ready, 4)
                rows, c0 = (DH, 0) if w % 2 == 0 else (ROPE, DH)
                for h in range(H):
                    o = start(("qkT", w, h))
                    for t in range(TB):
                        last = nc.tensor.transpose(o[0:rows, t * P:(t + 1) * P], src[:, t, h, c0:c0 + rows], ident)
                    done(last)
            emptied(pe, ("qkT", 3, H - 2))
            emptied(pe, ("qkT", 3, H - 1))
            units = [(h, t) for h in range(H) for t in range(TB)]
            for n in range(len(units) + 2):
                if n < len(units):
                    h, t = units[n]
                    o = start(("sc", h, t))
                    w = (t + 1) * P
                    mm(o[:, 0:w], qkT[:, 0, h, t * P:w], qkT[:, 2, h, 0:w], start=True, stop=False)
                    done(mm(o[:, 0:w], qkT[0:ROPE, 1, h, t * P:w], qkT[0:ROPE, 3, h, 0:w], start=False, stop=True))
                if 1 <= n <= len(units):
                    h, t = units[n - 1]
                    emptied(pe, ("sc", h, t))
                    o = start(("pT", h, t))
                    for kb in range(t + 1):
                        last = nc.tensor.transpose(o[:, kb * P:(kb + 1) * P],
                                                   p_nat[:, (n - 1) % 3, kb * P:(kb + 1) * P], ident)
                    done(last)
                if n >= 2:
                    h, t = units[n - 2]
                    emptied(pe, ("pT", h, t))
                    o = start(("pv", h, t))
                    for kb in range(t + 1):
                        last = mm(o[:, 0:DH], pT[:, (n - 2) % 3, kb * P:(kb + 1) * P], kv_nat[:, kb, h, 1, :],
                                  start=kb == 0, stop=kb == t)
                    done(last)
            emptied(pe, ("pv", H - 1, TB - 1))
            pe.wait_ge(mixed_ready, 1)
            for k in range(KD):
                o = start(("mT", k))
                for t in range(TB):
                    last = nc.tensor.transpose(o[:, t * P:(t + 1) * P], mixed[:, t, k * P:(k + 1) * P], ident)
                done(last)
            pe.wait_ge(wout_in, 16)
            emptied(pe, ("mT", KD - 2))
            emptied(pe, ("mT", KD - 1))
            for t in range(TB):
                for i in range(2):
                    o = start(("out", t, i))
                    for k in range(KD):
                        last = mm(o, mixT[:, k, t * P:(t + 1) * P], w_out[:, k, i * 512:(i + 1) * 512],
                                  start=k == 0, stop=k == KD - 1)
                    done(last)
            pe.wait_ge(h2_ready, TB)
            for k in range(KD):
                o = start(("h2T", k))
                for t in range(TB):
                    last = nc.tensor.transpose(o[:, t * P:(t + 1) * P], h2_nat[:, t, k * P:(k + 1) * P], ident)
                done(last)
            emptied(pe, ("h2T", KD - 1))
            for h in range(PH):
                pe.wait_ge(wq_in, 16 * 4)
                for s in range(2):
                    n = 2 * h + s
                    o = start(("qry", h, s))
                    for k in range(KD):
                        last = mm(o, w_q[:, k, n * P:(n + 1) * P], h2T[:, k, :], start=k == 0, stop=k == KD - 1)
                    done(last)
                emptied(pe, ("qry", h, 1))
                for i in range(2):
                    o = start(("s12", h, i))
                    for tt in range(2):
                        for s in range(2):
                            c0 = (2 * tt + s) * NK
                            t = 2 * i + tt
                            last = mm(o[:, c0:c0 + NK], qryT[:, (2 * h + s) % 3, t * P:(t + 1) * P],
                                      keysT[:, s, :], start=True, stop=True)
                    done(last)

            def first_product(n, j, first=False):
                pe.wait_ge(ulo_ready, n + 1)
                if not first:
                    pe.wait_ge(act_ready, n - 1)
                o, q = ps[:, j % 2, :], j % 2
                for x, (u, h2) in enumerate(((u_hi, h2_hi), (u_hi, h2_lo), (u_lo, h2_hi))):
                    for k in range(KD):
                        last = mm(o, u[:, q, k, :], h2[:, k, :], start=x + k == 0, stop=x == 2 and k == KD - 1)
                last.then_inc(z_done, 1)

            pe.wait_ge(h2lo_ready, KD)
            emptied(pe, ("s12", PH - 1, 1))
            for j in range(PRE_BODY):
                first_product(j, j, j < 2)
            with pe.Fori(1, PRE_TRIPS) as i:
                for j in range(PRE_BODY):
                    first_product(i * PRE_BODY + j, j)
            for t in range(TB):
                pe.wait_ge(tri_ready, 3 * t + 3)
                for w in range(3):
                    last = nc.tensor.transpose(ps[:, 4 + t, w * P:(w + 1) * P], tri[:, t, w, :], ident)
                last.then_inc(triT_done, 1)

            def gate_matrices(n, q, first=False):
                pe.wait_ge(oh_ready, n * 3 + 3)
                if not first:
                    pe.wait_ge(gate_staged, n - 1)
                for w in range(BATCH):
                    o = ps[:, 2 + q, w * NK:(w + 1) * NK]
                    mm(o, oh2[:, q, w, :], gate_hi[:, q, w, :], start=True, stop=False)
                    last = mm(o, oh2[:, q, w, :], gate_lo[:, q, w, :], start=False, stop=True)
                last.then_inc(gate_done, 1)

            def main(i, first=False):
                b = 0
                for j in range(MAIN_BODY):
                    first_product(i * MAIN_BODY + (PRE + j), j)
                    for _ in range(BATCHES_AT[j]):
                        gate_matrices(i * MAIN_BATCHES + b, b % 2, first and b < 2)
                        b += 1

            main(0, True)
            with pe.Fori(1, MAIN_TRIPS) as i:
                main(i)

            def second(i, first=False):
                for q in range(2):
                    g = i * 2 + q
                    pe.wait_ge(wlo_ready, g + 1)
                    pe.wait_ge(vlo_ready, (g + 1) * GROUP)
                    for o in range(8):
                        t, half = divmod(o, 2)
                        if not (first and q == 0):
                            pe.wait_ge(y_added, g * 8 + (o - 7))
                        ds = slice(half * 512, (half + 1) * 512)
                        for j in range(GROUP):
                            w = w_hi[:, q, j, t * P:(t + 1) * P]
                            mm(ps[:, o, :], w, v_hi[:, q, j, ds], start=j == 0, stop=False)
                            mm(ps[:, o, :], w, v_lo[:, q, j, ds], start=False, stop=False)
                            last = mm(ps[:, o, :], w_lo[:, q, j, t * P:(t + 1) * P], v_hi[:, q, j, ds],
                                      start=False, stop=j == GROUP - 1)
                        last.then_inc(y_done, 1)

            pe.wait_ge(act_ready, E_BLOCKS)
            pe.wait_ge(gate_staged, S // BATCH)
            second(0, True)
            with pe.Fori(1, GROUPS // 2) as i:
                second(i)


def kernel(x, positions, attn_norm_g, w_in, b_igate, b_fgate, mlstm_norm_g, cq_norm_g, w_uq, ckv_norm_g,
           w_ukv, q_norm_g, k_norm_g, w_out, ffn_norm_g, peer_w_q, peer_keys_1, peer_keys_2, peer_u, peer_v):
    import numpy as np
    import concourse.bacc as bacc
    from concourse import mybir
    from concourse.bass_utils import run_bass_kernel_spmd

    def col(v):
        return np.asarray(v).reshape(-1, P).T

    def rows(v):
        return np.broadcast_to(np.asarray(v).reshape(1, -1), (P, np.asarray(v).size))

    r = np.arange(P)
    inv_freq = (np.float32(10000.0) ** (-np.arange(0, ROPE, 2, dtype=np.float32) / np.float32(ROPE)))
    consts = np.concatenate([
        np.eye(P, dtype=np.float32),
        np.broadcast_to(r.astype(np.float32), (P, P)),
        np.where(r[:, None] <= r[None, :], 0.0, NEG).astype(np.float32),
        np.where(r[None, :] <= r[:, None], 0.0, NEG).astype(np.float32),
        np.broadcast_to(inv_freq.astype(np.float32), (P, HALF)),
        rows(q_norm_g), rows(k_norm_g)], axis=1)
    head_rows = np.zeros((H, H, P), np.float32)
    for h in range(H):
        head_rows[h, h, :] = 1.0
    biases = np.zeros((P, 2), np.float32)
    biases[:H, 0] = np.asarray(b_igate)[0]
    biases[:H, 1] = np.asarray(b_fgate)[0]
    vecs = np.concatenate([col(attn_norm_g), col(ffn_norm_g), col(mlstm_norm_g), col(cq_norm_g),
                           col(ckv_norm_g), biases], axis=1)
    arrays = {
        "x": np.asarray(x)[0],
        "positions": np.asarray(positions).reshape(TB, P).T,
        "consts": consts,
        "vecs": vecs,
        "head_rows": head_rows,
        "w_in": np.asarray(w_in)[0],
        "w_uq": np.asarray(w_uq)[0],
        "w_ukv": np.asarray(w_ukv)[0],
        "w_out": np.asarray(w_out)[0],
        "w_q": np.asarray(peer_w_q)[0],
        "keysT": np.stack([np.asarray(peer_keys_1)[0].T, np.asarray(peer_keys_2)[0].T], axis=1),
        "uT": np.asarray(peer_u)[0].reshape(NK, NK, KD, P).transpose(0, 3, 2, 1),
        "v": np.asarray(peer_v)[0].reshape(NK, NK, D),
    }
    arrays = {k: np.ascontiguousarray(v) for k, v in arrays.items()}
    nc = bacc.Bacc("TRN2", target_bir_lowering=False, num_devices=1)
    aps = {k: nc.dram_tensor("in_" + k, v.shape, mybir.dt.from_np(v.dtype), kind="ExternalInput").ap()
           for k, v in arrays.items()}
    aps["out"] = nc.dram_tensor("y", (S, D), mybir.dt.float32, kind="ExternalOutput").ap()
    build(nc, aps)
    res = run_bass_kernel_spmd(nc, [{"in_" + k: v for k, v in arrays.items()}], core_ids=[0])
    return res.results[0]["y"].reshape(1, S, D)
```

```python
from contextlib import ExitStack

import concourse.bass as bass
import numpy as np
from concourse import mybir

F32 = mybir.dt.float32
F32R = mybir.dt.float32r
I32 = mybir.dt.int32
U32 = mybir.dt.uint32
ALU = mybir.AluOpType
ACT = mybir.ActivationFunctionType
AX_X = mybir.AxisListType.X

P = 128
D = 1024
S = 512
TB = S // P
KD = D // P
H = 4
DH = 128
ROPE = 64
HALF = ROPE // 2
DQK = DH + ROPE
QR, KVR = 256, 128
D_IN = 4 * H * DH + 2 * H + QR + KVR + ROPE
COL_Q, COL_K, COL_V, COL_O = 0, H * DH, 2 * H * DH, 3 * H * DH
COL_G = 4 * H * DH
NW = D_IN - COL_G
N_Q = 2 * H
N_KV = N_Q + QR
N_KR = N_KV + KVR
UNIT = 2 * DH
UNITS = COL_G // UNIT
EPS = 1e-6
PH = 8
NK = 128
TOPK = 16
NEG = -1e30
LOWEST = -3.0e38
TWO_PI = 2.0 * np.pi
MAGIC = 1.5 * 2.0**23

RUNS = []
_pos, _a = 0, 0
while _a < TOPK:
    _len = TOPK // (_a + 1)
    _n = 1
    while _a + _n < TOPK and TOPK // (_a + _n + 1) == _len:
        _n += 1
    RUNS.append((_a, _n, _len, _pos))
    _pos += _n * _len
    _a += _n
CAND = _pos

C_ID, C_IOTA, C_MIN, C_NEG, C_FREQ, C_GQ, C_GK = 0, 128, 256, 384, 512, 544, 736
C_W = 928
V_ATT, V_FFN, V_ML, V_CQ, V_CKV, V_BI, V_BF = 0, 8, 16, 20, 22, 23, 24
V_W = 25

E_BLOCKS = NK
GROUP = 4
GROUPS = E_BLOCKS // GROUP
CHUNK = 32
CHUNKS = S // CHUNK
BATCH = 4
PRE_BODY, PRE_TRIPS = 4, 7
MAIN_BODY, MAIN_TRIPS = 12, 8
OH_RING = 4
RING = 4
MAIN_BATCHES = 16
PER_BLOCK = 3 * KD
PER_BATCH = MAIN_BODY * PER_BLOCK // MAIN_BATCHES
BATCHES_IN = [[b for b in range(MAIN_BATCHES) if ((b + 1) * PER_BATCH - 1) // PER_BLOCK == j]
              for j in range(MAIN_BODY)]
PRE = PRE_BODY * PRE_TRIPS
POST = PRE + MAIN_BODY * MAIN_TRIPS
assert POST + RING == E_BLOCKS and PRE_BODY % RING == 0 and MAIN_BODY % RING == 0
assert MAIN_BATCHES * BATCH * MAIN_TRIPS == S and MAIN_BATCHES * BATCH == 2 * CHUNK


def front_jobs():
    jobs = [(("hT", k), "D") for k in range(KD)]
    jobs += [(("c", t), "D") for t in range(TB)] + [(("gi",), "D"), (("gf",), "D")]
    jobs += [(("mq", h), "A") for h in range(H)] + [(("mk", h), "D") for h in range(H)]
    jobs += [(("cT", k), "D") for k in range(3)]
    jobs += [(("q", t, i), "A") for t in range(TB) for i in range(2)]
    jobs += [(("kv", t, i), "D") for t in range(TB) for i in range(2)]
    jobs += [((name, i, t), "A") for name in ("mv", "mo") for i in range(2) for t in range(TB)]
    jobs += [(("rowT",), "D")]
    for h in range(H + 1):
        if h < H:
            jobs += [(("negM", h), "D")] + [(("S", h, s), "D") for s in range(TB)]
            jobs += [(("qkT", h, x), "A") for x in range(H)]
        if h:
            jobs += [(("num", h - 1, i), "A") for i in range(2)]
    units = [(h, t) for h in range(H) for t in range(TB)]
    for n in range(len(units) + 2):
        if n < len(units):
            jobs.append((("sc", *units[n]), "A"))
        if 1 <= n <= len(units):
            jobs.append((("pT", *units[n - 1]), "A"))
        if n >= 2:
            jobs.append((("pv", *units[n - 2]), "D"))
    jobs += [(("mT", k), "DA"[k % 2]) for k in range(KD)]
    jobs += [(("out", t, i), "D") for t in range(TB) for i in range(2)]
    jobs += [(("h2T", k), "D") for k in range(KD)]
    for h in range(PH):
        jobs += [(("qry", h, s), "A") for s in range(2)]
        jobs += [(("s12", h, i), "D") for i in range(2)]
    return jobs


JOBS = front_jobs()
INDEX = {name: n for n, (name, _) in enumerate(JOBS)}
ENGINE_OF = dict(JOBS)
NTH = {name: sum(e == eng for _, e in JOBS[: n + 1]) for n, (name, eng) in enumerate(JOBS)}
D_OFF = [0, 512, 896, 1152]
D_ALL = 1280
MID = 9
LAST_OF_UNIT = [(n, h) for n in ("mq", "mk") for h in (1, 3)] + [(n, i, TB - 1) for n in ("mv", "mo") for i in (0, 1)]


def build(nc, a):
    ctx = ExitStack()
    with ctx:
        base = 16512

        def at(name, kb, shape, dt=F32):
            return nc.alloc_sbuf_tensor_at(name, shape, dt, offset=base + int(kb * 1024))

        def sem(name):
            return ctx.enter_context(nc.semaphore(name))

        fence = ctx.enter_context(nc.sbuf_tensor("whole_sbuf", [P, (212800 // 4)], F32))
        ps = ctx.enter_context(nc.psum_tensor("banks", [P, 8, 512], F32))

        x_res = at("x_res", 0, [P, TB, D])
        consts = at("consts", 16, [P, C_W])
        vecs = at("vecs", 19.75, [P, 32])
        sel = at("head_rows", 20, [H, H, P])
        ident = consts[:, C_ID:C_ID + P]
        iota = consts[:, C_IOTA:C_IOTA + P]
        mask_min = consts[:, C_MIN:C_MIN + P]
        mask_neg = consts[:, C_NEG:C_NEG + P]
        freq = consts[:, C_FREQ:C_FREQ + HALF]
        gq = consts[:, C_GQ:C_GQ + DQK]
        gk = consts[:, C_GK:C_GK + DQK]

        c_raw = at("c_raw", 22, [P, KD, NW])
        c_hi = at("c_hi", 36.5, [P, KD, NW], F32R)
        c_lo = at("c_lo", 51, [P, KD, NW], F32R)
        wi_raw = at("wi_raw", 65.5, [P, 3, KD, UNIT])
        wi_hi = at("wi_hi", 89.5, [P, 2, KD, UNIT], F32R)
        wi_lo = at("wi_lo", 105.5, [P, 2, KD, UNIT], F32R)
        hT_hi = at("hT_hi", 122, [P, KD, S], F32R)
        hT_lo = at("hT_lo", 138, [P, KD, S], F32R)
        mqT = at("mqT", 154, [P, H, S])
        mkT = at("mkT", 162, [P, H, S])
        v_aug = at("v_aug", 170, [P, TB, H, DH + 1])
        og = at("og", 178.5, [P, TB, H * DH])
        h_nat = at("h_nat", 186.5, [P, TB, D])
        x_junk = at("x_junk", 122, [P, D])
        g_i, g_f, g_tmp, g_F, g_u, g_M = [
            at(n, 186.5 + 2 * i, [H, S]) for i, n in enumerate(("g_i", "g_f", "g_tmp", "g_F", "g_u", "g_M"))]
        rtmp = at("rtmp", 198.5, [P, 2, TB, H, HALF])
        c_nat = at("c_nat", 170, [P, TB, NW])
        c_junk = at("c_junk", 177.5, [P, QR])
        cT = at("cT", 177.5, [P, 3, S])
        stat = at("stat", 204, [P, 16, 32])

        q_nat = at("q_nat", 22, [P, TB, H, DQK])
        kv_nat = at("kv_nat", 34, [P, TB, H, 2, DH])
        w_uq = at("w_uq", 50, [P, 2, H * DQK])
        w_ukv = at("w_ukv", 56, [P, 2 * H * DH])
        k_nat = at("k_nat", 50, [P, TB, H, DQK])
        cosin = at("cosin", 62.5, [P, 2, TB, HALF])
        pos_i = at("pos_i", 63.75, [P, TB], I32)
        pos_f = at("pos_f", 63.875, [P, TB])
        junk = at("junk", 64.25, [P, QR])
        ang = at("ang", 202.5, [P, 3, TB, HALF])
        qkT = at("qkT", 65.5, [P, 4, H, S])

        dexp = at("dexp", 97.5, [P, 2, D_ALL])
        sT = at("sT", 107.5, [P, 2, D_ALL])
        numall = at("numall", 117.5, [P, TB, H, DH + 1])
        h_sq = at("h_sq", 126, [P, TB, H, DH])
        mixed = at("mixed", 186.5, [P, TB, D])
        p_nat = at("p_nat", 22, [P, 3, S])
        pT = at("pT", 28, [P, 3, S])
        mixT = at("mixT", 98, [P, KD, S])
        w_out = at("w_out", 134, [P, KD, D])

        h2_nat = at("h2_nat", 114, [P, TB, D])
        h2T = at("h2T", 186, [P, KD, S])
        h2_hi = at("h2_hi", 150, [P, KD, S], F32R)
        h2_lo = at("h2_lo", 166, [P, KD, S], F32R)
        wq_raw = at("wq_raw", 22, [P, 3, KD, UNIT])
        wq_hi = at("wq_hi", 46, [P, 2, KD, UNIT], F32R)
        wq_lo = at("wq_lo", 62, [P, 2, KD, UNIT], F32R)
        qryT = at("qryT", 184, [P, 3, S])
        keysT = at("keysT", 206.25, [P, 2, NK])
        best_v = at("best_v", 86, [P, 2, TB, PH, TOPK])
        best_i = at("best_i", 90, [P, 2, TB, PH, TOPK], U32)
        best_tmp = at("best_tmp", 94, [P, 2, NK])

        u_raw = at("u_raw", 117, [P, 4, KD, P])
        u_hi = at("u_hi", 133, [P, 2, KD, P], F32R)
        u_lo = at("u_lo", 141, [P, 2, KD, P], F32R)
        act_out = at("act_out", 101, [P, RING, S])
        stage = at("stage", 22, [P, 2, NK, CHUNK])
        oh2 = at("oh2", 54, [P, OH_RING, BATCH, NK], F32R)
        oh1 = at("oh1", 62, [P, OH_RING, BATCH, NK])
        gate_rows = at("gate_rows", 70, [P, OH_RING, BATCH, 2, NK], F32R)
        cand = at("cand", 70, [P, PH, CAND])
        pay = at("pay", 71.75, [P, PH, CAND])
        picked = at("picked", 73.5, [P, PH // 2, TOPK, CAND])
        pay_f = at("pay_f", 94, [P, 2, PH, TOPK])
        cand_tmp = at("cand_tmp", 95, [P, PH, CAND])
        iota_c = at("iota_c", 96.75, [P, CAND])
        sc_v = at("sc_v", 97, [P, PH, TOPK])
        sc_i = at("sc_i", 97.5, [P, PH, TOPK], U32)
        sc_f = at("sc_f", 98, [P, PH, TOPK])
        e_f = at("e_f", 98.5, [P, PH, TOPK])
        e_i = at("e_i", 99, [P, 3, PH, TOPK], I32)
        sums = at("sums", 100.5, [P, 2, PH])
        tri = at("tri", 192, [P, TB, 3, PH * TOPK])
        tab = at("tab", 184, [P, 3, S])
        tab_hi = at("tab_hi", 190, [P, S], F32R)
        tab_lo = at("tab_lo", 198, [P, S])

        v_raw = at("v_raw", 22, [P, 4, D])
        v_hi = [at(f"v_hi{q}", kb, [P, GROUP, D], F32R) for q, kb in enumerate((38, 117))]
        v_lo = [at(f"v_lo{q}", kb, [P, GROUP, D], F32R) for q, kb in enumerate((54, 133))]
        act_in = [at(f"act_in{q}", kb, [P, GROUP, S]) for q, kb in enumerate((70, 150))]
        gates = [at(f"gates{q}", kb, [P, CHUNKS, GROUP, CHUNK]) for q, kb in enumerate((78, 158))]
        w32 = at("w32", 86, [P, GROUP, S])
        w_hi = [at(f"w_hi{q}", kb, [P, GROUP, S], F32R) for q, kb in enumerate((182, 166))]
        w_lo = [at(f"w_lo{q}", kb, [P, GROUP, S], F32R) for q, kb in enumerate((190, 174))]

        act_d = nc.dram_tensor("act_scratch", [E_BLOCKS, P, S], F32).ap()
        gate_d = nc.dram_tensor("gate_scratch", [CHUNKS, NK, NK, CHUNK], F32).ap()

        consts_in = sem("consts_in")
        x_in = [sem(f"x_in{t}") for t in range(TB)]
        c_in = sem("c_in")
        wi_in = [sem(f"wi_in{i}") for i in range(3)]
        chi_ready = sem("chi_ready")
        clo_ready = sem("clo_ready")
        wihi_ready = sem("wihi_ready")
        wilo_ready = sem("wilo_ready")
        hhi_ready = sem("hhi_ready")
        keys_in = sem("keys_in")
        pos_in = sem("pos_in")
        wsmall_in = sem("wsmall_in")
        wout_in = sem("wout_in")
        wq_in = [sem(f"wq_in{i}") for i in range(3)]
        wqhi_ready = sem("wqhi_ready")
        wqlo_ready = sem("wqlo_ready")
        bank_done = sem("bank_done")
        freed = {"A": sem("bank_freed_scalar"), "D": sem("bank_freed_vector")}
        dve_step = sem("dve_step")
        x_sq = sem("x_sq")
        exp_ready = sem("exp_ready")
        var_ready = sem("var_ready")
        root_ready = sem("root_ready")
        h_ready = sem("h_ready")
        fabs_ready = sem("fabs_ready")
        ln_ready = sem("ln_ready")
        m_ready = sem("m_ready")
        em_ready = sem("em_ready")
        c_sq = sem("c_sq")
        c_ready = sem("c_ready")
        kr_ready = sem("kr_ready")
        qk_sq = sem("qk_sq")
        ang_ready = sem("ang_ready")
        trig_ready = sem("trig_ready")
        ones_ready = sem("ones_ready")
        dpre_ready = sem("dpre_ready")
        dexp_ready = sem("dexp_ready")
        den_ready = sem("den_ready")
        h_scaled = sem("h_scaled")
        h_sq_ready = sem("h_sq_ready")
        h_summed = sem("h_summed")
        h_root = sem("h_root")
        h_normed = sem("h_normed")
        qk_ready = sem("qk_ready")
        rowmax_ready = sem("rowmax_ready")
        mixed_ready = sem("mixed_ready")
        x2_ready = sem("x2_ready")
        x2_sq = sem("x2_sq")
        h2_ready = sem("h2_ready")
        h2hi_ready = sem("h2hi_ready")
        h2lo_ready = sem("h2lo_ready")
        gate_pre = sem("gate_pre")
        gate_exp = sem("gate_exp")
        tri_ready = sem("tri_ready")
        triT_done = sem("triT_done")
        tab_ready = sem("tab_ready")
        u_in = [sem(f"u_in{i}") for i in range(4)]
        uhi_ready = sem("uhi_ready")
        ulo_ready = sem("ulo_ready")
        z_done = sem("z_done")
        act_ready = sem("act_ready")
        act_saved = [sem(f"act_saved{i}") for i in range(RING)]
        oh_step = sem("oh_step")
        oh_ready = sem("oh_ready")
        gate_done = sem("gate_done")
        gate_upper = sem("gate_upper")
        gate_staged = sem("gate_staged")
        gate_saved = [sem(f"gate_saved{i}") for i in range(2)]
        v_in = [sem(f"v_in{i}") for i in range(4)]
        actg_in = [sem(f"actg_in{i}") for i in range(2)]
        gates_in = [sem(f"gates_in{i}") for i in range(2)]
        vhi_ready = sem("vhi_ready")
        vlo_ready = sem("vlo_ready")
        w_ready = sem("w_ready")
        whi_ready = sem("whi_ready")
        wlo_ready = sem("wlo_ready")
        y_done = sem("y_done")
        y_added = sem("y_added")
        out_saved = sem("out_saved")

        def bank(job):
            return ps[:, INDEX[job] % 8, :]

        def arrived(eng, job):
            eng.wait_ge(bank_done, INDEX[job] + 1)

        def emptied(eng, job):
            eng.wait_ge(freed[ENGINE_OF[job]], NTH[job])

        def free(ins, job):
            ins.then_inc(freed[ENGINE_OF[job]], 1)

        def gate_banks(q):
            return ps[:, 4 + 2 * q:6 + 2 * q, :].rearrange("p b (w x n) -> p (b w) x n", w=BATCH // 2, x=2)

        def staged_at(b):
            chunk, t0 = divmod(b * BATCH, CHUNK)
            return stage[:, chunk, :, t0:t0 + BATCH].rearrange("p n t -> p t n")

        block = ctx.enter_context(nc.Block())

        @block.sync
        def _(sp):
            for t in range(TB):
                sp.dma_start(x_res[:, t, :], a["x"][t * P:(t + 1) * P, :]).then_inc(x_in[t], 16)
            sp.dma_start(consts[:], a["consts"]).then_inc(consts_in, 16)
            sp.dma_start(vecs[:, 0:V_W], a["vecs"]).then_inc(consts_in, 16)
            sp.dma_start(sel[:], a["head_rows"]).then_inc(consts_in, 16)
            w_v = a["w_in"].rearrange("(k p) n -> p k n", p=P)
            sp.dma_start(c_raw[:], w_v[:, :, COL_G:D_IN]).then_inc(c_in, 16)

            def load_unit(r):
                if r >= 3:
                    sp.wait_ge(wilo_ready, r - 2)
                sp.dma_start(wi_raw[:, r % 3, :, :], w_v[:, :, r * UNIT:(r + 1) * UNIT]).then_inc(wi_in[r % 3], 16)

            for r in range(3):
                load_unit(r)
            sp.dma_start(keysT[:], a["keysT"]).then_inc(keys_in, 16)
            arrived(sp, ("c", TB - 1))
            sp.dma_start(w_uq[:], a["w_uq"].rearrange("(k p) n -> p k n", p=P)).then_inc(wsmall_in, 16)
            sp.dma_start(w_ukv[:], a["w_ukv"]).then_inc(wsmall_in, 16)
            sp.dma_start(pos_i[:], a["positions"]).then_inc(pos_in, 16)
            for r in range(3, UNITS):
                load_unit(r)
            arrived(sp, ("S", H - 1, TB - 1))
            sp.dma_start(w_out[:], a["w_out"].rearrange("(k p) n -> p k n", p=P)).then_inc(wout_in, 16)
            arrived(sp, ("pv", H - 1, TB - 1))
            wq_v = a["w_q"].rearrange("(k p) n -> p k n", p=P)
            for h in range(PH):
                if h >= 3:
                    sp.wait_ge(wqlo_ready, h - 2)
                sp.dma_start(wq_raw[:, h % 3, :, :], wq_v[:, :, h * UNIT:(h + 1) * UNIT]).then_inc(wq_in[h % 3], 16)
            arrived(sp, ("h2T", KD - 1))

            def load_u(n, j):
                sp.dma_start(u_raw[:, j % 4, :, :],
                             a["uT"][bass.ds(n, 1)].rearrange("o p k e -> (o p) k e")).then_inc(u_in[j % 4], 16)

            def save_act(n, j):
                sp.wait_ge(act_ready, n + 1)
                sp.dma_start(act_d[bass.ds(n, 1)].rearrange("o p t -> (o p) t"),
                             act_out[:, j % RING, :]).then_inc(act_saved[j % RING], 16)

            for j in range(4):
                load_u(j, j)

            with sp.Fori(0, PRE_TRIPS) as i:
                for j in range(PRE_BODY):
                    n = i * PRE_BODY + j
                    sp.wait_ge(ulo_ready, n + 1)
                    load_u(n + 4, j)
                    save_act(n, j)

            def save_gates(i, chunk):
                sp.wait_ge(gate_staged, i * MAIN_BATCHES + (chunk + 1) * CHUNK // BATCH)
                sp.dma_start(gate_d[bass.ds(i * 2 + chunk, 1)].rearrange("o p n t -> (o p) (n t)"),
                             stage[:, chunk, :, :].rearrange("p n t -> p (n t)")).then_inc(gate_saved[chunk], 16)

            def main(i):
                for j in range(MAIN_BODY):
                    n = i * MAIN_BODY + (PRE + j)
                    sp.wait_ge(ulo_ready, n + 1)
                    load_u(n + 4, j)
                    save_act(n, j)
                    for b in BATCHES_IN[j]:
                        if (b + 2) * BATCH % CHUNK == 0 and b + 2 < MAIN_BATCHES:
                            save_gates(i, (b + 2) * BATCH // CHUNK - 1)
                save_gates(i, 1)

            with sp.Fori(0, MAIN_TRIPS) as i:
                main(i)

            def load_v(n, j):
                sp.dma_start(v_raw[:, j, :], a["v"][bass.ds(n, 1)].rearrange("o p d -> (o p) d")
                             ).then_inc(v_in[j], 16)

            def load_group(g, q):
                sp.dma_start(act_in[q][:], act_d[bass.ds(g * GROUP, GROUP)].rearrange("n p t -> p n t")
                             ).then_inc(actg_in[q], 16)
                sp.dma_start(gates[q][:].rearrange("p c n t -> p c (n t)"),
                             gate_d[:, :, bass.ds(g * GROUP, GROUP), :].rearrange("c p n t -> p c (n t)")
                             ).then_inc(gates_in[q], 16)

            for q in range(2):
                sp.wait_ge(gate_saved[q], 16 * CHUNKS // 2)
            for q in range(RING):
                sp.wait_ge(act_saved[q], 16)
            for j in range(GROUP):
                load_v(j, j)
            load_group(0, 0)
            for j in range(RING):
                save_act(POST + j, j)
            for q in range(RING):
                sp.wait_ge(act_saved[q], 16 * E_BLOCKS // RING)
            sp.wait_ge(z_done, E_BLOCKS)
            load_group(1, 1)

            def second(i):
                for q in range(2):
                    g = i * 2 + q
                    for j in range(GROUP):
                        sp.wait_ge(vlo_ready, g * GROUP + (j + 1))
                        if not isinstance(i, int) or g + 1 < GROUPS:
                            load_v(g * GROUP + (GROUP + j), j)
                    if not isinstance(i, int) or g + 2 < GROUPS:
                        sp.wait_ge(w_ready, g + 1)
                        load_group(g + 2, q)

            with sp.Fori(0, GROUPS // 2 - 1) as i:
                second(i)
            second(GROUPS // 2 - 1)
            for t in range(TB):
                sp.wait_ge(y_added, 8 * (GROUPS - 1) + 2 * t + 2)
                sp.dma_start(a["out"][t * P:(t + 1) * P, :], x_res[:, t, :]).then_inc(out_saved, 16)
            sp.wait_ge(out_saved, 16 * TB)

        @block.gpsimd
        def _(pool):
            def split_unit(r):
                pool.wait_ge(wihi_ready, r + 1)
                nc.gpsimd.tensor_tensor(wi_lo[:, r % 2, :, :], wi_raw[:, r % 3, :, :],
                                        wi_hi[:, r % 2, :, :].bitcast(F32), ALU.subtract).then_inc(wilo_ready, 1)

            for r in range(6):
                split_unit(r)
            pool.wait_ge(kr_ready, 1)
            nc.gpsimd.memset(v_aug[:, :, :, DH:DH + 1], 1.0).then_inc(ones_ready, 1)
            for r in range(6, UNITS):
                split_unit(r)

            def over_width(ap):
                u = ap.rearrange("p (t h) -> p t h", h=H).unsqueeze(3)
                return u.to_broadcast([P, TB, H, DH])
            num = numall[:, :, :, 0:DH]
            emptied(pool, ("num", H - 1, 1))
            pool.wait_ge(den_ready, 1)
            nc.gpsimd.tensor_tensor(num, num, over_width(stat[:, 13, 0:16]), ALU.mult).then_inc(h_scaled, 1)
            pool.wait_ge(h_scaled, 1)
            nc.gpsimd.tensor_tensor(h_sq[:], num, num, ALU.mult).then_inc(h_sq_ready, 1)
            pool.wait_ge(h_root, 1)
            nc.gpsimd.tensor_tensor(num, num, over_width(stat[:, 7, 0:16]), ALU.mult).then_inc(h_normed, 1)
            pool.wait_ge(h_normed, 1)
            nc.gpsimd.tensor_tensor(mixed[:, :, 0:H * DH].rearrange("p t (h d) -> p t h d", h=H), num,
                                    og[:].rearrange("p t (h d) -> p t h d", h=H), ALU.mult).then_inc(mixed_ready, 1)
            for h in range(PH):
                pool.wait_ge(wqhi_ready, h + 1)
                nc.gpsimd.tensor_tensor(wq_lo[:, h % 2, :, :], wq_raw[:, h % 3, :, :],
                                        wq_hi[:, h % 2, :, :].bitcast(F32), ALU.subtract).then_inc(wqlo_ready, 1)

            def split_u(n, j):
                pool.wait_ge(uhi_ready, n + 1)
                nc.gpsimd.tensor_tensor(u_lo[:, j % 2, :, :], u_raw[:, j % 4, :, :],
                                        u_hi[:, j % 2, :, :].bitcast(F32), ALU.subtract).then_inc(ulo_ready, 1)

            with pool.Fori(0, PRE_TRIPS) as i:
                for j in range(PRE_BODY):
                    split_u(i * PRE_BODY + j, j)
            with pool.Fori(0, GROUPS // 2) as i:
                for q in range(2):
                    for j in range(GROUP):
                        pool.wait_ge(vhi_ready, (i * 2 + q) * GROUP + (j + 1))
                        nc.gpsimd.tensor_tensor(v_lo[q][:, j, :], v_raw[:, j, :],
                                                v_hi[q][:, j, :].bitcast(F32), ALU.subtract).then_inc(vlo_ready, 1)

        @block.scalar
        def _(act):
            roots = [0]

            def root(cols):
                roots[0] += 1
                act.wait_ge(var_ready, roots[0])
                nc.scalar.activation(cols, cols, ACT.Sqrt).then_inc(root_ready, 1)

            def copy(out, src):
                return nc.scalar.activation(out, src, ACT.Copy)

            def round_unit(r):
                act.wait_ge(wi_in[r % 3], r // 3 * 16 + 16)
                if r >= 2:
                    arrived(act, LAST_OF_UNIT[r - 2])
                copy(wi_hi[:, r % 2, :, :], wi_raw[:, r % 3, :, :]).then_inc(wihi_ready, 1)

            for t in range(TB):
                act.wait_ge(x_in[t], 16)
                nc.scalar.activation(x_junk[:], x_res[:, t, :], ACT.Square,
                                     accum_out=stat[:, 0, t:t + 1]).then_inc(x_sq, 1)
                act.wait_ge(x_sq, t + 1)
            root(stat[:, 1, 0:TB])
            act.wait_ge(c_in, 16)
            copy(c_hi[:], c_raw[:]).then_inc(chi_ready, 1)
            act.wait_ge(consts_in, 48)
            for k in range(KD):
                arrived(act, ("hT", k))
                nc.scalar.activation(hT_hi[:, k, :], bank(("hT", k)), ACT.Copy,
                                     scale=vecs[:, V_ATT + k:V_ATT + k + 1]).then_inc(hhi_ready, 1)
            round_unit(0)
            round_unit(1)
            for t in range(TB):
                emptied(act, ("c", t))
                for x, (c0, c1) in enumerate(((N_Q, N_KV), (N_KV, N_KR), (N_KR, NW))):
                    nc.scalar.activation(c_junk[:, 0:c1 - c0], c_nat[:, t, c0:c1], ACT.Square,
                                         accum_out=stat[:, 0, 4 + 4 * x + t:5 + 4 * x + t]).then_inc(c_sq, 1)
                    act.wait_ge(c_sq, 3 * t + x + 1)
            root(stat[:, 1, 4:12])
            for h in range(2):
                arrived(act, ("mq", h))
                free(copy(mqT[:, h, :], bank(("mq", h))), ("mq", h))
            round_unit(2)
            act.wait_ge(fabs_ready, 1)
            nc.scalar.activation(g_tmp[:], g_tmp[:], ACT.Exp, scale=-1.0).then_inc(exp_ready, 1)
            act.wait_ge(exp_ready, 1)
            nc.scalar.activation(g_tmp[:], g_tmp[:], ACT.Ln, bias=1.0).then_inc(ln_ready, 1)
            for h in range(2, H):
                arrived(act, ("mq", h))
                free(copy(mqT[:, h, :], bank(("mq", h))), ("mq", h))
            round_unit(3)
            round_unit(4)
            act.wait_ge(m_ready, 1)
            nc.scalar.activation(g_f[:], g_f[:], ACT.Exp, scale=-1.0).then_inc(em_ready, 1)
            round_unit(5)
            for t in range(TB):
                for i in range(2):
                    j = ("q", t, i)
                    arrived(act, j)
                    free(copy(q_nat[:, t, 2 * i:2 * i + 2, :],
                              bank(j)[:, 0:2 * DQK].rearrange("p (h d) -> p h d", h=2)), j)
            emptied(act, ("q", TB - 1, 1))
            for t in range(TB):
                for h in range(H):
                    nc.scalar.activation(junk[:, 0:DQK], q_nat[:, t, h, :], ACT.Square,
                                         accum_out=stat[:, 3, t * H + h:t * H + h + 1]).then_inc(qk_sq, 1)
                    act.wait_ge(qk_sq, t * H + h + 1)

            def take_v(i, t):
                j = ("mv", i, t)
                arrived(act, j)
                free(copy(v_aug[:, t, 2 * i:2 * i + 2, 0:DH],
                          bank(j)[:, 0:UNIT].rearrange("p (h d) -> p h d", h=2)), j)

            act.wait_ge(kr_ready, 1)
            for t in range(TB):
                take_v(0, t)
            round_unit(6)
            emptied(act, ("kv", TB - 1, 1))
            for t in range(TB):
                for h in range(H):
                    nc.scalar.activation(junk[:, 0:DH], kv_nat[:, t, h, 0, :], ACT.Square,
                                         accum_out=stat[:, 3, 16 + t * H + h:17 + t * H + h]).then_inc(qk_sq, 1)
                    act.wait_ge(qk_sq, (TB + t) * H + h + 1)
            for t in range(TB):
                take_v(1, t)
            round_unit(7)
            root(stat[:, 4, 0:32])
            act.wait_ge(ang_ready, 1)
            nc.scalar.activation(cosin[:], ang[:, 0:2, :, :], ACT.Sin).then_inc(trig_ready, 1)
            for i in range(2):
                for t in range(TB):
                    j = ("mo", i, t)
                    arrived(act, j)
                    free(nc.scalar.activation(og[:, t, i * UNIT:(i + 1) * UNIT], bank(j)[:, 0:UNIT],
                                              ACT.Sigmoid), j)
            for h in range(H + 1):
                if h < H:
                    act.wait_ge(dpre_ready, h + 1)
                    nc.scalar.activation(dexp[:, h % 2, :], dexp[:, h % 2, :], ACT.Exp).then_inc(dexp_ready, 1)
                    rows = DH if h % 2 == 0 else ROPE
                    for x in range(H):
                        j = ("qkT", h, x)
                        arrived(act, j)
                        free(copy(qkT[0:rows, h, x, :], bank(j)[0:rows, :]), j)
                if h:
                    for i in range(2):
                        j = ("num", h - 1, i)
                        arrived(act, j)
                        free(copy(numall[:, 2 * i:2 * i + 2, h - 1, :],
                                  bank(j)[:, 0:2 * (DH + 1)].rearrange("p (t d) -> p t d", t=2)), j)
            units = [(h, t) for h in range(H) for t in range(TB)]
            for n in range(len(units) + 1):
                if n == MID:
                    root(stat[:, 6, 0:16])
                if n < len(units):
                    h, t = units[n]
                    j = ("sc", h, t)
                    act.wait_ge(rowmax_ready, n + 1)
                    if n >= 3:
                        arrived(act, ("pT", *units[n - 3]))
                    w = (t + 1) * P
                    free(nc.scalar.activation(p_nat[:, n % 3, 0:w], bank(j)[:, 0:w], ACT.Exp,
                                              bias=stat[:, 8, n:n + 1], scale=float(DQK) ** -0.5,
                                              accum_out=stat[:, 9, n:n + 1]), j)
                if n >= 1:
                    h, t = units[n - 1]
                    j = ("pT", h, t)
                    arrived(act, j)
                    if n >= 4:
                        arrived(act, ("pv", *units[n - 4]))
                    w = (t + 1) * P
                    free(nc.scalar.activation(pT[:, (n - 1) % 3, 0:w], bank(j)[:, 0:w], ACT.Copy), j)
            for k in range(1, KD, 2):
                j = ("mT", k)
                arrived(act, j)
                if k < H:
                    free(nc.scalar.activation(mixT[:, k, :], bank(j), ACT.Copy,
                                              scale=vecs[:, V_ML + k:V_ML + k + 1]), j)
                else:
                    free(nc.scalar.activation(mixT[:, k, :], bank(j), ACT.Copy), j)
            for t in range(TB):
                act.wait_ge(x2_ready, 2 * t + 2)
                nc.scalar.activation(h2_nat[:, 0, :], x_res[:, t, :], ACT.Square,
                                     accum_out=stat[:, 10, t:t + 1]).then_inc(x2_sq, 1)
                act.wait_ge(x2_sq, t + 1)
            root(stat[:, 11, 0:TB])

            def round_q(h):
                act.wait_ge(wq_in[h % 3], h // 3 * 16 + 16)
                if h >= 2:
                    arrived(act, ("qry", h - 2, 1))
                copy(wq_hi[:, h % 2, :, :], wq_raw[:, h % 3, :, :]).then_inc(wqhi_ready, 1)

            round_q(0)
            round_q(1)
            for k in range(KD):
                emptied(act, ("h2T", k))
                nc.scalar.activation(h2_hi[:, k, :], h2T[:, k, :], ACT.Copy).then_inc(h2hi_ready, 1)
            for h in range(PH):
                for s in range(2):
                    j = ("qry", h, s)
                    n = 2 * h + s
                    arrived(act, j)
                    if n >= 3:
                        arrived(act, ("s12", (n - 3) // 2, 1))
                    free(copy(qryT[:, n % 3, :], bank(j)), j)
                if h + 2 < PH:
                    round_q(h + 2)

            def round_u(n, j, first=False):
                act.wait_ge(u_in[j % 4], n // 4 * 16 + 16 if isinstance(n, int) else (n - j % 4) * 4 + 16)
                if not first:
                    act.wait_ge(z_done, n - 1)
                nc.scalar.activation(u_hi[:, j % 2, :, :], u_raw[:, j % 4, :, :], ACT.Copy).then_inc(uhi_ready, 1)

            def gelu(n, j, first=False):
                act.wait_ge(z_done, n + 1)
                if not first:
                    act.wait_ge(act_saved[j % RING], (n - j % RING) * (16 // RING))
                nc.scalar.activation(act_out[:, j % RING, :], ps[:, j % RING, :], ACT.Gelu).then_inc(act_ready, 1)

            def trip(i):
                for j in range(PRE_BODY):
                    n = i * PRE_BODY + j
                    round_u(n + 1, j + 1, isinstance(n, int) and n == 0)
                    gelu(n, j, isinstance(i, int) and i == 0)

            emptied(act, ("s12", PH - 1, 1))
            round_u(0, 0, True)
            trip(0)
            for t in range(TB):
                trip(1 + t)
                act.wait_ge(gate_pre, t + 1)
                nc.scalar.activation(sc_v[:], sc_v[:], ACT.Exp).then_inc(gate_exp, 1)
            with act.Fori(1 + TB, PRE_TRIPS) as i:
                trip(i)

            def main(i, first=False):
                for j in range(MAIN_BODY):
                    n = i * MAIN_BODY + (PRE + j)
                    round_u(n + 1, j + 1)
                    for b in BATCHES_IN[j]:
                        act.wait_ge(gate_done, i * MAIN_BATCHES + (b + 1))
                        if b * BATCH % CHUNK == 0 and not first:
                            act.wait_ge(gate_saved[b * BATCH // CHUNK], i * 16)
                        nc.scalar.activation(staged_at(b), gate_banks(b % 2)[:, :, 0, :], ACT.Copy
                                             ).then_inc(gate_upper, 1)
                    gelu(n, j)

            main(0, True)
            with act.Fori(1, MAIN_TRIPS) as i:
                main(i)

            def round_v(g, q, j, first=False):
                act.wait_ge(v_in[j], g * 16 + 16)
                if not first:
                    act.wait_ge(y_done, (g - 1) * 8)
                nc.scalar.activation(v_hi[q][:, j, :], v_raw[:, j, :], ACT.Copy).then_inc(vhi_ready, 1)

            def round_w(g, q):
                act.wait_ge(w_ready, g + 1)
                nc.scalar.activation(w_hi[q][:], w32[:], ACT.Copy).then_inc(whi_ready, 1)

            for j in range(RING):
                if j + 1 < RING:
                    round_u(POST + j + 1, j + 1)
                gelu(POST + j, j)
                if j == 1:
                    for k in range(GROUP):
                        round_v(0, 0, k, True)
            round_w(0, 0)
            act.wait_ge(z_done, E_BLOCKS)
            for j in range(GROUP):
                round_v(1, 1, j, True)
            round_w(1, 1)
            with act.Fori(1, GROUPS // 2) as i:
                for q in range(2):
                    for j in range(GROUP):
                        round_v(i * 2 + q, q, j)
                    round_w(i * 2 + q, q)

        @block.vector
        def _(dve):
            steps = [0]

            def step(ins):
                steps[0] += 1
                ins.then_inc(dve_step, 1)

            def settle():
                dve.wait_ge(dve_step, steps[0])

            roots = [0]

            def inv_root(sums_ap, n, var, out):
                roots[0] += 1
                nc.vector.tensor_scalar(var, sums_ap, 1.0 / n, EPS, ALU.mult, ALU.add).then_inc(var_ready, 1)
                dve.wait_ge(root_ready, roots[0])
                step(nc.vector.reciprocal(out, var))
                settle()

            def bc(ap, axis, n):
                u = ap.unsqueeze(axis)
                shape = list(u.shape)
                shape[axis] = n
                return u.to_broadcast(shape)

            dve.wait_ge(x_sq, TB)
            inv_root(stat[:, 0, 0:TB], D, stat[:, 1, 0:TB], stat[:, 2, 0:TB])
            for t in range(TB):
                nc.vector.tensor_scalar(h_nat[:, t, :], x_res[:, t, :], stat[:, 2, t:t + 1], None,
                                        ALU.mult).then_inc(h_ready, 1)
            dve.wait_ge(chi_ready, 1)
            nc.vector.tensor_tensor(c_lo[:], c_raw[:], c_hi[:].bitcast(F32), ALU.subtract).then_inc(clo_ready, 1)
            dve.wait_ge(consts_in, 48)
            for k in range(KD):
                dve.wait_ge(hhi_ready, k + 1)
                free(nc.vector.scalar_tensor_tensor(
                    out=hT_lo[:, k, :], in0=bank(("hT", k)), scalar=vecs[:, V_ATT + k:V_ATT + k + 1],
                    in1=hT_hi[:, k, :].bitcast(F32), op0=ALU.mult, op1=ALU.subtract), ("hT", k))
            for t in range(TB):
                arrived(dve, ("c", t))
                free(nc.vector.tensor_copy(c_nat[:, t, :], bank(("c", t))[:, 0:NW]), ("c", t))
            for j, row, v in ((("gi",), g_i, V_BI), (("gf",), g_f, V_BF)):
                arrived(dve, j)
                free(nc.vector.tensor_scalar(row[:], bank(j)[0:H, :], vecs[0:H, v:v + 1], None, ALU.add), j)
            emptied(dve, ("gf",))
            step(nc.vector.tensor_scalar(g_F[:], g_f[:], -1.0, None, ALU.mult))
            settle()
            nc.vector.tensor_tensor(g_tmp[:], g_f[:], g_F[:], ALU.max).then_inc(fabs_ready, 1)
            dve.wait_ge(c_sq, 3 * TB)
            step(nc.vector.tensor_scalar(stat[:, 0, 8:12], stat[:, 0, 8:12], float(QR) / KVR, None, ALU.mult))
            settle()
            inv_root(stat[:, 0, 4:12], QR, stat[:, 1, 4:12], stat[:, 2, 4:12])
            for c0, c1, x in ((N_Q, N_KV, 4), (N_KV, N_KR, 8)):
                v = c_nat[:, :, c0:c1]
                nc.vector.tensor_tensor(v, v, bc(stat[:, 2, x:x + 4], 2, c1 - c0), ALU.mult).then_inc(c_ready, 1)
            dve.wait_ge(ln_ready, 1)
            step(nc.vector.scalar_tensor_tensor(out=g_f[:], in0=g_f[:], scalar=0.0, in1=g_tmp[:],
                                                op0=ALU.min, op1=ALU.subtract))
            settle()
            step(nc.vector.memset(g_tmp[:], 1.0))
            settle()
            step(nc.vector.tensor_tensor_scan(out=g_F[:], data0=g_tmp[:], data1=g_f[:], initial=0.0,
                                              op0=ALU.mult, op1=ALU.add))
            settle()
            step(nc.vector.tensor_tensor(g_u[:], g_i[:], g_F[:], ALU.subtract))
            settle()
            step(nc.vector.tensor_tensor_scan(out=g_M[:], data0=g_tmp[:], data1=g_u[:], initial=0.0,
                                              op0=ALU.mult, op1=ALU.max))
            settle()
            nc.vector.tensor_tensor(g_f[:], g_F[:], g_M[:], ALU.add).then_inc(m_ready, 1)
            nc.vector.tensor_scalar(g_i[:], g_M[:], -1.0, None, ALU.mult).then_inc(m_ready, 1)
            dve.wait_ge(pos_in, 16)
            step(nc.vector.tensor_copy(pos_f[:], pos_i[:]))
            settle()
            for t in range(TB):
                step(nc.vector.tensor_scalar(ang[:, 0, t, :], freq, pos_f[:, t:t + 1], None, ALU.mult))
            settle()
            step(nc.vector.tensor_scalar(ang[:, 1, :, :], ang[:, 0, :, :], 1.0 / TWO_PI, MAGIC, ALU.mult, ALU.add))
            settle()
            step(nc.vector.tensor_scalar(ang[:, 1, :, :], ang[:, 1, :, :], MAGIC, None, ALU.subtract))
            settle()
            c1 = 6.28125
            c2 = float(np.float32(np.round((TWO_PI - c1) * 2**20) / 2**20))
            c3 = float(TWO_PI - c1 - c2)
            for c in (c1, c2, c3):
                step(nc.vector.scalar_tensor_tensor(out=ang[:, 0, :, :], in0=ang[:, 1, :, :], scalar=-c,
                                                    in1=ang[:, 0, :, :], op0=ALU.mult, op1=ALU.add))
                settle()
            pi = float(np.float32(3.1415925))
            step(nc.vector.tensor_scalar(ang[:, 0, :, :], ang[:, 0, :, :], pi, -pi, ALU.min, ALU.max))
            settle()
            step(nc.vector.tensor_scalar(ang[:, 2, :, :], ang[:, 0, :, :], -1.0, None, ALU.mult))
            settle()
            step(nc.vector.tensor_tensor(ang[:, 1, :, :], ang[:, 0, :, :], ang[:, 2, :, :], ALU.max))
            settle()
            nc.vector.tensor_scalar(ang[:, 1, :, :], ang[:, 1, :, :], -1.0, TWO_PI / 4, ALU.mult,
                                    ALU.add).then_inc(ang_ready, 1)
            for h in range(H):
                arrived(dve, ("mk", h))
                free(nc.vector.tensor_copy(mkT[:, h, :], bank(("mk", h))), ("mk", h))
            for k in range(3):
                j = ("cT", k)
                arrived(dve, j)
                free(nc.vector.tensor_scalar(cT[:, k, :], bank(j), vecs[:, V_CQ + k:V_CQ + k + 1], None,
                                             ALU.mult), j)
            for t in range(TB):
                for i in range(2):
                    j = ("kv", t, i)
                    arrived(dve, j)
                    free(nc.vector.tensor_copy(kv_nat[:, t, 2 * i:2 * i + 2, :, :],
                                               bank(j).rearrange("p (h w d) -> p h w d", h=2, w=2)), j)
            nc.vector.tensor_copy(k_nat[:, :, :, DH:DQK], bc(c_nat[:, :, N_KR:NW], 2, H)).then_inc(kr_ready, 1)

            dve.wait_ge(qk_sq, 2 * TB * H)
            k_sums = stat[:, 3, 16:32].rearrange("p (t h) -> p t h", h=H)
            step(nc.vector.tensor_tensor(k_sums, k_sums, bc(stat[:, 0, 12:16], 2, H), ALU.add))
            settle()
            inv_root(stat[:, 3, 0:32], DQK, stat[:, 4, 0:32], stat[:, 5, 0:32])
            rq = stat[:, 5, 0:16].rearrange("p (t h) -> p t h", h=H)
            rk = stat[:, 5, 16:32].rearrange("p (t h) -> p t h", h=H)
            dve.wait_ge(kr_ready, 1)
            emptied(dve, ("kv", TB - 1, 1))
            step(nc.vector.tensor_tensor(q_nat[:], q_nat[:], bc(rq, 3, DQK), ALU.mult))
            step(nc.vector.tensor_tensor(k_nat[:, :, :, 0:DH], kv_nat[:, :, :, 0, :], bc(rk, 3, DH), ALU.mult))
            step(nc.vector.tensor_tensor(k_nat[:, :, :, DH:DQK], k_nat[:, :, :, DH:DQK], bc(rk, 3, ROPE),
                                         ALU.mult))
            settle()
            for x_nat, g in ((q_nat, gq), (k_nat, gk)):
                v = x_nat[:].rearrange("p t h d -> p (t h) d")
                step(nc.vector.tensor_tensor(v, v, bc(g, 1, TB * H), ALU.mult))
            dve.wait_ge(trig_ready, 1)
            settle()
            sin_t = bc(cosin[:, 0, :, :], 2, H)
            cos_t = bc(cosin[:, 1, :, :], 2, H)
            for x, x_nat in enumerate((q_nat, k_nat)):
                r1 = x_nat[:, :, :, DH:DH + HALF]
                r2 = x_nat[:, :, :, DH + HALF:DQK]
                step(nc.vector.tensor_tensor(rtmp[:, 0, :, :, :], r2, sin_t, ALU.mult))
                step(nc.vector.tensor_tensor(rtmp[:, 1, :, :, :], r1, sin_t, ALU.mult))
                settle()
                step(nc.vector.tensor_tensor(r1, r1, cos_t, ALU.mult))
                step(nc.vector.tensor_tensor(r2, r2, cos_t, ALU.mult))
                settle()
                nc.vector.tensor_tensor(r1, r1, rtmp[:, 0, :, :, :], ALU.subtract).then_inc(qk_ready, 1)
                nc.vector.tensor_tensor(r2, r2, rtmp[:, 1, :, :, :], ALU.add).then_inc(qk_ready, 1)
                dve.wait_ge(qk_ready, 2 * x + 2)

            arrived(dve, ("rowT",))
            free(nc.vector.tensor_copy(stat[:, 12, 0:32], bank(("rowT",))[:, 0:32]), ("rowT",))
            emptied(dve, ("rowT",))
            u_col = stat[:, 12, 0:16].rearrange("p (t h) -> p t h", h=H)
            em_col = stat[:, 12, 16:32]
            for h in range(H):
                j = ("negM", h)
                arrived(dve, j)
                neg_m = bank(j)
                for s in range(TB):
                    lo = D_OFF[s]
                    step(nc.vector.scalar_tensor_tensor(
                        out=dexp[:, h % 2, lo:lo + P], in0=neg_m[:, s * P:(s + 1) * P],
                        scalar=u_col[:, s, h:h + 1], in1=mask_min, op0=ALU.add, op1=ALU.min))
                    if s < TB - 1:
                        step(nc.vector.tensor_scalar(dexp[:, h % 2, lo + P:lo + (TB - s) * P],
                                                     neg_m[:, (s + 1) * P:], u_col[:, s, h:h + 1], None, ALU.add))
                settle()
                dve.sem_inc(freed["D"], 1)
                dve.sem_inc(dpre_ready, 1)
                dve.wait_ge(dexp_ready, h + 1)
                if h >= 2:
                    arrived(dve, ("num", h - 2, 1))
                for s in range(TB):
                    j = ("S", h, s)
                    arrived(dve, j)
                    lo, w = D_OFF[s], (TB - s) * P
                    free(nc.vector.scalar_tensor_tensor(
                        out=sT[:, h % 2, lo:lo + w], in0=bank(j)[:, 0:w], scalar=float(DH) ** -0.5,
                        in1=dexp[:, h % 2, lo:lo + w], op0=ALU.mult, op1=ALU.mult), j)
                emptied(dve, ("S", h, TB - 1))

            emptied(dve, ("num", H - 1, 1))
            den = numall[:, :, :, DH]
            dd = stat[:, 13, 0:16].rearrange("p (t h) -> p t h", h=H)
            em3 = em_col.rearrange("p (t h) -> p t h", h=H)
            step(nc.vector.tensor_scalar(dd, den, -1.0, None, ALU.mult))
            settle()
            step(nc.vector.tensor_tensor(dd, dd, den, ALU.max))
            settle()
            step(nc.vector.tensor_tensor(dd, dd, em3, ALU.max))
            settle()
            nc.vector.reciprocal(dd, dd).then_inc(den_ready, 1)
            units = [(h, t) for h in range(H) for t in range(TB)]
            for n in range(len(units) + 2):
                if n == MID:
                    dve.wait_ge(h_sq_ready, 1)
                    step(nc.vector.reduce_sum(stat[:, 14, 0:16].rearrange("p (t h) -> p t h", h=H), h_sq[:],
                                              axis=AX_X))
                    settle()
                    inv_root(stat[:, 14, 0:16], DH, stat[:, 6, 0:16], stat[:, 7, 0:16])
                    dve.sem_inc(h_root, 1)
                if n < len(units):
                    h, t = units[n]
                    j = ("sc", h, t)
                    arrived(dve, j)
                    w = t * P
                    step(nc.vector.tensor_tensor(bank(j)[:, w:w + P], bank(j)[:, w:w + P], mask_neg, ALU.add))
                    settle()
                    step(nc.vector.reduce_max(stat[:, 13, 16 + n % 16:17 + n % 16], bank(j)[:, 0:w + P], axis=AX_X))
                    settle()
                    nc.vector.tensor_scalar(stat[:, 8, n:n + 1], stat[:, 13, 16 + n % 16:17 + n % 16],
                                            -float(DQK) ** -0.5, None, ALU.mult).then_inc(rowmax_ready, 1)
                if n >= 2:
                    h, t = units[n - 2]
                    j = ("pv", h, t)
                    emptied(dve, ("sc", h, t))
                    step(nc.vector.reciprocal(stat[:, 9, n - 2:n - 1], stat[:, 9, n - 2:n - 1]))
                    arrived(dve, j)
                    settle()
                    c0 = (H + h) * DH
                    free(nc.vector.tensor_scalar(mixed[:, t, c0:c0 + DH], bank(j)[:, 0:DH],
                                                 stat[:, 9, n - 2:n - 1], None, ALU.mult), j)
            for k in range(0, KD, 2):
                j = ("mT", k)
                arrived(dve, j)
                if k < H:
                    free(nc.vector.tensor_scalar(mixT[:, k, :], bank(j), vecs[:, V_ML + k:V_ML + k + 1], None,
                                                 ALU.mult), j)
                else:
                    free(nc.vector.tensor_copy(mixT[:, k, :], bank(j)), j)
            for t in range(TB):
                for i in range(2):
                    j = ("out", t, i)
                    arrived(dve, j)
                    v = x_res[:, t, i * 512:(i + 1) * 512]
                    step(nc.vector.tensor_tensor(v, v, bank(j), ALU.add))
                    settle()
                    dve.sem_inc(x2_ready, 1)
                    dve.sem_inc(freed["D"], 1)
            dve.wait_ge(x2_sq, TB)
            inv_root(stat[:, 10, 0:TB], D, stat[:, 11, 0:TB], stat[:, 15, 0:TB])
            for t in range(TB):
                nc.vector.tensor_scalar(h2_nat[:, t, :], x_res[:, t, :], stat[:, 15, t:t + 1], None,
                                        ALU.mult).then_inc(h2_ready, 1)
            for k in range(KD):
                j = ("h2T", k)
                arrived(dve, j)
                free(nc.vector.tensor_scalar(h2T[:, k, :], bank(j), vecs[:, V_FFN + k:V_FFN + k + 1], None,
                                             ALU.mult), j)
            for k in range(KD):
                dve.wait_ge(h2hi_ready, k + 1)
                nc.vector.tensor_tensor(h2_lo[:, k, :], h2T[:, k, :], h2_hi[:, k, :].bitcast(F32),
                                        ALU.subtract).then_inc(h2lo_ready, 1)
            for h in range(PH):
                for i in range(2):
                    j = ("s12", h, i)
                    arrived(dve, j)
                    for tt in range(2):
                        t = 2 * i + tt
                        sc = [bank(j)[:, (2 * tt + s) * NK:(2 * tt + s + 1) * NK] for s in range(2)]
                        bv = [best_v[:, s, t, h, :] for s in range(2)]
                        bi = [best_i[:, s, t, h, :] for s in range(2)]
                        for s in range(2):
                            step(nc.vector.max(bv[s][:, 0:8], sc[s]))
                        settle()
                        for s in range(2):
                            step(nc.vector.max_index(bi[s][:, 0:8], bv[s][:, 0:8], sc[s]))
                            step(nc.vector.match_replace(best_tmp[:, s, :], bv[s][:, 0:8], sc[s], LOWEST))
                        settle()
                        for s in range(2):
                            step(nc.vector.max(bv[s][:, 8:16], best_tmp[:, s, :]))
                        settle()
                        for s in range(2):
                            step(nc.vector.max_index(bi[s][:, 8:16], bv[s][:, 8:16], best_tmp[:, s, :]))
                        settle()
                    dve.sem_inc(freed["D"], 1)
            step(nc.vector.tensor_copy(iota_c[:], consts[:, C_IOTA:C_IOTA + CAND]))
            for t in range(TB):
                step(nc.vector.tensor_scalar(pay_f[:, 0, :, :], best_i[:, 0, t, :, :], float(NK), None, ALU.mult))
                step(nc.vector.tensor_copy(pay_f[:, 1, :, :], best_i[:, 1, t, :, :]))
                settle()
                for src, dst in ((best_v[:, :, t, :, :], cand), (pay_f[:], pay)):
                    for a0, na, nb, at0 in RUNS:
                        out = dst[:, :, at0:at0 + na * nb].rearrange("p h (a b) -> p h a b", a=na)
                        step(nc.vector.tensor_tensor(out, bc(src[:, 0, :, a0:a0 + na], 3, nb),
                                                     bc(src[:, 1, :, 0:nb], 2, na), ALU.add))
                settle()
                for h in range(PH):
                    step(nc.vector.max(sc_v[:, h, 0:8], cand[:, h, :]))
                settle()
                for h in range(PH):
                    step(nc.vector.max_index(sc_i[:, h, 0:8], sc_v[:, h, 0:8], cand[:, h, :]))
                    step(nc.vector.match_replace(cand_tmp[:, h, :], sc_v[:, h, 0:8], cand[:, h, :], LOWEST))
                settle()
                for h in range(PH):
                    step(nc.vector.max(sc_v[:, h, 8:16], cand_tmp[:, h, :]))
                settle()
                for h in range(PH):
                    step(nc.vector.max_index(sc_i[:, h, 8:16], sc_v[:, h, 8:16], cand_tmp[:, h, :]))
                settle()
                step(nc.vector.tensor_copy(sums[:, 1, :], sc_v[:, :, 0]))
                step(nc.vector.tensor_copy(sc_f[:], sc_i[:]))
                settle()
                nc.vector.tensor_tensor(sc_v[:], sc_v[:], bc(sums[:, 1, :], 2, TOPK), ALU.subtract
                                        ).then_inc(gate_pre, 1)
                for hh in range(2):
                    hs = slice(hh * PH // 2, (hh + 1) * PH // 2)
                    step(nc.vector.tensor_tensor(
                        picked[:], bc(sc_f[:, hs, :], 3, CAND),
                        bc(bc(iota_c[:], 1, TOPK), 1, PH // 2), ALU.is_equal))
                    settle()
                    step(nc.vector.tensor_tensor(picked[:], picked[:], bc(pay[:, hs, :], 2, TOPK), ALU.mult))
                    settle()
                    step(nc.vector.reduce_sum(e_f[:, hs, :], picked[:], axis=AX_X))
                    settle()
                step(nc.vector.tensor_copy(e_i[:, 0, :, :], e_f[:]))
                settle()
                step(nc.vector.tensor_scalar(e_i[:, 1, :, :], e_i[:, 0, :, :], 7, None, ALU.logical_shift_right))
                step(nc.vector.tensor_scalar(e_i[:, 2, :, :], e_i[:, 0, :, :], NK - 1, None, ALU.bitwise_and))
                settle()
                for s in range(2):
                    nc.vector.tensor_copy(tri[:, t, 1 + s, :].rearrange("p (h k) -> p h k", h=PH),
                                          e_i[:, 1 + s, :, :]).then_inc(tri_ready, 1)
                dve.wait_ge(gate_exp, t + 1)
                step(nc.vector.reduce_sum(sums[:, 0, :], sc_v[:], axis=AX_X))
                settle()
                step(nc.vector.reciprocal(sums[:, 0, :], sums[:, 0, :]))
                settle()
                nc.vector.tensor_tensor(tri[:, t, 0, :].rearrange("p (h k) -> p h k", h=PH), sc_v[:],
                                        bc(sums[:, 0, :], 2, TOPK), ALU.mult).then_inc(tri_ready, 1)
                dve.wait_ge(tri_ready, 3 * t + 3)
            for t in range(TB):
                dve.wait_ge(triT_done, t + 1)
                step(nc.vector.tensor_copy(tab[:, :, t * P:(t + 1) * P],
                                           ps[:, 4 + t, 0:3 * P].rearrange("p (w t) -> p w t", w=3)))
            settle()
            dve.wait_ge(triT_done, TB)
            step(nc.vector.tensor_copy(tab_hi[:], tab[:, 0, :]))
            settle()
            step(nc.vector.tensor_tensor(tab_lo[:], tab[:, 0, :], tab_hi[:].bitcast(F32), ALU.subtract))
            settle()

            iota_b = bc(iota, 1, BATCH)

            def split_u(n, j):
                dve.wait_ge(uhi_ready, n + 1)
                nc.vector.tensor_tensor(u_lo[:, j % 2, :, :], u_raw[:, j % RING, :, :],
                                        u_hi[:, j % 2, :, :].bitcast(F32), ALU.subtract).then_inc(ulo_ready, 1)

            def one_hots(i, b, first):
                n = i * MAIN_BATCHES + b
                t0 = n * BATCH
                q = b % OH_RING

                def col(ap):
                    return bc(ap, 2, NK)
                if not first:
                    dve.wait_ge(gate_done, n - (OH_RING - 1))
                nc.vector.tensor_tensor(oh2[:, q, :, :], iota_b, col(tab[:, 2, bass.ds(t0, BATCH)]), ALU.is_equal
                                        ).then_inc(oh_ready, 1)
                nc.vector.tensor_tensor(oh1[:, q, :, :], iota_b, col(tab[:, 1, bass.ds(t0, BATCH)]), ALU.is_equal
                                        ).then_inc(oh_step, 1)
                dve.wait_ge(oh_step, n + 1)
                nc.vector.tensor_tensor(gate_rows[:, q, :, 0, :], oh1[:, q, :, :],
                                        col(tab_hi[:, bass.ds(t0, BATCH)].bitcast(F32)), ALU.mult
                                        ).then_inc(oh_ready, 1)
                nc.vector.tensor_tensor(gate_rows[:, q, :, 1, :], oh1[:, q, :, :],
                                        col(tab_lo[:, bass.ds(t0, BATCH)]), ALU.mult).then_inc(oh_ready, 1)

            def stage_gates(i, b, q):
                dve.wait_ge(gate_upper, i * MAIN_BATCHES + (b + 1))
                staged = staged_at(b)
                nc.vector.tensor_tensor(staged, staged, gate_banks(q)[:, :, 1, :], ALU.add).then_inc(gate_staged, 1)

            def main(i, first=False, last=False):
                for j in range(MAIN_BODY):
                    split_u(i * MAIN_BODY + (PRE + j + 1), j + 1)
                    for b in BATCHES_IN[j]:
                        if b:
                            stage_gates(i, b - 1, (b - 1) % 2)
                        elif not first:
                            stage_gates(i - 1, MAIN_BATCHES - 1, 1)
                        if not (last and b + 2 >= MAIN_BATCHES):
                            one_hots(i, b + 2, first and b + 2 < OH_RING)

            split_u(PRE, 0)
            one_hots(0, 0, True)
            one_hots(0, 1, True)
            main(0, True)
            with dve.Fori(1, MAIN_TRIPS - 1) as i:
                main(i)
            main(MAIN_TRIPS - 1, last=True)
            stage_gates(MAIN_TRIPS - 1, MAIN_BATCHES - 1, 1)
            for j in range(1, RING):
                split_u(POST + j, j)

            def weights(g, q, first=False):
                dve.wait_ge(actg_in[q], (g - q) * 8 + 16)
                dve.wait_ge(gates_in[q], (g - q) * 8 + 16)
                if not first:
                    dve.wait_ge(wlo_ready, g)
                nc.vector.tensor_tensor(
                    w32[:].rearrange("p n (c t) -> p n c t", t=CHUNK),
                    act_in[q][:].rearrange("p n (c t) -> p n c t", t=CHUNK),
                    gates[q][:].rearrange("p c n t -> p n c t"), ALU.mult).then_inc(w_ready, 1)

            def split_w(g, q):
                dve.wait_ge(whi_ready, g + 1)
                nc.vector.tensor_tensor(w_lo[q][:], w32[:], w_hi[q][:].bitcast(F32),
                                        ALU.subtract).then_inc(wlo_ready, 1)

            def add_y(g, o):
                t, half = divmod(o, 2)
                dve.wait_ge(y_done, g * 8 + (o + 1))
                v = x_res[:, t, half * 512:(half + 1) * 512]
                nc.vector.tensor_tensor(v, v, ps[:, o, :], ALU.add).then_inc(y_added, 1)

            def second(i, last=False):
                for q in range(2):
                    g = i * 2 + q
                    if not (last and q == 1):
                        weights(g + 1, 1 - q)
                    for o in range(4):
                        add_y(g, o)
                    if not (last and q == 1):
                        split_w(g + 1, 1 - q)
                    for o in range(4, 8):
                        add_y(g, o)

            weights(0, 0, True)
            split_w(0, 0)
            with dve.Fori(0, GROUPS // 2 - 1) as i:
                second(i)
            second(GROUPS // 2 - 1, True)

        @block.tensor
        def _(pe):
            mm = nc.tensor.matmul

            def start(job):
                n = INDEX[job]
                if n >= 8:
                    emptied(pe, JOBS[n - 8][0])
                return bank(job)

            def done(ins):
                ins.then_inc(bank_done, 1)

            pe.wait_ge(h_ready, TB)
            pe.wait_ge(consts_in, 48)
            for k in range(KD):
                o = start(("hT", k))
                for t in range(TB):
                    last = nc.tensor.transpose(o[:, t * P:(t + 1) * P], h_nat[:, t, k * P:(k + 1) * P], ident)
                done(last)
            emptied(pe, ("hT", KD - 1))

            def three_passes(o, lhs, rhs):
                n = 0
                for x, y in ((0, 0), (0, 1), (1, 0)):
                    for k in range(KD):
                        last = mm(o, lhs(x, k), rhs(y, k), start=n == 0, stop=n == PER_BLOCK - 1)
                        n += 1
                return last

            h_parts = (hT_hi, hT_lo)
            pe.wait_ge(clo_ready, 1)
            for t in range(TB):
                o = start(("c", t))
                done(three_passes(o[:, 0:NW], lambda x, k: h_parts[x][:, k, t * P:(t + 1) * P],
                                  lambda x, k: (c_hi, c_lo)[x][:, k, :]))
            for w, j in enumerate((("gi",), ("gf",))):
                o = start(j)
                emptied(pe, ("c", TB - 1))
                for t in range(TB):
                    last = nc.tensor.transpose(o[0:H, t * P:(t + 1) * P], c_nat[:, t, w * H:(w + 1) * H], ident)
                done(last)
            for w, name in enumerate(("mq", "mk")):
                for h in range(H):
                    r = 2 * w + h // 2
                    pe.wait_ge(wilo_ready, r + 1)
                    o = start((name, h))
                    c0 = h % 2 * DH
                    done(three_passes(o, lambda x, k: (wi_hi, wi_lo)[x][:, r % 2, k, c0:c0 + DH],
                                      lambda x, k: h_parts[x][:, k, :]))
            pe.wait_ge(c_ready, 2)
            for k in range(3):
                o = start(("cT", k))
                for t in range(TB):
                    last = nc.tensor.transpose(o[:, t * P:(t + 1) * P],
                                               c_nat[:, t, N_Q + k * P:N_Q + (k + 1) * P], ident)
                done(last)
            pe.wait_ge(wsmall_in, 32)
            emptied(pe, ("cT", 2))
            for t in range(TB):
                for i in range(2):
                    o = start(("q", t, i))
                    for k in range(2):
                        last = mm(o[:, 0:2 * DQK], cT[:, k, t * P:(t + 1) * P],
                                  w_uq[:, k, i * 2 * DQK:(i + 1) * 2 * DQK], start=k == 0, stop=k == 1)
                    done(last)
            for t in range(TB):
                for i in range(2):
                    o = start(("kv", t, i))
                    done(mm(o, cT[:, 2, t * P:(t + 1) * P], w_ukv[:, i * 512:(i + 1) * 512], start=True, stop=True))
            for w, name in enumerate(("mv", "mo")):
                for i in range(2):
                    r = 4 + 2 * w + i
                    pe.wait_ge(wilo_ready, r + 1)
                    for t in range(TB):
                        o = start((name, i, t))
                        done(three_passes(o[:, 0:UNIT], lambda x, k: h_parts[x][:, k, t * P:(t + 1) * P],
                                          lambda x, k: (wi_hi, wi_lo)[x][:, r % 2, k, :]))
            pe.wait_ge(m_ready, 2)
            pe.wait_ge(em_ready, 1)
            o = start(("rowT",))
            for w, row in enumerate((g_u, g_f)):
                for t in range(TB):
                    last = nc.tensor.transpose(o[:, (w * TB + t) * H:(w * TB + t + 1) * H],
                                               row[:, t * P:(t + 1) * P], ident[0:H, 0:H])
            done(last)
            emptied(pe, ("mq", H - 1))
            emptied(pe, ("mk", H - 1))
            emptied(pe, ("mv", 1, TB - 1))
            pe.wait_ge(ones_ready, 1)
            for h in range(H + 1):
                if h < H:
                    o = start(("negM", h))
                    done(mm(o, sel[:, h, :], g_i[:], start=True, stop=True))
                    for s in range(TB):
                        o = start(("S", h, s))
                        done(mm(o[:, 0:(TB - s) * P], mkT[:, h, s * P:(s + 1) * P], mqT[:, h, s * P:], start=True,
                                stop=True))
                    pe.wait_ge(qk_ready, 4)
                    src = q_nat if h < 2 else k_nat
                    rows, c0 = (DH, 0) if h % 2 == 0 else (ROPE, DH)
                    for x in range(H):
                        o = start(("qkT", h, x))
                        for t in range(TB):
                            last = nc.tensor.transpose(o[0:rows, t * P:(t + 1) * P], src[:, t, x, c0:c0 + rows],
                                                       ident)
                        done(last)
                if h:
                    emptied(pe, ("S", h - 1, TB - 1))
                    for i in range(2):
                        o = start(("num", h - 1, i))
                        for tt in range(2):
                            t = 2 * i + tt
                            for s in range(t + 1):
                                c0 = D_OFF[s] + (t - s) * P
                                last = mm(o[:, tt * (DH + 1):(tt + 1) * (DH + 1)], sT[:, (h - 1) % 2, c0:c0 + P],
                                          v_aug[:, s, h - 1, :], start=s == 0, stop=s == t)
                        done(last)
            emptied(pe, ("qkT", 3, H - 1))
            units = [(h, t) for h in range(H) for t in range(TB)]
            for n in range(len(units) + 2):
                if n < len(units):
                    h, t = units[n]
                    o = start(("sc", h, t))
                    w = (t + 1) * P
                    mm(o[:, 0:w], qkT[:, 0, h, t * P:w], qkT[:, 2, h, 0:w], start=True, stop=False)
                    done(mm(o[:, 0:w], qkT[0:ROPE, 1, h, t * P:w], qkT[0:ROPE, 3, h, 0:w], start=False, stop=True))
                if 1 <= n <= len(units):
                    h, t = units[n - 1]
                    emptied(pe, ("sc", h, t))
                    o = start(("pT", h, t))
                    for kb in range(t + 1):
                        last = nc.tensor.transpose(o[:, kb * P:(kb + 1) * P],
                                                   p_nat[:, (n - 1) % 3, kb * P:(kb + 1) * P], ident)
                    done(last)
                if n >= 2:
                    h, t = units[n - 2]
                    emptied(pe, ("pT", h, t))
                    o = start(("pv", h, t))
                    for kb in range(t + 1):
                        last = mm(o[:, 0:DH], pT[:, (n - 2) % 3, kb * P:(kb + 1) * P], kv_nat[:, kb, h, 1, :],
                                  start=kb == 0, stop=kb == t)
                    done(last)
            emptied(pe, ("pv", H - 1, TB - 1))
            pe.wait_ge(mixed_ready, 1)
            for k in range(KD):
                o = start(("mT", k))
                for t in range(TB):
                    last = nc.tensor.transpose(o[:, t * P:(t + 1) * P], mixed[:, t, k * P:(k + 1) * P], ident)
                done(last)
            pe.wait_ge(wout_in, 16)
            emptied(pe, ("mT", KD - 2))
            emptied(pe, ("mT", KD - 1))
            for t in range(TB):
                for i in range(2):
                    o = start(("out", t, i))
                    for k in range(KD):
                        last = mm(o, mixT[:, k, t * P:(t + 1) * P], w_out[:, k, i * 512:(i + 1) * 512],
                                  start=k == 0, stop=k == KD - 1)
                    done(last)
            pe.wait_ge(h2_ready, TB)
            for k in range(KD):
                o = start(("h2T", k))
                for t in range(TB):
                    last = nc.tensor.transpose(o[:, t * P:(t + 1) * P], h2_nat[:, t, k * P:(k + 1) * P], ident)
                done(last)
            pe.wait_ge(h2lo_ready, KD)
            pe.wait_ge(keys_in, 16)
            for h in range(PH):
                pe.wait_ge(wqlo_ready, h + 1)
                for s in range(2):
                    o = start(("qry", h, s))
                    done(three_passes(o, lambda x, k: (wq_hi, wq_lo)[x][:, h % 2, k, s * P:(s + 1) * P],
                                      lambda x, k: (h2_hi, h2_lo)[x][:, k, :]))
                emptied(pe, ("qry", h, 1))
                for i in range(2):
                    o = start(("s12", h, i))
                    for tt in range(2):
                        for s in range(2):
                            c0 = (2 * tt + s) * NK
                            t = 2 * i + tt
                            last = mm(o[:, c0:c0 + NK], qryT[:, (2 * h + s) % 3, t * P:(t + 1) * P],
                                      keysT[:, s, :], start=True, stop=True)
                    done(last)

            def first_product(n, j, first=False, between=()):
                pe.wait_ge(ulo_ready, n + 1)
                if not first:
                    pe.wait_ge(act_ready, n - (RING - 1))
                o, q = ps[:, j % RING, :], j % 2
                for m in range(PER_BLOCK):
                    x, k = divmod(m, KD)
                    u, h2 = ((u_hi, h2_hi), (u_hi, h2_lo), (u_lo, h2_hi))[x]
                    last = mm(o, u[:, q, k, :], h2[:, k, :], start=m == 0, stop=m == PER_BLOCK - 1)
                    if m == PER_BLOCK - 1:
                        last.then_inc(z_done, 1)
                    for at_m, make in between:
                        if at_m == m:
                            make()

            emptied(pe, ("s12", PH - 1, 1))
            for j in range(PRE_BODY):
                first_product(j, j, True)
            with pe.Fori(1, PRE_TRIPS) as i:
                for j in range(PRE_BODY):
                    first_product(i * PRE_BODY + j, j)
            for t in range(TB):
                pe.wait_ge(tri_ready, 3 * t + 3)
                for w in range(3):
                    last = nc.tensor.transpose(ps[:, 4 + t, w * P:(w + 1) * P], tri[:, t, w, :], ident)
                last.then_inc(triT_done, 1)

            def gate_matrices(n, b, first=False):
                pe.wait_ge(oh_ready, n * 3 + 3)
                if not first:
                    pe.wait_ge(gate_staged, n - 1)
                q, slot = b % 2, b % OH_RING
                for w in range(BATCH):
                    o = ps[:, 4 + 2 * q + w // 2, w % 2 * 2 * NK:(w % 2 + 1) * 2 * NK]
                    last = mm(o, oh2[:, slot, w, :], gate_rows[:, slot, w, :, :].rearrange("p x n -> p (x n)"),
                              start=True, stop=True)
                last.then_inc(gate_done, 1)

            def main(i, first=False):
                for j in range(MAIN_BODY):
                    between = [((b + 1) * PER_BATCH - 1 - j * PER_BLOCK,
                                lambda b=b: gate_matrices(i * MAIN_BATCHES + b, b, first and b < 2))
                               for b in BATCHES_IN[j]]
                    first_product(i * MAIN_BODY + (PRE + j), j, between=between)

            main(0, True)
            with pe.Fori(1, MAIN_TRIPS) as i:
                main(i)
            for j in range(RING):
                first_product(POST + j, j)

            def second(i, first=False):
                for q in range(2):
                    g = i * 2 + q
                    pe.wait_ge(wlo_ready, g + 1)
                    pe.wait_ge(vlo_ready, (g + 1) * GROUP)
                    for o in range(8):
                        t, half = divmod(o, 2)
                        if not (first and q == 0):
                            pe.wait_ge(y_added, g * 8 + (o - 7))
                        ds = slice(half * 512, (half + 1) * 512)
                        for j in range(GROUP):
                            w = w_hi[q][:, j, t * P:(t + 1) * P]
                            mm(ps[:, o, :], w, v_hi[q][:, j, ds], start=j == 0, stop=False)
                            mm(ps[:, o, :], w, v_lo[q][:, j, ds], start=False, stop=False)
                            last = mm(ps[:, o, :], w_lo[q][:, j, t * P:(t + 1) * P], v_hi[q][:, j, ds],
                                      start=False, stop=j == GROUP - 1)
                        last.then_inc(y_done, 1)

            pe.wait_ge(act_ready, E_BLOCKS)
            pe.wait_ge(gate_staged, S // BATCH)
            second(0, True)
            with pe.Fori(1, GROUPS // 2) as i:
                second(i)


def kernel(x, positions, attn_norm_g, w_in, b_igate, b_fgate, mlstm_norm_g, cq_norm_g, w_uq, ckv_norm_g,
           w_ukv, q_norm_g, k_norm_g, w_out, ffn_norm_g, peer_w_q, peer_keys_1, peer_keys_2, peer_u, peer_v):
    import numpy as np
    import concourse.bacc as bacc
    from concourse import mybir
    from concourse.bass_utils import run_bass_kernel_spmd

    def col(v):
        return np.asarray(v).reshape(-1, P).T

    def rows(v):
        return np.broadcast_to(np.asarray(v).reshape(1, -1), (P, np.asarray(v).size))

    r = np.arange(P)
    inv_freq = (np.float32(10000.0) ** (-np.arange(0, ROPE, 2, dtype=np.float32) / np.float32(ROPE)))
    consts = np.concatenate([
        np.eye(P, dtype=np.float32),
        np.broadcast_to(r.astype(np.float32), (P, P)),
        np.where(r[:, None] <= r[None, :], 0.0, NEG).astype(np.float32),
        np.where(r[None, :] <= r[:, None], 0.0, NEG).astype(np.float32),
        np.broadcast_to(inv_freq.astype(np.float32), (P, HALF)),
        rows(q_norm_g), rows(k_norm_g)], axis=1)
    head_rows = np.zeros((H, H, P), np.float32)
    for h in range(H):
        head_rows[h, h, :] = 1.0
    biases = np.zeros((P, 2), np.float32)
    biases[:H, 0] = np.asarray(b_igate)[0]
    biases[:H, 1] = np.asarray(b_fgate)[0]
    vecs = np.concatenate([col(attn_norm_g), col(ffn_norm_g), col(mlstm_norm_g), col(cq_norm_g),
                           col(ckv_norm_g), biases], axis=1)
    arrays = {
        "x": np.asarray(x)[0],
        "positions": np.asarray(positions).reshape(TB, P).T,
        "consts": consts,
        "vecs": vecs,
        "head_rows": head_rows,
        "w_in": np.asarray(w_in)[0],
        "w_uq": np.asarray(w_uq)[0],
        "w_ukv": np.asarray(w_ukv)[0],
        "w_out": np.asarray(w_out)[0],
        "w_q": np.asarray(peer_w_q)[0],
        "keysT": np.stack([np.asarray(peer_keys_1)[0].T, np.asarray(peer_keys_2)[0].T], axis=1),
        "uT": np.asarray(peer_u)[0].reshape(NK, NK, KD, P).transpose(0, 3, 2, 1),
        "v": np.asarray(peer_v)[0].reshape(NK, NK, D),
    }
    arrays = {k: np.ascontiguousarray(v) for k, v in arrays.items()}
    nc = bacc.Bacc("TRN2", target_bir_lowering=False, num_devices=1)
    aps = {k: nc.dram_tensor("in_" + k, v.shape, mybir.dt.from_np(v.dtype), kind="ExternalInput").ap()
           for k, v in arrays.items()}
    aps["out"] = nc.dram_tensor("y", (S, D), mybir.dt.float32, kind="ExternalOutput").ap()
    build(nc, aps)
    res = run_bass_kernel_spmd(nc, [{"in_" + k: v for k, v in arrays.items()}], core_ids=[0])
    return res.results[0]["y"].reshape(1, S, D)
```

```python
from contextlib import ExitStack

import concourse.bass as bass
import numpy as np
from concourse import mybir

F32 = mybir.dt.float32
F32R = mybir.dt.float32r
I32 = mybir.dt.int32
U32 = mybir.dt.uint32
ALU = mybir.AluOpType
ACT = mybir.ActivationFunctionType
AX_X = mybir.AxisListType.X

P = 128
D = 1024
S = 512
TB = S // P
KD = D // P
H = 4
DH = 128
ROPE = 64
HALF = ROPE // 2
DQK = DH + ROPE
QR, KVR = 256, 128
D_IN = 4 * H * DH + 2 * H + QR + KVR + ROPE
COL_Q, COL_K, COL_V, COL_O = 0, H * DH, 2 * H * DH, 3 * H * DH
COL_G = 4 * H * DH
NW = D_IN - COL_G
N_Q = 2 * H
N_KV = N_Q + QR
N_KR = N_KV + KVR
UNIT = 2 * DH
UNITS = COL_G // UNIT
EPS = 1e-6
PH = 8
NK = 128
TOPK = 16
NEG = -1e30
LOWEST = -3.0e38
TWO_PI = 2.0 * np.pi
MAGIC = 1.5 * 2.0**23

RUNS = []
_pos, _a = 0, 0
while _a < TOPK:
    _len = TOPK // (_a + 1)
    _n = 1
    while _a + _n < TOPK and TOPK // (_a + _n + 1) == _len:
        _n += 1
    RUNS.append((_a, _n, _len, _pos))
    _pos += _n * _len
    _a += _n
CAND = _pos

C_ID, C_IOTA, C_MIN, C_NEG, C_FREQ, C_GQ, C_GK = 0, 128, 256, 384, 512, 544, 736
C_W = 928
V_ATT, V_ML, V_CQ, V_CKV, V_BI, V_BF = 0, 8, 12, 14, 15, 16
V_W = 17

E_BLOCKS = NK
GROUP = 4
GROUPS = E_BLOCKS // GROUP
CHUNK = 32
CHUNKS = S // CHUNK
BATCH = 4
PRE_BODY, PRE_TRIPS = 4, 7
MAIN_BODY, MAIN_TRIPS = 12, 8
OH_RING = 4
RING = 4
MAIN_BATCHES = 16
PER_BLOCK = 3 * KD
PER_BATCH = MAIN_BODY * PER_BLOCK // MAIN_BATCHES
BATCHES_IN = [[b for b in range(MAIN_BATCHES) if ((b + 1) * PER_BATCH - 1) // PER_BLOCK == j]
              for j in range(MAIN_BODY)]
PRE = PRE_BODY * PRE_TRIPS
POST = PRE + MAIN_BODY * MAIN_TRIPS
assert POST + RING == E_BLOCKS and PRE_BODY % RING == 0 and MAIN_BODY % RING == 0
assert MAIN_BATCHES * BATCH * MAIN_TRIPS == S and MAIN_BATCHES * BATCH == 2 * CHUNK


def front_jobs():
    jobs = [(("hT", k), "D") for k in range(KD)]
    jobs += [(("c", t), "D") for t in range(TB)] + [(("gi",), "D"), (("gf",), "D")]
    jobs += [(("mq", h), "A") for h in range(H)] + [(("mk", h), "D") for h in range(H)]
    jobs += [(("cT", k), "D") for k in range(3)]
    jobs += [(("q", t, i), "A") for t in range(TB) for i in range(2)]
    jobs += [(("kv", t, i), "D") for t in range(TB) for i in range(2)]
    jobs += [((name, i, t), "A") for name in ("mv", "mo") for i in range(2) for t in range(TB)]
    jobs += [(("rowT",), "D")]
    for h in range(H + 1):
        if h < H:
            jobs += [(("negM", h), "D")] + [(("S", h, s), "D") for s in range(TB)]
            jobs += [(("qkT", h, x), "A") for x in range(H)]
        if h:
            jobs += [(("num", h - 1, i), "A") for i in range(2)]
    units = [(h, t) for h in range(H) for t in range(TB)]
    for n in range(len(units) + 2):
        if n < len(units):
            jobs.append((("sc", *units[n]), "A"))
        if 1 <= n <= len(units):
            jobs.append((("pT", *units[n - 1]), "A"))
        if n >= 2:
            jobs.append((("pv", *units[n - 2]), "D"))
    jobs += [(("mT", k), "DA"[k % 2]) for k in range(KD)]
    for t in range(TB):
        jobs += [(("out", t, i), "D") for i in range(2)]
        if t:
            jobs += [(("h2T", t - 1, i), "D") for i in range(2)]
    jobs += [(("h2T", TB - 1, i), "D") for i in range(2)]
    jobs += [(("qry", 0, s), "A") for s in range(2)]
    for h in range(PH):
        if h + 1 < PH:
            jobs.append((("qry", h + 1, 0), "A"))
        jobs += [(("s12", h, i), "D") for i in range(2)]
        if h + 1 < PH:
            jobs.append((("qry", h + 1, 1), "A"))
    return jobs


JOBS = front_jobs()
INDEX = {name: n for n, (name, _) in enumerate(JOBS)}
ENGINE_OF = dict(JOBS)
NTH = {name: sum(e == eng for _, e in JOBS[: n + 1]) for n, (name, eng) in enumerate(JOBS)}
D_OFF = [0, 512, 896, 1152]
D_ALL = 1280
MID = 9
WO_AT = 5
LAST_OF_UNIT = [(n, h) for n in ("mq", "mk") for h in (1, 3)] + [(n, i, TB - 1) for n in ("mv", "mo") for i in (0, 1)]


def build(nc, a):
    ctx = ExitStack()
    with ctx:
        base = 16512

        def at(name, kb, shape, dt=F32):
            return nc.alloc_sbuf_tensor_at(name, shape, dt, offset=base + int(kb * 1024))

        def sem(name):
            return ctx.enter_context(nc.semaphore(name))

        fence = ctx.enter_context(nc.sbuf_tensor("whole_sbuf", [P, (212800 // 4)], F32))
        ps = ctx.enter_context(nc.psum_tensor("banks", [P, 8, 512], F32))

        x_res = at("x_res", 0, [P, TB, D])
        consts = at("consts", 16, [P, C_W])
        vecs = at("vecs", 19.75, [P, 32])
        sel = at("head_rows", 20, [H, H, P])
        ident = consts[:, C_ID:C_ID + P]
        iota = consts[:, C_IOTA:C_IOTA + P]
        mask_min = consts[:, C_MIN:C_MIN + P]
        mask_neg = consts[:, C_NEG:C_NEG + P]
        freq = consts[:, C_FREQ:C_FREQ + HALF]
        gq = consts[:, C_GQ:C_GQ + DQK]
        gk = consts[:, C_GK:C_GK + DQK]

        c_raw = at("c_raw", 22, [P, KD, NW])
        c_hi = at("c_hi", 36.5, [P, KD, NW], F32R)
        c_lo = at("c_lo", 51, [P, KD, NW], F32R)
        wi_raw = at("wi_raw", 65.5, [P, 3, KD, UNIT])
        wi_hi = at("wi_hi", 89.5, [P, 2, KD, UNIT], F32R)
        wi_lo = at("wi_lo", 105.5, [P, 2, KD, UNIT], F32R)
        hT_hi = at("hT_hi", 122, [P, KD, S], F32R)
        hT_lo = at("hT_lo", 138, [P, KD, S], F32R)
        mqT = at("mqT", 154, [P, H, S])
        mkT = at("mkT", 162, [P, H, S])
        v_aug = at("v_aug", 170, [P, TB, H, DH + 1])
        og = at("og", 178.5, [P, TB, H * DH])
        h_nat = at("h_nat", 186.5, [P, TB, D])
        x_junk = at("x_junk", 122, [P, D])
        g_i, g_f, g_tmp, g_F, g_u, g_M = [
            at(n, 186.5 + 2 * i, [H, S]) for i, n in enumerate(("g_i", "g_f", "g_tmp", "g_F", "g_u", "g_M"))]
        rtmp = at("rtmp", 198.5, [P, 2, TB, H, HALF])
        c_nat = at("c_nat", 170, [P, TB, NW])
        c_junk = at("c_junk", 177.5, [P, QR])
        cT = at("cT", 177.5, [P, 3, S])
        stat = at("stat", 204, [P, 16, 32])

        q_nat = at("q_nat", 22, [P, TB, H, DQK])
        kv_nat = at("kv_nat", 34, [P, TB, H, 2, DH])
        w_uq = at("w_uq", 50, [P, 2, H * DQK])
        w_ukv = at("w_ukv", 56, [P, 2 * H * DH])
        k_nat = at("k_nat", 50, [P, TB, H, DQK])
        cosin = at("cosin", 62.5, [P, 2, TB, HALF])
        pos_i = at("pos_i", 63.75, [P, TB], I32)
        pos_f = at("pos_f", 63.875, [P, TB])
        junk = at("junk", 64.25, [P, QR])
        ang = at("ang", 202.5, [P, 3, TB, HALF])
        qkT = at("qkT", 65.5, [P, 4, H, S])

        dexp = at("dexp", 97.5, [P, 2, D_ALL])
        sT = at("sT", 107.5, [P, 2, D_ALL])
        numall = at("numall", 117.5, [P, TB, H, DH + 1])
        h_sq = at("h_sq", 126, [P, TB, H, DH])
        mixed = at("mixed", 186.5, [P, TB, D])
        p_nat = at("p_nat", 22, [P, 3, S])
        pT = at("pT", 28, [P, 3, S])
        mix_hi = at("mix_hi", 65.5, [P, KD, S], F32R)
        mix_lo = at("mix_lo", 81.5, [P, KD, S], F32R)
        w_out = at("w_out", 134, [P, KD, D])
        wo_lo = at("wo_lo", 134, [P, KD, D], F32R)
        wo_hi_a = at("wo_hi_a", 97.5, [P, 5, D], F32R)
        wo_hi_b = at("wo_hi_b", 50, [P, KD - 5, D], F32R)
        wo_hi = [wo_hi_a[:, k, :] if k < 5 else wo_hi_b[:, k - 5, :] for k in range(KD)]

        ffn_gain = at("ffn_gain", 38, [P, D])
        sq_junk = at("sq_junk", 182, [P, D])
        h2_nat = at("h2_nat", 186, [P, 2, D])
        h2_hi = at("h2_hi", 22, [P, KD, S], F32R)
        h2_lo = at("h2_lo", 166, [P, KD, S], F32R)
        wq_raw = [at(f"wq_raw{i}", kb, [P, KD, UNIT]) for i, kb in enumerate((42, 117.5, 106))]
        wq_hi = [at(f"wq_hi{i}", kb, [P, KD, UNIT], F32R) for i, kb in enumerate((126, 66))]
        wq_lo = [at(f"wq_lo{i}", kb, [P, KD, UNIT], F32R) for i, kb in enumerate((194, 74))]
        qryT = at("qryT", 184, [P, 3, S])
        keysT = at("keysT", 206.25, [P, 2, NK])
        best_v = at("best_v", 86, [P, 2, TB, PH, TOPK])
        best_i = at("best_i", 90, [P, 2, TB, PH, TOPK], U32)
        best_tmp = at("best_tmp", 94, [P, 2, NK])

        u_raw = at("u_raw", 118, [P, 4, KD, P])
        u_hi = at("u_hi", 134, [P, 2, KD, P], F32R)
        u_lo = at("u_lo", 142, [P, 2, KD, P], F32R)
        act_out = at("act_out", 102, [P, RING, S])
        stage = [at(f"stage{i}", kb, [P, NK, CHUNK]) for i, kb in enumerate((38, 150))]
        oh2 = at("oh2", 54, [P, OH_RING, BATCH, NK], F32R)
        oh1 = at("oh1", 62, [P, OH_RING, BATCH, NK])
        gate_rows = at("gate_rows", 70, [P, OH_RING, BATCH, 2, NK], F32R)
        cand = at("cand", 70, [P, PH, CAND])
        pay = at("pay", 71.75, [P, PH, CAND])
        picked = at("picked", 73.5, [P, PH // 2, TOPK, CAND])
        pay_f = at("pay_f", 94, [P, 2, PH, TOPK])
        cand_tmp = at("cand_tmp", 95, [P, PH, CAND])
        iota_c = at("iota_c", 96.75, [P, CAND])
        sc_v = at("sc_v", 110, [P, TB, PH, TOPK])
        sc_i = at("sc_i", 97.5, [P, PH, TOPK], U32)
        sc_f = at("sc_f", 98, [P, PH, TOPK])
        e_f = at("e_f", 98.5, [P, PH, TOPK])
        e_i = at("e_i", 99, [P, 3, PH, TOPK], I32)
        tops = at("tops", 100.5, [P, PH])
        sums = at("sums", 112, [P, TB, PH])
        tri = at("tri", 192, [P, TB, 3, PH * TOPK])
        tab = at("tab", 184, [P, 3, S])
        tab_hi = at("tab_hi", 190, [P, S], F32R)
        tab_lo = at("tab_lo", 198, [P, S])

        v_raw = at("v_raw", 38, [P, 4, D])
        v_hi = [at(f"v_hi{q}", kb, [P, GROUP, D], F32R) for q, kb in enumerate((54, 118))]
        v_lo = [at(f"v_lo{q}", kb, [P, GROUP, D], F32R) for q, kb in enumerate((86, 134))]
        act_in = [at(f"act_in{q}", kb, [P, GROUP, S]) for q, kb in enumerate((70, 150))]
        gates = [at(f"gates{q}", kb, [P, CHUNKS, GROUP, CHUNK]) for q, kb in enumerate((78, 198))]
        w32 = at("w32", 110, [P, GROUP, S])
        w_hi = [at(f"w_hi{q}", kb, [P, GROUP, S], F32R) for q, kb in enumerate((182, 166))]
        w_lo = [at(f"w_lo{q}", kb, [P, GROUP, S], F32R) for q, kb in enumerate((190, 174))]

        act_d = nc.dram_tensor("act_scratch", [E_BLOCKS, P, S], F32).ap()
        gate_d = nc.dram_tensor("gate_scratch", [CHUNKS, NK, NK, CHUNK], F32).ap()

        consts_in = sem("consts_in")
        x_in = [sem(f"x_in{t}") for t in range(TB)]
        c_in = sem("c_in")
        wi_in = [sem(f"wi_in{i}") for i in range(3)]
        chi_ready = sem("chi_ready")
        clo_ready = sem("clo_ready")
        wihi_ready = sem("wihi_ready")
        wilo_ready = sem("wilo_ready")
        hhi_ready = sem("hhi_ready")
        keys_in = sem("keys_in")
        pos_in = sem("pos_in")
        wsmall_in = sem("wsmall_in")
        wout_in = sem("wout_in")
        wohi_ready = sem("wohi_ready")
        wolo_ready = sem("wolo_ready")
        mixhi_ready = sem("mixhi_ready")
        gain_in = sem("gain_in")
        wq_in = [sem(f"wq_in{i}") for i in range(3)]
        wqhi_ready = sem("wqhi_ready")
        wqlo_ready = sem("wqlo_ready")
        bank_done = sem("bank_done")
        freed = {"A": sem("bank_freed_scalar"), "D": sem("bank_freed_vector")}
        dve_step = sem("dve_step")
        x_sq = sem("x_sq")
        exp_ready = sem("exp_ready")
        var_ready = sem("var_ready")
        root_ready = sem("root_ready")
        h_ready = sem("h_ready")
        fabs_ready = sem("fabs_ready")
        ln_ready = sem("ln_ready")
        m_ready = sem("m_ready")
        em_ready = sem("em_ready")
        c_sq = sem("c_sq")
        c_ready = sem("c_ready")
        kr_ready = sem("kr_ready")
        qk_sq = sem("qk_sq")
        ang_ready = sem("ang_ready")
        trig_ready = sem("trig_ready")
        ones_ready = sem("ones_ready")
        dpre_ready = sem("dpre_ready")
        dexp_ready = sem("dexp_ready")
        den_ready = sem("den_ready")
        h_scaled = sem("h_scaled")
        h_sq_ready = sem("h_sq_ready")
        h_summed = sem("h_summed")
        h_root = sem("h_root")
        h_normed = sem("h_normed")
        qk_ready = sem("qk_ready")
        rowmax_ready = sem("rowmax_ready")
        mixed_ready = sem("mixed_ready")
        x2_ready = sem("x2_ready")
        x2_sq = sem("x2_sq")
        h2_ready = sem("h2_ready")
        h2hi_ready = sem("h2hi_ready")
        h2lo_ready = sem("h2lo_ready")
        gate_pre = sem("gate_pre")
        gate_exp = sem("gate_exp")
        tri_ready = sem("tri_ready")
        triT_done = sem("triT_done")
        tab_ready = sem("tab_ready")
        u_in = [sem(f"u_in{i}") for i in range(4)]
        uhi_ready = sem("uhi_ready")
        ulo_ready = sem("ulo_ready")
        ulo_main = sem("ulo_main")
        z_done = sem("z_done")
        act_ready = sem("act_ready")
        act_saved = [sem(f"act_saved{i}") for i in range(RING)]
        oh_step = sem("oh_step")
        oh_ready = sem("oh_ready")
        gate_done = sem("gate_done")
        gate_upper = sem("gate_upper")
        gate_staged = sem("gate_staged")
        gate_head_saved = sem("gate_head_saved")
        gate_saved = [sem(f"gate_saved{i}") for i in range(2)]
        v_in = [sem(f"v_in{i}") for i in range(4)]
        actg_in = [sem(f"actg_in{i}") for i in range(2)]
        gates_in = [sem(f"gates_in{i}") for i in range(2)]
        vhi_ready = sem("vhi_ready")
        vlo_ready = sem("vlo_ready")
        w_ready = sem("w_ready")
        whi_ready = sem("whi_ready")
        wlo_ready = sem("wlo_ready")
        y_done = sem("y_done")
        y_added = sem("y_added")
        out_saved = sem("out_saved")

        def bank(job):
            return ps[:, INDEX[job] % 8, :]

        def arrived(eng, job):
            eng.wait_ge(bank_done, INDEX[job] + 1)

        def emptied(eng, job):
            eng.wait_ge(freed[ENGINE_OF[job]], NTH[job])

        def free(ins, job):
            ins.then_inc(freed[ENGINE_OF[job]], 1)

        def gate_banks(q):
            return ps[:, 4 + 2 * q:6 + 2 * q, :].rearrange("p b (w x n) -> p (b w) x n", w=BATCH // 2, x=2)

        def staged_at(b):
            chunk, t0 = divmod(b * BATCH, CHUNK)
            return stage[chunk][:, :, t0:t0 + BATCH].rearrange("p n t -> p t n")

        block = ctx.enter_context(nc.Block())

        @block.sync
        def _(sp):
            for t in range(TB):
                sp.dma_start(x_res[:, t, :], a["x"][t * P:(t + 1) * P, :]).then_inc(x_in[t], 16)
            sp.dma_start(consts[:], a["consts"]).then_inc(consts_in, 16)
            sp.dma_start(vecs[:, 0:V_W], a["vecs"]).then_inc(consts_in, 16)
            sp.dma_start(sel[:], a["head_rows"]).then_inc(consts_in, 16)
            w_v = a["w_in"].rearrange("(k p) n -> p k n", p=P)
            sp.dma_start(c_raw[:], w_v[:, :, COL_G:D_IN]).then_inc(c_in, 16)

            def load_unit(r):
                if r >= 3:
                    sp.wait_ge(wilo_ready, r - 2)
                sp.dma_start(wi_raw[:, r % 3, :, :], w_v[:, :, r * UNIT:(r + 1) * UNIT]).then_inc(wi_in[r % 3], 16)

            for r in range(3):
                load_unit(r)
            sp.dma_start(keysT[:], a["keysT"]).then_inc(keys_in, 16)
            arrived(sp, ("c", TB - 1))
            sp.dma_start(w_uq[:], a["w_uq"].rearrange("(k p) n -> p k n", p=P)).then_inc(wsmall_in, 16)
            sp.dma_start(w_ukv[:], a["w_ukv"]).then_inc(wsmall_in, 16)
            sp.dma_start(pos_i[:], a["positions"]).then_inc(pos_in, 16)
            for r in range(3, UNITS):
                load_unit(r)
            arrived(sp, ("S", H - 1, TB - 1))
            sp.dma_start(w_out[:], a["w_out"].rearrange("(k p) n -> p k n", p=P)).then_inc(wout_in, 16)
            arrived(sp, ("pv", H - 1, TB - 1))
            sp.dma_start(ffn_gain[:], a["ffn_gain"]).then_inc(gain_in, 16)
            wq_v = a["w_q"].rearrange("(k p) n -> p k n", p=P)
            for h in range(PH):
                if h == 1:
                    sp.wait_ge(mixed_ready, 1)
                if h == 2:
                    arrived(sp, ("out", TB - 1, 1))
                if h >= 3:
                    sp.wait_ge(wqlo_ready, h - 2)
                sp.dma_start(wq_raw[h % 3][:], wq_v[:, :, h * UNIT:(h + 1) * UNIT]).then_inc(wq_in[h % 3], 16)

            def load_u(n, j):
                sp.dma_start(u_raw[:, j % 4, :, :],
                             a["uT"][bass.ds(n, 1)].rearrange("o p k e -> (o p) k e")).then_inc(u_in[j % 4], 16)

            sp.wait_ge(wqlo_ready, PH)
            load_u(0, 0)
            arrived(sp, ("qry", PH - 2, 1))
            for j in range(1, 4):
                load_u(j, j)

            def save_act(n, j):
                sp.wait_ge(act_ready, n + 1)
                sp.dma_start(act_d[bass.ds(n, 1)].rearrange("o p t -> (o p) t"),
                             act_out[:, j % RING, :]).then_inc(act_saved[j % RING], 16)

            with sp.Fori(0, PRE_TRIPS) as i:
                for j in range(PRE_BODY):
                    n = i * PRE_BODY + j
                    sp.wait_ge(ulo_ready, n + 1)
                    load_u(n + 4, j)
                    save_act(n, j)

            def save_gates(i, chunk):
                sp.wait_ge(gate_staged, i * MAIN_BATCHES + (chunk + 1) * CHUNK // BATCH)
                sp.dma_start(gate_d[bass.ds(i * 2 + chunk, 1)].rearrange("o p n t -> (o p) (n t)"),
                             stage[chunk][:].rearrange("p n t -> p (n t)")).then_inc(gate_saved[chunk], 16)

            def main(i):
                for j in range(MAIN_BODY):
                    n = i * MAIN_BODY + (PRE + j)
                    sp.wait_ge(ulo_main, i * MAIN_BODY + (j + 1))
                    load_u(n + 4, j)
                    save_act(n, j)
                    for b in BATCHES_IN[j]:
                        if (b + 2) * BATCH % CHUNK == 0 and b + 2 < MAIN_BATCHES:
                            save_gates(i, (b + 2) * BATCH // CHUNK - 1)

            with sp.Fori(0, MAIN_TRIPS - 1) as i:
                main(i)
                save_gates(i, 1)
            main(MAIN_TRIPS - 1)

            def load_v(n, j):
                sp.dma_start(v_raw[:, j, :], a["v"][bass.ds(n, 1)].rearrange("o p d -> (o p) d")
                             ).then_inc(v_in[j], 16)

            def load_act(g, q):
                sp.dma_start(act_in[q][:], act_d[bass.ds(g * GROUP, GROUP)].rearrange("n p t -> p n t")
                             ).then_inc(actg_in[q], 16)

            def load_gates(g, q):
                sp.dma_start(gates[q][:].rearrange("p c n t -> p c (n t)"),
                             gate_d[:, :, bass.ds(g * GROUP, GROUP), :].rearrange("c p n t -> p c (n t)")
                             ).then_inc(gates_in[q], 16)

            sp.wait_ge(gate_saved[0], 16 * CHUNKS // 2)
            for j in range(GROUP):
                load_v(j, j)
            sp.wait_ge(gate_staged, MAIN_TRIPS * MAIN_BATCHES)
            last = gate_d[CHUNKS - 1]
            sp.dma_start(last[:, 0:GROUP, :].rearrange("p n t -> p (n t)"),
                         stage[1][:, 0:GROUP, :].rearrange("p n t -> p (n t)")).then_inc(gate_head_saved, 16)
            for q in range(RING):
                sp.wait_ge(act_saved[q], 16)
            load_act(0, 0)
            sp.wait_ge(gate_saved[1], 16 * (CHUNKS // 2 - 1))
            sp.wait_ge(gate_head_saved, 16)
            load_gates(0, 0)
            sp.dma_start(last[:, GROUP:, :].rearrange("p n t -> p (n t)"),
                         stage[1][:, GROUP:, :].rearrange("p n t -> p (n t)")).then_inc(gate_saved[1], 16)
            for j in range(RING):
                save_act(POST + j, j)
            sp.wait_ge(gate_saved[1], 16 * CHUNKS // 2)
            load_act(1, 1)
            load_gates(1, 1)
            for q in range(RING):
                sp.wait_ge(act_saved[q], 16 * E_BLOCKS // RING)

            def second(i):
                for q in range(2):
                    g = i * 2 + q
                    for j in range(GROUP):
                        sp.wait_ge(vlo_ready, g * GROUP + (j + 1))
                        if not isinstance(i, int) or g + 1 < GROUPS:
                            load_v(g * GROUP + (GROUP + j), j)
                    if not isinstance(i, int) or g + 2 < GROUPS:
                        sp.wait_ge(w_ready, g + 1)
                        load_act(g + 2, q)
                        load_gates(g + 2, q)

            with sp.Fori(0, GROUPS // 2 - 1) as i:
                second(i)
            second(GROUPS // 2 - 1)
            for t in range(TB):
                sp.wait_ge(y_added, 8 * (GROUPS - 1) + 2 * t + 2)
                sp.dma_start(a["out"][t * P:(t + 1) * P, :], x_res[:, t, :]).then_inc(out_saved, 16)
            sp.wait_ge(out_saved, 16 * TB)

        @block.gpsimd
        def _(pool):
            def split_unit(r):
                pool.wait_ge(wihi_ready, r + 1)
                nc.gpsimd.tensor_tensor(wi_lo[:, r % 2, :, :], wi_raw[:, r % 3, :, :],
                                        wi_hi[:, r % 2, :, :].bitcast(F32), ALU.subtract).then_inc(wilo_ready, 1)

            for r in range(6):
                split_unit(r)
            pool.wait_ge(kr_ready, 1)
            nc.gpsimd.memset(v_aug[:, :, :, DH:DH + 1], 1.0).then_inc(ones_ready, 1)
            for r in range(6, UNITS):
                split_unit(r)

            def over_width(ap):
                u = ap.rearrange("p (t h) -> p t h", h=H).unsqueeze(3)
                return u.to_broadcast([P, TB, H, DH])
            num = numall[:, :, :, 0:DH]
            emptied(pool, ("num", H - 1, 1))
            pool.wait_ge(den_ready, 1)
            nc.gpsimd.tensor_tensor(num, num, over_width(stat[:, 13, 0:16]), ALU.mult).then_inc(h_scaled, 1)
            pool.wait_ge(h_scaled, 1)
            nc.gpsimd.tensor_tensor(h_sq[:], num, num, ALU.mult).then_inc(h_sq_ready, 1)
            pool.wait_ge(h_root, 1)
            nc.gpsimd.tensor_tensor(num, num, over_width(stat[:, 7, 0:16]), ALU.mult).then_inc(h_normed, 1)
            pool.wait_ge(h_normed, 1)
            nc.gpsimd.tensor_tensor(mixed[:, :, 0:H * DH].rearrange("p t (h d) -> p t h d", h=H), num,
                                    og[:].rearrange("p t (h d) -> p t h d", h=H), ALU.mult).then_inc(mixed_ready, 1)
            for h in range(PH):
                pool.wait_ge(wqhi_ready, h + 1)
                nc.gpsimd.tensor_tensor(wq_lo[h % 2][:], wq_raw[h % 3][:], wq_hi[h % 2][:].bitcast(F32), ALU.subtract).then_inc(wqlo_ready, 1)

            def split_u(n, j):
                pool.wait_ge(uhi_ready, n + 1)
                nc.gpsimd.tensor_tensor(u_lo[:, j % 2, :, :], u_raw[:, j % 4, :, :],
                                        u_hi[:, j % 2, :, :].bitcast(F32), ALU.subtract).then_inc(ulo_ready, 1)

            with pool.Fori(0, PRE_TRIPS) as i:
                for j in range(PRE_BODY):
                    split_u(i * PRE_BODY + j, j)
            with pool.Fori(0, GROUPS // 2) as i:
                for q in range(2):
                    for j in range(GROUP):
                        pool.wait_ge(vhi_ready, (i * 2 + q) * GROUP + (j + 1))
                        nc.gpsimd.tensor_tensor(v_lo[q][:, j, :], v_raw[:, j, :],
                                                v_hi[q][:, j, :].bitcast(F32), ALU.subtract).then_inc(vlo_ready, 1)

        @block.scalar
        def _(act):
            roots = [0]

            def root(cols):
                roots[0] += 1
                act.wait_ge(var_ready, roots[0])
                nc.scalar.activation(cols, cols, ACT.Sqrt).then_inc(root_ready, 1)

            def copy(out, src):
                return nc.scalar.activation(out, src, ACT.Copy)

            def round_unit(r):
                act.wait_ge(wi_in[r % 3], r // 3 * 16 + 16)
                if r >= 2:
                    arrived(act, LAST_OF_UNIT[r - 2])
                copy(wi_hi[:, r % 2, :, :], wi_raw[:, r % 3, :, :]).then_inc(wihi_ready, 1)

            for t in range(TB):
                act.wait_ge(x_in[t], 16)
                nc.scalar.activation(x_junk[:], x_res[:, t, :], ACT.Square,
                                     accum_out=stat[:, 0, t:t + 1]).then_inc(x_sq, 1)
                act.wait_ge(x_sq, t + 1)
            root(stat[:, 1, 0:TB])
            act.wait_ge(c_in, 16)
            copy(c_hi[:], c_raw[:]).then_inc(chi_ready, 1)
            act.wait_ge(consts_in, 48)
            for k in range(KD):
                arrived(act, ("hT", k))
                nc.scalar.activation(hT_hi[:, k, :], bank(("hT", k)), ACT.Copy,
                                     scale=vecs[:, V_ATT + k:V_ATT + k + 1]).then_inc(hhi_ready, 1)
            round_unit(0)
            round_unit(1)
            for t in range(TB):
                emptied(act, ("c", t))
                for x, (c0, c1) in enumerate(((N_Q, N_KV), (N_KV, N_KR), (N_KR, NW))):
                    nc.scalar.activation(c_junk[:, 0:c1 - c0], c_nat[:, t, c0:c1], ACT.Square,
                                         accum_out=stat[:, 0, 4 + 4 * x + t:5 + 4 * x + t]).then_inc(c_sq, 1)
                    act.wait_ge(c_sq, 3 * t + x + 1)
            root(stat[:, 1, 4:12])
            for h in range(2):
                arrived(act, ("mq", h))
                free(copy(mqT[:, h, :], bank(("mq", h))), ("mq", h))
            round_unit(2)
            act.wait_ge(fabs_ready, 1)
            nc.scalar.activation(g_tmp[:], g_tmp[:], ACT.Exp, scale=-1.0).then_inc(exp_ready, 1)
            act.wait_ge(exp_ready, 1)
            nc.scalar.activation(g_tmp[:], g_tmp[:], ACT.Ln, bias=1.0).then_inc(ln_ready, 1)
            for h in range(2, H):
                arrived(act, ("mq", h))
                free(copy(mqT[:, h, :], bank(("mq", h))), ("mq", h))
            round_unit(3)
            round_unit(4)
            act.wait_ge(m_ready, 1)
            nc.scalar.activation(g_f[:], g_f[:], ACT.Exp, scale=-1.0).then_inc(em_ready, 1)
            round_unit(5)
            for t in range(TB):
                for i in range(2):
                    j = ("q", t, i)
                    arrived(act, j)
                    free(copy(q_nat[:, t, 2 * i:2 * i + 2, :],
                              bank(j)[:, 0:2 * DQK].rearrange("p (h d) -> p h d", h=2)), j)
            emptied(act, ("q", TB - 1, 1))
            for t in range(TB):
                for h in range(H):
                    nc.scalar.activation(junk[:, 0:DQK], q_nat[:, t, h, :], ACT.Square,
                                         accum_out=stat[:, 3, t * H + h:t * H + h + 1]).then_inc(qk_sq, 1)
                    act.wait_ge(qk_sq, t * H + h + 1)

            def take_v(i, t):
                j = ("mv", i, t)
                arrived(act, j)
                free(copy(v_aug[:, t, 2 * i:2 * i + 2, 0:DH],
                          bank(j)[:, 0:UNIT].rearrange("p (h d) -> p h d", h=2)), j)

            act.wait_ge(kr_ready, 1)
            for t in range(TB):
                take_v(0, t)
            round_unit(6)
            emptied(act, ("kv", TB - 1, 1))
            for t in range(TB):
                for h in range(H):
                    nc.scalar.activation(junk[:, 0:DH], kv_nat[:, t, h, 0, :], ACT.Square,
                                         accum_out=stat[:, 3, 16 + t * H + h:17 + t * H + h]).then_inc(qk_sq, 1)
                    act.wait_ge(qk_sq, (TB + t) * H + h + 1)
            for t in range(TB):
                take_v(1, t)
            round_unit(7)
            root(stat[:, 4, 0:32])
            act.wait_ge(ang_ready, 1)
            nc.scalar.activation(cosin[:], ang[:, 0:2, :, :], ACT.Sin).then_inc(trig_ready, 1)
            for i in range(2):
                for t in range(TB):
                    j = ("mo", i, t)
                    arrived(act, j)
                    free(nc.scalar.activation(og[:, t, i * UNIT:(i + 1) * UNIT], bank(j)[:, 0:UNIT],
                                              ACT.Sigmoid), j)
            for h in range(H + 1):
                if h < H:
                    act.wait_ge(dpre_ready, h + 1)
                    nc.scalar.activation(dexp[:, h % 2, :], dexp[:, h % 2, :], ACT.Exp).then_inc(dexp_ready, 1)
                    rows = DH if h % 2 == 0 else ROPE
                    for x in range(H):
                        j = ("qkT", h, x)
                        arrived(act, j)
                        free(copy(qkT[0:rows, h, x, :], bank(j)[0:rows, :]), j)
                if h:
                    for i in range(2):
                        j = ("num", h - 1, i)
                        arrived(act, j)
                        free(copy(numall[:, 2 * i:2 * i + 2, h - 1, :],
                                  bank(j)[:, 0:2 * (DH + 1)].rearrange("p (t d) -> p t d", t=2)), j)
            units = [(h, t) for h in range(H) for t in range(TB)]
            for n in range(len(units) + 1):
                if n == MID:
                    root(stat[:, 6, 0:16])
                if WO_AT <= n < WO_AT + KD:
                    act.wait_ge(wout_in, 16)
                    copy(wo_hi[n - WO_AT], w_out[:, n - WO_AT, :]).then_inc(wohi_ready, 1)
                if n < len(units):
                    h, t = units[n]
                    j = ("sc", h, t)
                    act.wait_ge(rowmax_ready, n + 1)
                    if n >= 3:
                        arrived(act, ("pT", *units[n - 3]))
                    w = (t + 1) * P
                    free(nc.scalar.activation(p_nat[:, n % 3, 0:w], bank(j)[:, 0:w], ACT.Exp,
                                              bias=stat[:, 8, n:n + 1], scale=float(DQK) ** -0.5,
                                              accum_out=stat[:, 9, n:n + 1]), j)
                if n >= 1:
                    h, t = units[n - 1]
                    j = ("pT", h, t)
                    arrived(act, j)
                    if n >= 4:
                        arrived(act, ("pv", *units[n - 4]))
                    w = (t + 1) * P
                    free(nc.scalar.activation(pT[:, (n - 1) % 3, 0:w], bank(j)[:, 0:w], ACT.Copy), j)
            for k in range(KD):
                j = ("mT", k)
                arrived(act, j)
                if k < H:
                    nc.scalar.activation(mix_hi[:, k, :], bank(j), ACT.Copy,
                                         scale=vecs[:, V_ML + k:V_ML + k + 1]).then_inc(mixhi_ready, 1)
                else:
                    nc.scalar.activation(mix_hi[:, k, :], bank(j), ACT.Copy).then_inc(mixhi_ready, 1)

            def take_h2(t):
                for i in range(2):
                    j = ("h2T", t, i)
                    arrived(act, j)
                    nc.scalar.activation(h2_hi[:, 4 * i:4 * i + 4, t * P:(t + 1) * P],
                                         bank(j).rearrange("p (k t) -> p k t", k=4), ACT.Copy
                                         ).then_inc(h2hi_ready, 1)

            for t in range(TB):
                act.wait_ge(x2_ready, 2 * t + 2)
                nc.scalar.activation(sq_junk[:], x_res[:, t, :], ACT.Square,
                                     accum_out=stat[:, 10, t:t + 1]).then_inc(x2_sq, 1)
                act.wait_ge(x2_sq, t + 1)
                root(stat[:, 11, t:t + 1])
                if t:
                    take_h2(t - 1)

            def round_q(h):
                act.wait_ge(wq_in[h % 3], h // 3 * 16 + 16)
                if h >= 2:
                    arrived(act, ("qry", h - 2, 1))
                copy(wq_hi[h % 2][:], wq_raw[h % 3][:]).then_inc(wqhi_ready, 1)

            round_q(0)
            take_h2(TB - 1)
            arrived(act, ("out", TB - 1, 1))
            round_q(1)

            def round_u(n, j, first=False):
                act.wait_ge(u_in[j % 4], n // 4 * 16 + 16 if isinstance(n, int) else (n - j % 4) * 4 + 16)
                if not first:
                    act.wait_ge(z_done, n - 1)
                nc.scalar.activation(u_hi[:, j % 2, :, :], u_raw[:, j % 4, :, :], ACT.Copy).then_inc(uhi_ready, 1)

            for h in range(PH):
                for s in range(2):
                    j = ("qry", h, s)
                    n = 2 * h + s
                    arrived(act, j)
                    if n >= 4:
                        arrived(act, ("s12", (n - 3) // 2, 1))
                    free(copy(qryT[:, n % 3, :], bank(j)), j)
                if h + 2 < PH:
                    round_q(h + 2)
                if h == PH - 2:
                    round_u(0, 0, True)

            def gelu(n, j, first=False):
                act.wait_ge(z_done, n + 1)
                if not first:
                    act.wait_ge(act_saved[j % RING], (n - j % RING) * (16 // RING))
                nc.scalar.activation(act_out[:, j % RING, :], ps[:, j % RING, :], ACT.Gelu).then_inc(act_ready, 1)

            def trip(i, exp_after=None):
                for j in range(PRE_BODY):
                    n = i * PRE_BODY + j
                    round_u(n + 1, j + 1, isinstance(n, int) and n == 0)
                    gelu(n, j, isinstance(i, int) and i == 0)
                    if j == exp_after:
                        act.wait_ge(gate_pre, TB)
                        nc.scalar.activation(sc_v[:], sc_v[:], ACT.Exp).then_inc(gate_exp, 1)

            trip(0)
            with act.Fori(1, PRE_TRIPS - 2) as i:
                trip(i)
            trip(PRE_TRIPS - 2, exp_after=PRE_BODY // 2)
            trip(PRE_TRIPS - 1)

            def main(i, first=False):
                for j in range(MAIN_BODY):
                    n = i * MAIN_BODY + (PRE + j)
                    round_u(n + 1, j + 1)
                    for b in BATCHES_IN[j]:
                        act.wait_ge(gate_done, i * MAIN_BATCHES + (b + 1))
                        if b * BATCH % CHUNK == 0 and not first:
                            act.wait_ge(gate_saved[b * BATCH // CHUNK], i * 16)
                        nc.scalar.activation(staged_at(b), gate_banks(b % 2)[:, :, 0, :], ACT.Copy
                                             ).then_inc(gate_upper, 1)
                    gelu(n, j)

            main(0, True)
            with act.Fori(1, MAIN_TRIPS) as i:
                main(i)

            def round_v(g, q, j, first=False):
                act.wait_ge(v_in[j], g * 16 + 16)
                if not first:
                    act.wait_ge(y_done, (g - 1) * 8)
                nc.scalar.activation(v_hi[q][:, j, :], v_raw[:, j, :], ACT.Copy).then_inc(vhi_ready, 1)

            def round_w(g, q):
                act.wait_ge(w_ready, g + 1)
                nc.scalar.activation(w_hi[q][:], w32[:], ACT.Copy).then_inc(whi_ready, 1)

            for j in range(RING):
                if j + 1 < RING:
                    round_u(POST + j + 1, j + 1)
                else:
                    round_w(0, 0)
                gelu(POST + j, j)
                if j < 2:
                    for k in range(2 * j, 2 * j + 2):
                        round_v(0, 0, k, True)
            act.wait_ge(z_done, E_BLOCKS)
            for j in range(GROUP):
                round_v(1, 1, j, True)
            round_w(1, 1)
            with act.Fori(1, GROUPS // 2) as i:
                for q in range(2):
                    for j in range(GROUP):
                        round_v(i * 2 + q, q, j)
                    round_w(i * 2 + q, q)

        @block.vector
        def _(dve):
            steps = [0]

            def step(ins):
                steps[0] += 1
                ins.then_inc(dve_step, 1)

            def settle():
                dve.wait_ge(dve_step, steps[0])

            roots = [0]

            def inv_root(sums_ap, n, var, out):
                roots[0] += 1
                nc.vector.tensor_scalar(var, sums_ap, 1.0 / n, EPS, ALU.mult, ALU.add).then_inc(var_ready, 1)
                dve.wait_ge(root_ready, roots[0])
                step(nc.vector.reciprocal(out, var))
                settle()

            def bc(ap, axis, n):
                u = ap.unsqueeze(axis)
                shape = list(u.shape)
                shape[axis] = n
                return u.to_broadcast(shape)

            dve.wait_ge(x_sq, TB)
            inv_root(stat[:, 0, 0:TB], D, stat[:, 1, 0:TB], stat[:, 2, 0:TB])
            for t in range(TB):
                nc.vector.tensor_scalar(h_nat[:, t, :], x_res[:, t, :], stat[:, 2, t:t + 1], None,
                                        ALU.mult).then_inc(h_ready, 1)
            dve.wait_ge(chi_ready, 1)
            nc.vector.tensor_tensor(c_lo[:], c_raw[:], c_hi[:].bitcast(F32), ALU.subtract).then_inc(clo_ready, 1)
            dve.wait_ge(consts_in, 48)
            for k in range(KD):
                dve.wait_ge(hhi_ready, k + 1)
                free(nc.vector.scalar_tensor_tensor(
                    out=hT_lo[:, k, :], in0=bank(("hT", k)), scalar=vecs[:, V_ATT + k:V_ATT + k + 1],
                    in1=hT_hi[:, k, :].bitcast(F32), op0=ALU.mult, op1=ALU.subtract), ("hT", k))
            for t in range(TB):
                arrived(dve, ("c", t))
                free(nc.vector.tensor_copy(c_nat[:, t, :], bank(("c", t))[:, 0:NW]), ("c", t))
            for j, row, v in ((("gi",), g_i, V_BI), (("gf",), g_f, V_BF)):
                arrived(dve, j)
                free(nc.vector.tensor_scalar(row[:], bank(j)[0:H, :], vecs[0:H, v:v + 1], None, ALU.add), j)
            emptied(dve, ("gf",))
            step(nc.vector.tensor_scalar(g_F[:], g_f[:], -1.0, None, ALU.mult))
            settle()
            nc.vector.tensor_tensor(g_tmp[:], g_f[:], g_F[:], ALU.max).then_inc(fabs_ready, 1)
            dve.wait_ge(c_sq, 3 * TB)
            step(nc.vector.tensor_scalar(stat[:, 0, 8:12], stat[:, 0, 8:12], float(QR) / KVR, None, ALU.mult))
            settle()
            inv_root(stat[:, 0, 4:12], QR, stat[:, 1, 4:12], stat[:, 2, 4:12])
            for c0, c1, x in ((N_Q, N_KV, 4), (N_KV, N_KR, 8)):
                v = c_nat[:, :, c0:c1]
                nc.vector.tensor_tensor(v, v, bc(stat[:, 2, x:x + 4], 2, c1 - c0), ALU.mult).then_inc(c_ready, 1)
            dve.wait_ge(ln_ready, 1)
            step(nc.vector.scalar_tensor_tensor(out=g_f[:], in0=g_f[:], scalar=0.0, in1=g_tmp[:],
                                                op0=ALU.min, op1=ALU.subtract))
            settle()
            step(nc.vector.memset(g_tmp[:], 1.0))
            settle()
            step(nc.vector.tensor_tensor_scan(out=g_F[:], data0=g_tmp[:], data1=g_f[:], initial=0.0,
                                              op0=ALU.mult, op1=ALU.add))
            settle()
            step(nc.vector.tensor_tensor(g_u[:], g_i[:], g_F[:], ALU.subtract))
            settle()
            step(nc.vector.tensor_tensor_scan(out=g_M[:], data0=g_tmp[:], data1=g_u[:], initial=0.0,
                                              op0=ALU.mult, op1=ALU.max))
            settle()
            nc.vector.tensor_tensor(g_f[:], g_F[:], g_M[:], ALU.add).then_inc(m_ready, 1)
            nc.vector.tensor_scalar(g_i[:], g_M[:], -1.0, None, ALU.mult).then_inc(m_ready, 1)
            dve.wait_ge(pos_in, 16)
            step(nc.vector.tensor_copy(pos_f[:], pos_i[:]))
            settle()
            for t in range(TB):
                step(nc.vector.tensor_scalar(ang[:, 0, t, :], freq, pos_f[:, t:t + 1], None, ALU.mult))
            settle()
            step(nc.vector.tensor_scalar(ang[:, 1, :, :], ang[:, 0, :, :], 1.0 / TWO_PI, MAGIC, ALU.mult, ALU.add))
            settle()
            step(nc.vector.tensor_scalar(ang[:, 1, :, :], ang[:, 1, :, :], MAGIC, None, ALU.subtract))
            settle()
            c1 = 6.28125
            c2 = float(np.float32(np.round((TWO_PI - c1) * 2**20) / 2**20))
            c3 = float(TWO_PI - c1 - c2)
            for c in (c1, c2, c3):
                step(nc.vector.scalar_tensor_tensor(out=ang[:, 0, :, :], in0=ang[:, 1, :, :], scalar=-c,
                                                    in1=ang[:, 0, :, :], op0=ALU.mult, op1=ALU.add))
                settle()
            pi = float(np.float32(3.1415925))
            step(nc.vector.tensor_scalar(ang[:, 0, :, :], ang[:, 0, :, :], pi, -pi, ALU.min, ALU.max))
            settle()
            step(nc.vector.tensor_scalar(ang[:, 2, :, :], ang[:, 0, :, :], -1.0, None, ALU.mult))
            settle()
            step(nc.vector.tensor_tensor(ang[:, 1, :, :], ang[:, 0, :, :], ang[:, 2, :, :], ALU.max))
            settle()
            nc.vector.tensor_scalar(ang[:, 1, :, :], ang[:, 1, :, :], -1.0, TWO_PI / 4, ALU.mult,
                                    ALU.add).then_inc(ang_ready, 1)
            for h in range(H):
                arrived(dve, ("mk", h))
                free(nc.vector.tensor_copy(mkT[:, h, :], bank(("mk", h))), ("mk", h))
            for k in range(3):
                j = ("cT", k)
                arrived(dve, j)
                free(nc.vector.tensor_scalar(cT[:, k, :], bank(j), vecs[:, V_CQ + k:V_CQ + k + 1], None,
                                             ALU.mult), j)
            for t in range(TB):
                for i in range(2):
                    j = ("kv", t, i)
                    arrived(dve, j)
                    free(nc.vector.tensor_copy(kv_nat[:, t, 2 * i:2 * i + 2, :, :],
                                               bank(j).rearrange("p (h w d) -> p h w d", h=2, w=2)), j)
            nc.vector.tensor_copy(k_nat[:, :, :, DH:DQK], bc(c_nat[:, :, N_KR:NW], 2, H)).then_inc(kr_ready, 1)

            dve.wait_ge(qk_sq, 2 * TB * H)
            k_sums = stat[:, 3, 16:32].rearrange("p (t h) -> p t h", h=H)
            step(nc.vector.tensor_tensor(k_sums, k_sums, bc(stat[:, 0, 12:16], 2, H), ALU.add))
            settle()
            inv_root(stat[:, 3, 0:32], DQK, stat[:, 4, 0:32], stat[:, 5, 0:32])
            rq = stat[:, 5, 0:16].rearrange("p (t h) -> p t h", h=H)
            rk = stat[:, 5, 16:32].rearrange("p (t h) -> p t h", h=H)
            dve.wait_ge(kr_ready, 1)
            emptied(dve, ("kv", TB - 1, 1))
            step(nc.vector.tensor_tensor(q_nat[:], q_nat[:], bc(rq, 3, DQK), ALU.mult))
            step(nc.vector.tensor_tensor(k_nat[:, :, :, 0:DH], kv_nat[:, :, :, 0, :], bc(rk, 3, DH), ALU.mult))
            step(nc.vector.tensor_tensor(k_nat[:, :, :, DH:DQK], k_nat[:, :, :, DH:DQK], bc(rk, 3, ROPE),
                                         ALU.mult))
            settle()
            for x_nat, g in ((q_nat, gq), (k_nat, gk)):
                v = x_nat[:].rearrange("p t h d -> p (t h) d")
                step(nc.vector.tensor_tensor(v, v, bc(g, 1, TB * H), ALU.mult))
            dve.wait_ge(trig_ready, 1)
            settle()
            sin_t = bc(cosin[:, 0, :, :], 2, H)
            cos_t = bc(cosin[:, 1, :, :], 2, H)
            for x, x_nat in enumerate((q_nat, k_nat)):
                r1 = x_nat[:, :, :, DH:DH + HALF]
                r2 = x_nat[:, :, :, DH + HALF:DQK]
                step(nc.vector.tensor_tensor(rtmp[:, 0, :, :, :], r2, sin_t, ALU.mult))
                step(nc.vector.tensor_tensor(rtmp[:, 1, :, :, :], r1, sin_t, ALU.mult))
                settle()
                step(nc.vector.tensor_tensor(r1, r1, cos_t, ALU.mult))
                step(nc.vector.tensor_tensor(r2, r2, cos_t, ALU.mult))
                settle()
                nc.vector.tensor_tensor(r1, r1, rtmp[:, 0, :, :, :], ALU.subtract).then_inc(qk_ready, 1)
                nc.vector.tensor_tensor(r2, r2, rtmp[:, 1, :, :, :], ALU.add).then_inc(qk_ready, 1)
                dve.wait_ge(qk_ready, 2 * x + 2)

            arrived(dve, ("rowT",))
            free(nc.vector.tensor_copy(stat[:, 12, 0:32], bank(("rowT",))[:, 0:32]), ("rowT",))
            emptied(dve, ("rowT",))
            u_col = stat[:, 12, 0:16].rearrange("p (t h) -> p t h", h=H)
            em_col = stat[:, 12, 16:32]
            for h in range(H):
                j = ("negM", h)
                arrived(dve, j)
                neg_m = bank(j)
                for s in range(TB):
                    lo = D_OFF[s]
                    step(nc.vector.scalar_tensor_tensor(
                        out=dexp[:, h % 2, lo:lo + P], in0=neg_m[:, s * P:(s + 1) * P],
                        scalar=u_col[:, s, h:h + 1], in1=mask_min, op0=ALU.add, op1=ALU.min))
                    if s < TB - 1:
                        step(nc.vector.tensor_scalar(dexp[:, h % 2, lo + P:lo + (TB - s) * P],
                                                     neg_m[:, (s + 1) * P:], u_col[:, s, h:h + 1], None, ALU.add))
                settle()
                dve.sem_inc(freed["D"], 1)
                dve.sem_inc(dpre_ready, 1)
                dve.wait_ge(dexp_ready, h + 1)
                if h >= 2:
                    arrived(dve, ("num", h - 2, 1))
                for s in range(TB):
                    j = ("S", h, s)
                    arrived(dve, j)
                    lo, w = D_OFF[s], (TB - s) * P
                    free(nc.vector.scalar_tensor_tensor(
                        out=sT[:, h % 2, lo:lo + w], in0=bank(j)[:, 0:w], scalar=float(DH) ** -0.5,
                        in1=dexp[:, h % 2, lo:lo + w], op0=ALU.mult, op1=ALU.mult), j)
                emptied(dve, ("S", h, TB - 1))

            emptied(dve, ("num", H - 1, 1))
            den = numall[:, :, :, DH]
            dd = stat[:, 13, 0:16].rearrange("p (t h) -> p t h", h=H)
            em3 = em_col.rearrange("p (t h) -> p t h", h=H)
            step(nc.vector.tensor_scalar(dd, den, -1.0, None, ALU.mult))
            settle()
            step(nc.vector.tensor_tensor(dd, dd, den, ALU.max))
            settle()
            step(nc.vector.tensor_tensor(dd, dd, em3, ALU.max))
            settle()
            nc.vector.reciprocal(dd, dd).then_inc(den_ready, 1)
            units = [(h, t) for h in range(H) for t in range(TB)]
            for n in range(len(units) + 2):
                if n == MID:
                    dve.wait_ge(h_sq_ready, 1)
                    step(nc.vector.reduce_sum(stat[:, 14, 0:16].rearrange("p (t h) -> p t h", h=H), h_sq[:],
                                              axis=AX_X))
                    settle()
                    inv_root(stat[:, 14, 0:16], DH, stat[:, 6, 0:16], stat[:, 7, 0:16])
                    dve.sem_inc(h_root, 1)
                if WO_AT < n <= WO_AT + KD:
                    k = n - WO_AT - 1
                    dve.wait_ge(wohi_ready, k + 1)
                    nc.vector.tensor_tensor(wo_lo[:, k, :], w_out[:, k, :], wo_hi[k].bitcast(F32),
                                            ALU.subtract).then_inc(wolo_ready, 1)
                if n < len(units):
                    h, t = units[n]
                    j = ("sc", h, t)
                    arrived(dve, j)
                    w = t * P
                    step(nc.vector.tensor_tensor(bank(j)[:, w:w + P], bank(j)[:, w:w + P], mask_neg, ALU.add))
                    settle()
                    step(nc.vector.reduce_max(stat[:, 13, 16 + n % 16:17 + n % 16], bank(j)[:, 0:w + P], axis=AX_X))
                    settle()
                    nc.vector.tensor_scalar(stat[:, 8, n:n + 1], stat[:, 13, 16 + n % 16:17 + n % 16],
                                            -float(DQK) ** -0.5, None, ALU.mult).then_inc(rowmax_ready, 1)
                if n >= 2:
                    h, t = units[n - 2]
                    j = ("pv", h, t)
                    emptied(dve, ("sc", h, t))
                    step(nc.vector.reciprocal(stat[:, 9, n - 2:n - 1], stat[:, 9, n - 2:n - 1]))
                    arrived(dve, j)
                    settle()
                    c0 = (H + h) * DH
                    free(nc.vector.tensor_scalar(mixed[:, t, c0:c0 + DH], bank(j)[:, 0:DH],
                                                 stat[:, 9, n - 2:n - 1], None, ALU.mult), j)
            for k in range(KD):
                j = ("mT", k)
                dve.wait_ge(mixhi_ready, k + 1)
                hi = mix_hi[:, k, :].bitcast(F32)
                if k < H:
                    free(nc.vector.scalar_tensor_tensor(
                        out=mix_lo[:, k, :], in0=bank(j), scalar=vecs[:, V_ML + k:V_ML + k + 1], in1=hi,
                        op0=ALU.mult, op1=ALU.subtract), j)
                else:
                    free(nc.vector.tensor_tensor(mix_lo[:, k, :], bank(j), hi, ALU.subtract), j)

            def take_h2(t):
                for i in range(2):
                    dve.wait_ge(h2hi_ready, 2 * t + i + 1)
                    part = (slice(None), slice(4 * i, 4 * i + 4), slice(t * P, (t + 1) * P))
                    j = ("h2T", t, i)
                    nc.vector.tensor_tensor(h2_lo[part], bank(j).rearrange("p (k t) -> p k t", k=4),
                                            h2_hi[part].bitcast(F32), ALU.subtract).then_inc(h2lo_ready, 1)
                    dve.wait_ge(h2lo_ready, 2 * t + i + 1)
                    dve.sem_inc(freed["D"], 1)

            for t in range(TB):
                for i in range(2):
                    j = ("out", t, i)
                    arrived(dve, j)
                    v = x_res[:, t, i * 512:(i + 1) * 512]
                    step(nc.vector.tensor_tensor(v, v, bank(j), ALU.add))
                    settle()
                    dve.sem_inc(x2_ready, 1)
                    dve.sem_inc(freed["D"], 1)
                dve.wait_ge(x2_sq, t + 1)
                inv_root(stat[:, 10, t:t + 1], D, stat[:, 11, t:t + 1], stat[:, 15, t:t + 1])
                dve.wait_ge(gain_in, 16)
                if t >= 2:
                    arrived(dve, ("h2T", t - 2, 1))
                nc.vector.scalar_tensor_tensor(out=h2_nat[:, t % 2, :], in0=x_res[:, t, :],
                                               scalar=stat[:, 15, t:t + 1], in1=ffn_gain[:],
                                               op0=ALU.mult, op1=ALU.mult).then_inc(h2_ready, 1)
                if t:
                    take_h2(t - 1)
            take_h2(TB - 1)
            for h in range(PH):
                for i in range(2):
                    j = ("s12", h, i)
                    arrived(dve, j)
                    for tt in range(2):
                        t = 2 * i + tt
                        sc = [bank(j)[:, (2 * tt + s) * NK:(2 * tt + s + 1) * NK] for s in range(2)]
                        bv = [best_v[:, s, t, h, :] for s in range(2)]
                        bi = [best_i[:, s, t, h, :] for s in range(2)]
                        for s in range(2):
                            step(nc.vector.max(bv[s][:, 0:8], sc[s]))
                        settle()
                        for s in range(2):
                            step(nc.vector.max_index(bi[s][:, 0:8], bv[s][:, 0:8], sc[s]))
                            step(nc.vector.match_replace(best_tmp[:, s, :], bv[s][:, 0:8], sc[s], LOWEST))
                        settle()
                        for s in range(2):
                            step(nc.vector.max(bv[s][:, 8:16], best_tmp[:, s, :]))
                        settle()
                        for s in range(2):
                            step(nc.vector.max_index(bi[s][:, 8:16], bv[s][:, 8:16], best_tmp[:, s, :]))
                        settle()
                    dve.sem_inc(freed["D"], 1)
            step(nc.vector.tensor_copy(iota_c[:], consts[:, C_IOTA:C_IOTA + CAND]))
            for t in range(TB):
                step(nc.vector.tensor_scalar(pay_f[:, 0, :, :], best_i[:, 0, t, :, :], float(NK), None, ALU.mult))
                step(nc.vector.tensor_copy(pay_f[:, 1, :, :], best_i[:, 1, t, :, :]))
                settle()
                for src, dst in ((best_v[:, :, t, :, :], cand), (pay_f[:], pay)):
                    for a0, na, nb, at0 in RUNS:
                        out = dst[:, :, at0:at0 + na * nb].rearrange("p h (a b) -> p h a b", a=na)
                        step(nc.vector.tensor_tensor(out, bc(src[:, 0, :, a0:a0 + na], 3, nb),
                                                     bc(src[:, 1, :, 0:nb], 2, na), ALU.add))
                settle()
                for h in range(PH):
                    step(nc.vector.max(sc_v[:, t, h, 0:8], cand[:, h, :]))
                settle()
                for h in range(PH):
                    step(nc.vector.max_index(sc_i[:, h, 0:8], sc_v[:, t, h, 0:8], cand[:, h, :]))
                    step(nc.vector.match_replace(cand_tmp[:, h, :], sc_v[:, t, h, 0:8], cand[:, h, :], LOWEST))
                settle()
                for h in range(PH):
                    step(nc.vector.max(sc_v[:, t, h, 8:16], cand_tmp[:, h, :]))
                settle()
                for h in range(PH):
                    step(nc.vector.max_index(sc_i[:, h, 8:16], sc_v[:, t, h, 8:16], cand_tmp[:, h, :]))
                settle()
                step(nc.vector.tensor_copy(tops[:], sc_v[:, t, :, 0]))
                step(nc.vector.tensor_copy(sc_f[:], sc_i[:]))
                settle()
                nc.vector.tensor_tensor(sc_v[:, t, :, :], sc_v[:, t, :, :], bc(tops[:], 2, TOPK), ALU.subtract
                                        ).then_inc(gate_pre, 1)
                for hh in range(2):
                    hs = slice(hh * PH // 2, (hh + 1) * PH // 2)
                    step(nc.vector.tensor_tensor(
                        picked[:], bc(sc_f[:, hs, :], 3, CAND),
                        bc(bc(iota_c[:], 1, TOPK), 1, PH // 2), ALU.is_equal))
                    settle()
                    step(nc.vector.tensor_tensor(picked[:], picked[:], bc(pay[:, hs, :], 2, TOPK), ALU.mult))
                    settle()
                    step(nc.vector.reduce_sum(e_f[:, hs, :], picked[:], axis=AX_X))
                    settle()
                step(nc.vector.tensor_copy(e_i[:, 0, :, :], e_f[:]))
                settle()
                step(nc.vector.tensor_scalar(e_i[:, 1, :, :], e_i[:, 0, :, :], 7, None, ALU.logical_shift_right))
                step(nc.vector.tensor_scalar(e_i[:, 2, :, :], e_i[:, 0, :, :], NK - 1, None, ALU.bitwise_and))
                settle()
                for s in range(2):
                    nc.vector.tensor_copy(tri[:, t, 1 + s, :].rearrange("p (h k) -> p h k", h=PH),
                                          e_i[:, 1 + s, :, :]).then_inc(tri_ready, 1)
                dve.wait_ge(tri_ready, 2 * t + 2)
            dve.wait_ge(gate_exp, 1)
            step(nc.vector.reduce_sum(sums[:], sc_v[:], axis=AX_X))
            settle()
            step(nc.vector.reciprocal(sums[:], sums[:]))
            settle()
            nc.vector.tensor_tensor(tri[:, :, 0, :].rearrange("p t (h k) -> p t h k", h=PH), sc_v[:],
                                    bc(sums[:], 3, TOPK), ALU.mult).then_inc(tri_ready, 1)
            for t in range(TB):
                dve.wait_ge(triT_done, t + 1)
                step(nc.vector.tensor_copy(tab[:, :, t * P:(t + 1) * P],
                                           ps[:, 4 + t, 0:3 * P].rearrange("p (w t) -> p w t", w=3)))
            settle()
            dve.wait_ge(triT_done, TB)
            step(nc.vector.tensor_copy(tab_hi[:], tab[:, 0, :]))
            settle()
            step(nc.vector.tensor_tensor(tab_lo[:], tab[:, 0, :], tab_hi[:].bitcast(F32), ALU.subtract))
            settle()

            iota_b = bc(iota, 1, BATCH)

            def split_u(n, j):
                dve.wait_ge(uhi_ready, n + 1)
                nc.vector.tensor_tensor(u_lo[:, j % 2, :, :], u_raw[:, j % RING, :, :],
                                        u_hi[:, j % 2, :, :].bitcast(F32), ALU.subtract).then_inc(ulo_main, 1)

            def one_hots(i, b, first):
                n = i * MAIN_BATCHES + b
                t0 = n * BATCH
                q = b % OH_RING

                def col(ap):
                    return bc(ap, 2, NK)
                if not first:
                    dve.wait_ge(gate_done, n - (OH_RING - 1))
                nc.vector.tensor_tensor(oh2[:, q, :, :], iota_b, col(tab[:, 2, bass.ds(t0, BATCH)]), ALU.is_equal
                                        ).then_inc(oh_ready, 1)
                nc.vector.tensor_tensor(oh1[:, q, :, :], iota_b, col(tab[:, 1, bass.ds(t0, BATCH)]), ALU.is_equal
                                        ).then_inc(oh_step, 1)
                dve.wait_ge(oh_step, n + 1)
                nc.vector.tensor_tensor(gate_rows[:, q, :, 0, :], oh1[:, q, :, :],
                                        col(tab_hi[:, bass.ds(t0, BATCH)].bitcast(F32)), ALU.mult
                                        ).then_inc(oh_ready, 1)
                nc.vector.tensor_tensor(gate_rows[:, q, :, 1, :], oh1[:, q, :, :],
                                        col(tab_lo[:, bass.ds(t0, BATCH)]), ALU.mult).then_inc(oh_ready, 1)

            def stage_gates(i, b, q):
                dve.wait_ge(gate_upper, i * MAIN_BATCHES + (b + 1))
                staged = staged_at(b)
                nc.vector.tensor_tensor(staged, staged, gate_banks(q)[:, :, 1, :], ALU.add).then_inc(gate_staged, 1)

            def main(i, first=False, last=False):
                for j in range(MAIN_BODY):
                    split_u(i * MAIN_BODY + (PRE + j + 1), j + 1)
                    for b in BATCHES_IN[j]:
                        if b:
                            stage_gates(i, b - 1, (b - 1) % 2)
                        elif not first:
                            stage_gates(i - 1, MAIN_BATCHES - 1, 1)
                        if not (last and b + 2 >= MAIN_BATCHES):
                            one_hots(i, b + 2, first and b + 2 < OH_RING)

            split_u(PRE, 0)
            one_hots(0, 0, True)
            one_hots(0, 1, True)
            main(0, True)
            with dve.Fori(1, MAIN_TRIPS - 1) as i:
                main(i)
            main(MAIN_TRIPS - 1, last=True)
            stage_gates(MAIN_TRIPS - 1, MAIN_BATCHES - 1, 1)
            for j in range(1, RING):
                split_u(POST + j, j)

            def weights(g, q, first=False):
                dve.wait_ge(actg_in[q], (g - q) * 8 + 16)
                dve.wait_ge(gates_in[q], (g - q) * 8 + 16)
                if not first:
                    dve.wait_ge(wlo_ready, g)
                nc.vector.tensor_tensor(
                    w32[:].rearrange("p n (c t) -> p n c t", t=CHUNK),
                    act_in[q][:].rearrange("p n (c t) -> p n c t", t=CHUNK),
                    gates[q][:].rearrange("p c n t -> p n c t"), ALU.mult).then_inc(w_ready, 1)

            def split_w(g, q):
                dve.wait_ge(whi_ready, g + 1)
                nc.vector.tensor_tensor(w_lo[q][:], w32[:], w_hi[q][:].bitcast(F32),
                                        ALU.subtract).then_inc(wlo_ready, 1)

            def add_y(g, o):
                t, half = divmod(o, 2)
                dve.wait_ge(y_done, g * 8 + (o + 1))
                v = x_res[:, t, half * 512:(half + 1) * 512]
                nc.vector.tensor_tensor(v, v, ps[:, o, :], ALU.add).then_inc(y_added, 1)

            def second(i, last=False):
                for q in range(2):
                    g = i * 2 + q
                    if not (last and q == 1):
                        weights(g + 1, 1 - q)
                    for o in range(4):
                        add_y(g, o)
                    if not (last and q == 1):
                        split_w(g + 1, 1 - q)
                    for o in range(4, 8):
                        add_y(g, o)

            weights(0, 0, True)
            split_w(0, 0)
            with dve.Fori(0, GROUPS // 2 - 1) as i:
                second(i)
            second(GROUPS // 2 - 1, True)

        @block.tensor
        def _(pe):
            mm = nc.tensor.matmul

            def start(job):
                n = INDEX[job]
                if n >= 8:
                    emptied(pe, JOBS[n - 8][0])
                return bank(job)

            def done(ins):
                ins.then_inc(bank_done, 1)

            pe.wait_ge(h_ready, TB)
            pe.wait_ge(consts_in, 48)
            for k in range(KD):
                o = start(("hT", k))
                for t in range(TB):
                    last = nc.tensor.transpose(o[:, t * P:(t + 1) * P], h_nat[:, t, k * P:(k + 1) * P], ident)
                done(last)
            emptied(pe, ("hT", KD - 1))

            def three_passes(o, lhs, rhs):
                n = 0
                for x, y in ((0, 0), (0, 1), (1, 0)):
                    for k in range(KD):
                        last = mm(o, lhs(x, k), rhs(y, k), start=n == 0, stop=n == PER_BLOCK - 1)
                        n += 1
                return last

            h_parts = (hT_hi, hT_lo)
            pe.wait_ge(clo_ready, 1)
            for t in range(TB):
                o = start(("c", t))
                done(three_passes(o[:, 0:NW], lambda x, k: h_parts[x][:, k, t * P:(t + 1) * P],
                                  lambda x, k: (c_hi, c_lo)[x][:, k, :]))
            for w, j in enumerate((("gi",), ("gf",))):
                o = start(j)
                emptied(pe, ("c", TB - 1))
                for t in range(TB):
                    last = nc.tensor.transpose(o[0:H, t * P:(t + 1) * P], c_nat[:, t, w * H:(w + 1) * H], ident)
                done(last)
            for w, name in enumerate(("mq", "mk")):
                for h in range(H):
                    r = 2 * w + h // 2
                    pe.wait_ge(wilo_ready, r + 1)
                    o = start((name, h))
                    c0 = h % 2 * DH
                    done(three_passes(o, lambda x, k: (wi_hi, wi_lo)[x][:, r % 2, k, c0:c0 + DH],
                                      lambda x, k: h_parts[x][:, k, :]))
            pe.wait_ge(c_ready, 2)
            for k in range(3):
                o = start(("cT", k))
                for t in range(TB):
                    last = nc.tensor.transpose(o[:, t * P:(t + 1) * P],
                                               c_nat[:, t, N_Q + k * P:N_Q + (k + 1) * P], ident)
                done(last)
            pe.wait_ge(wsmall_in, 32)
            emptied(pe, ("cT", 2))
            for t in range(TB):
                for i in range(2):
                    o = start(("q", t, i))
                    for k in range(2):
                        last = mm(o[:, 0:2 * DQK], cT[:, k, t * P:(t + 1) * P],
                                  w_uq[:, k, i * 2 * DQK:(i + 1) * 2 * DQK], start=k == 0, stop=k == 1)
                    done(last)
            for t in range(TB):
                for i in range(2):
                    o = start(("kv", t, i))
                    done(mm(o, cT[:, 2, t * P:(t + 1) * P], w_ukv[:, i * 512:(i + 1) * 512], start=True, stop=True))
            for w, name in enumerate(("mv", "mo")):
                for i in range(2):
                    r = 4 + 2 * w + i
                    pe.wait_ge(wilo_ready, r + 1)
                    for t in range(TB):
                        o = start((name, i, t))
                        done(three_passes(o[:, 0:UNIT], lambda x, k: h_parts[x][:, k, t * P:(t + 1) * P],
                                          lambda x, k: (wi_hi, wi_lo)[x][:, r % 2, k, :]))
            pe.wait_ge(m_ready, 2)
            pe.wait_ge(em_ready, 1)
            o = start(("rowT",))
            for w, row in enumerate((g_u, g_f)):
                for t in range(TB):
                    last = nc.tensor.transpose(o[:, (w * TB + t) * H:(w * TB + t + 1) * H],
                                               row[:, t * P:(t + 1) * P], ident[0:H, 0:H])
            done(last)
            emptied(pe, ("mq", H - 1))
            emptied(pe, ("mk", H - 1))
            emptied(pe, ("mv", 1, TB - 1))
            pe.wait_ge(ones_ready, 1)
            for h in range(H + 1):
                if h < H:
                    o = start(("negM", h))
                    done(mm(o, sel[:, h, :], g_i[:], start=True, stop=True))
                    for s in range(TB):
                        o = start(("S", h, s))
                        done(mm(o[:, 0:(TB - s) * P], mkT[:, h, s * P:(s + 1) * P], mqT[:, h, s * P:], start=True,
                                stop=True))
                    pe.wait_ge(qk_ready, 4)
                    src = q_nat if h < 2 else k_nat
                    rows, c0 = (DH, 0) if h % 2 == 0 else (ROPE, DH)
                    for x in range(H):
                        o = start(("qkT", h, x))
                        for t in range(TB):
                            last = nc.tensor.transpose(o[0:rows, t * P:(t + 1) * P], src[:, t, x, c0:c0 + rows],
                                                       ident)
                        done(last)
                if h:
                    emptied(pe, ("S", h - 1, TB - 1))
                    for i in range(2):
                        o = start(("num", h - 1, i))
                        for tt in range(2):
                            t = 2 * i + tt
                            for s in range(t + 1):
                                c0 = D_OFF[s] + (t - s) * P
                                last = mm(o[:, tt * (DH + 1):(tt + 1) * (DH + 1)], sT[:, (h - 1) % 2, c0:c0 + P],
                                          v_aug[:, s, h - 1, :], start=s == 0, stop=s == t)
                        done(last)
            emptied(pe, ("qkT", 3, H - 1))
            units = [(h, t) for h in range(H) for t in range(TB)]
            for n in range(len(units) + 2):
                if n < len(units):
                    h, t = units[n]
                    o = start(("sc", h, t))
                    w = (t + 1) * P
                    mm(o[:, 0:w], qkT[:, 0, h, t * P:w], qkT[:, 2, h, 0:w], start=True, stop=False)
                    done(mm(o[:, 0:w], qkT[0:ROPE, 1, h, t * P:w], qkT[0:ROPE, 3, h, 0:w], start=False, stop=True))
                if 1 <= n <= len(units):
                    h, t = units[n - 1]
                    emptied(pe, ("sc", h, t))
                    o = start(("pT", h, t))
                    for kb in range(t + 1):
                        last = nc.tensor.transpose(o[:, kb * P:(kb + 1) * P],
                                                   p_nat[:, (n - 1) % 3, kb * P:(kb + 1) * P], ident)
                    done(last)
                if n >= 2:
                    h, t = units[n - 2]
                    emptied(pe, ("pT", h, t))
                    o = start(("pv", h, t))
                    for kb in range(t + 1):
                        last = mm(o[:, 0:DH], pT[:, (n - 2) % 3, kb * P:(kb + 1) * P], kv_nat[:, kb, h, 1, :],
                                  start=kb == 0, stop=kb == t)
                    done(last)
            emptied(pe, ("pv", H - 1, TB - 1))
            pe.wait_ge(mixed_ready, 1)
            for k in range(KD):
                o = start(("mT", k))
                for t in range(TB):
                    last = nc.tensor.transpose(o[:, t * P:(t + 1) * P], mixed[:, t, k * P:(k + 1) * P], ident)
                done(last)
            pe.wait_ge(wolo_ready, KD)
            emptied(pe, ("mT", KD - 1))

            def transpose_h2(t):
                pe.wait_ge(h2_ready, t + 1)
                for i in range(2):
                    o = start(("h2T", t, i))
                    for k in range(4):
                        c0 = (4 * i + k) * P
                        last = nc.tensor.transpose(o[:, k * P:(k + 1) * P], h2_nat[:, t % 2, c0:c0 + P], ident)
                    done(last)

            for t in range(TB):
                for i in range(2):
                    o = start(("out", t, i))
                    done(three_passes(o, lambda x, k: (mix_hi, mix_lo)[x][:, k, t * P:(t + 1) * P],
                                      lambda x, k: (wo_hi[k], wo_lo[:, k, :])[x][:, i * 512:(i + 1) * 512]))
                if t:
                    transpose_h2(t - 1)
            transpose_h2(TB - 1)
            pe.wait_ge(h2lo_ready, KD)
            pe.wait_ge(keys_in, 16)

            def queries(h, s):
                pe.wait_ge(wqlo_ready, h + 1)
                o = start(("qry", h, s))
                done(three_passes(o, lambda x, k: (wq_hi, wq_lo)[x][h % 2][:, k, s * P:(s + 1) * P],
                                  lambda x, k: (h2_hi, h2_lo)[x][:, k, :]))

            queries(0, 0)
            queries(0, 1)
            for h in range(PH):
                if h + 1 < PH:
                    queries(h + 1, 0)
                emptied(pe, ("qry", h, 1))
                for i in range(2):
                    o = start(("s12", h, i))
                    for tt in range(2):
                        for s in range(2):
                            c0 = (2 * tt + s) * NK
                            t = 2 * i + tt
                            last = mm(o[:, c0:c0 + NK], qryT[:, (2 * h + s) % 3, t * P:(t + 1) * P],
                                      keysT[:, s, :], start=True, stop=True)
                    done(last)
                if h + 1 < PH:
                    queries(h + 1, 1)

            def first_product(n, j, first=False, between=(), ready=ulo_ready, count=None):
                pe.wait_ge(ready, n + 1 if count is None else count)
                if not first:
                    pe.wait_ge(act_ready, n - (RING - 1))
                o, q = ps[:, j % RING, :], j % 2
                for m in range(PER_BLOCK):
                    x, k = divmod(m, KD)
                    u, h2 = ((u_hi, h2_hi), (u_hi, h2_lo), (u_lo, h2_hi))[x]
                    last = mm(o, u[:, q, k, :], h2[:, k, :], start=m == 0, stop=m == PER_BLOCK - 1)
                    if m == PER_BLOCK - 1:
                        last.then_inc(z_done, 1)
                    for at_m, make in between:
                        if at_m == m:
                            make()

            assert RING <= INDEX[("s12", PH - 1, 0)] % 8
            for j in range(PRE_BODY):
                emptied(pe, JOBS[(len(JOBS) - 1) // 8 * 8 + j][0])
                first_product(j, j, True)
            with pe.Fori(1, PRE_TRIPS - 1) as i:
                for j in range(PRE_BODY):
                    first_product(i * PRE_BODY + j, j)
            last_trip = (PRE_TRIPS - 1) * PRE_BODY
            for j in range(2):
                first_product(last_trip + j, j)
            pe.wait_ge(tri_ready, 2 * TB + 1)
            for t in range(TB):
                for w in range(3):
                    last = nc.tensor.transpose(ps[:, 4 + t, w * P:(w + 1) * P], tri[:, t, w, :], ident)
                last.then_inc(triT_done, 1)
            for j in range(2, PRE_BODY):
                first_product(last_trip + j, j)

            def gate_matrices(n, b, first=False):
                pe.wait_ge(oh_ready, n * 3 + 3)
                if not first:
                    pe.wait_ge(gate_staged, n - 1)
                q, slot = b % 2, b % OH_RING
                for w in range(BATCH):
                    o = ps[:, 4 + 2 * q + w // 2, w % 2 * 2 * NK:(w % 2 + 1) * 2 * NK]
                    last = mm(o, oh2[:, slot, w, :], gate_rows[:, slot, w, :, :].rearrange("p x n -> p (x n)"),
                              start=True, stop=True)
                last.then_inc(gate_done, 1)

            def main(i, first=False):
                for j in range(MAIN_BODY):
                    between = [((b + 1) * PER_BATCH - 1 - j * PER_BLOCK,
                                lambda b=b: gate_matrices(i * MAIN_BATCHES + b, b, first and b < 2))
                               for b in BATCHES_IN[j]]
                    first_product(i * MAIN_BODY + (PRE + j), j, between=between, ready=ulo_main,
                                  count=i * MAIN_BODY + (j + 1))

            main(0, True)
            with pe.Fori(1, MAIN_TRIPS) as i:
                main(i)
            for j in range(RING):
                first_product(POST + j, j, ready=ulo_main, count=POST - PRE + j + 1)

            def second(i, first=False):
                for q in range(2):
                    g = i * 2 + q
                    pe.wait_ge(wlo_ready, g + 1)
                    pe.wait_ge(vlo_ready, (g + 1) * GROUP)
                    for o in range(8):
                        t, half = divmod(o, 2)
                        if not (first and q == 0):
                            pe.wait_ge(y_added, g * 8 + (o - 7))
                        ds = slice(half * 512, (half + 1) * 512)
                        for j in range(GROUP):
                            w = w_hi[q][:, j, t * P:(t + 1) * P]
                            mm(ps[:, o, :], w, v_hi[q][:, j, ds], start=j == 0, stop=False)
                            mm(ps[:, o, :], w, v_lo[q][:, j, ds], start=False, stop=False)
                            last = mm(ps[:, o, :], w_lo[q][:, j, t * P:(t + 1) * P], v_hi[q][:, j, ds],
                                      start=False, stop=j == GROUP - 1)
                        last.then_inc(y_done, 1)

            pe.wait_ge(act_ready, E_BLOCKS)
            pe.wait_ge(gate_staged, S // BATCH)
            second(0, True)
            with pe.Fori(1, GROUPS // 2) as i:
                second(i)


def kernel(x, positions, attn_norm_g, w_in, b_igate, b_fgate, mlstm_norm_g, cq_norm_g, w_uq, ckv_norm_g,
           w_ukv, q_norm_g, k_norm_g, w_out, ffn_norm_g, peer_w_q, peer_keys_1, peer_keys_2, peer_u, peer_v):
    import numpy as np
    import concourse.bacc as bacc
    from concourse import mybir
    from concourse.bass_utils import run_bass_kernel_spmd

    def col(v):
        return np.asarray(v).reshape(-1, P).T

    def rows(v):
        return np.broadcast_to(np.asarray(v).reshape(1, -1), (P, np.asarray(v).size))

    r = np.arange(P)
    inv_freq = (np.float32(10000.0) ** (-np.arange(0, ROPE, 2, dtype=np.float32) / np.float32(ROPE)))
    consts = np.concatenate([
        np.eye(P, dtype=np.float32),
        np.broadcast_to(r.astype(np.float32), (P, P)),
        np.where(r[:, None] <= r[None, :], 0.0, NEG).astype(np.float32),
        np.where(r[None, :] <= r[:, None], 0.0, NEG).astype(np.float32),
        np.broadcast_to(inv_freq.astype(np.float32), (P, HALF)),
        rows(q_norm_g), rows(k_norm_g)], axis=1)
    head_rows = np.zeros((H, H, P), np.float32)
    for h in range(H):
        head_rows[h, h, :] = 1.0
    biases = np.zeros((P, 2), np.float32)
    biases[:H, 0] = np.asarray(b_igate)[0]
    biases[:H, 1] = np.asarray(b_fgate)[0]
    vecs = np.concatenate([col(attn_norm_g), col(mlstm_norm_g), col(cq_norm_g),
                           col(ckv_norm_g), biases], axis=1)
    arrays = {
        "x": np.asarray(x)[0],
        "positions": np.asarray(positions).reshape(TB, P).T,
        "consts": consts,
        "vecs": vecs,
        "head_rows": head_rows,
        "ffn_gain": rows(ffn_norm_g),
        "w_in": np.asarray(w_in)[0],
        "w_uq": np.asarray(w_uq)[0],
        "w_ukv": np.asarray(w_ukv)[0],
        "w_out": np.asarray(w_out)[0],
        "w_q": np.asarray(peer_w_q)[0],
        "keysT": np.stack([np.asarray(peer_keys_1)[0].T, np.asarray(peer_keys_2)[0].T], axis=1),
        "uT": np.asarray(peer_u)[0].reshape(NK, NK, KD, P).transpose(0, 3, 2, 1),
        "v": np.asarray(peer_v)[0].reshape(NK, NK, D),
    }
    arrays = {k: np.ascontiguousarray(v) for k, v in arrays.items()}
    nc = bacc.Bacc("TRN2", target_bir_lowering=False, num_devices=1)
    aps = {k: nc.dram_tensor("in_" + k, v.shape, mybir.dt.from_np(v.dtype), kind="ExternalInput").ap()
           for k, v in arrays.items()}
    aps["out"] = nc.dram_tensor("y", (S, D), mybir.dt.float32, kind="ExternalOutput").ap()
    build(nc, aps)
    res = run_bass_kernel_spmd(nc, [{"in_" + k: v for k, v in arrays.items()}], core_ids=[0])
    return res.results[0]["y"].reshape(1, S, D)
```
